# Optimizing a Trainium2 kernel written in Bass

```python
import math
import jax
import jax.numpy as jnp
from jax import lax

D_MODEL = 1024
BATCH = 1
SEQ = 1024
DEPTH = 1

CHUNK = 64
Q_BLOCK = 128
HEAD_DIM = D_MODEL // 16
NEG_INF = -1e30
H_A = 4
H_IDX = 4
D_IDX = HEAD_DIM // 2
TOPK_MAX = 256
H_B = 4
CONV_K = 4
H_C = 4
N_PREV_CHUNKS = 8
MAX_REL_PAST = 128
N_REL = CHUNK + MAX_REL_PAST
H_D = 4
DQ_D = HEAD_DIM // 2
W_A = H_A * HEAD_DIM
W_B = H_B * HEAD_DIM
W_C = H_C * HEAD_DIM
W_D = H_D * 2 * DQ_D
W_BRANCH = W_A
N_BRANCH = 4
COL_SIZES = (W_A, W_A, W_A, H_IDX * D_IDX, D_IDX, H_IDX,
             W_B, W_B, W_B, H_B, H_B, W_B,
             W_C, W_C, W_C,
             W_D, W_D, W_D)
C_IN = sum(COL_SIZES)
N_GROUPS = 4
EXPERTS_PER_GROUP = 8
N_EXPERTS = N_GROUPS * EXPERTS_PER_GROUP
TOP_K_INNER = 2
F_EXPERT = D_MODEL // 2
MOE_BLOCK = 128

kernel_name = 'hybrid_gated_dsa_mlstm_band_diffattn_hmoe'

def rmsnorm(x, g, eps=1e-6):
    xf = x.astype(jnp.float32)
    y = xf * lax.rsqrt(jnp.mean(xf * xf, axis=-1, keepdims=True) + eps)
    return (y * g.astype(jnp.float32)).astype(x.dtype)

def head_rmsnorm(x, g):
    h, d = x.shape[-2:]
    return rmsnorm(x, g.reshape(h, d))

def chunk_visible(t_pos, s_pos):
    return (s_pos // CHUNK) <= (t_pos // CHUNK)

def causal_dwconv(x, w, b):
    k, c = w.shape
    y = lax.conv_general_dilated(x, w[:, None, :].astype(x.dtype), window_strides=(1,),
                                 padding=[(k - 1, 0)], dimension_numbers=('NWC', 'WIO', 'NWC'),
                                 feature_group_count=c)
    return y + b.astype(x.dtype)

def split_columns(proj):
    parts = []
    off = 0
    for sz in COL_SIZES:
        parts.append(proj[..., off:off + sz])
        off += sz
    return parts

def dsa_mixer(q, k, v, q_idx, k_idx, w_idx):
    b, s, h, dh = q.shape
    topk = min(TOPK_MAX, s // 4)
    nqb = s // Q_BLOCK
    s_pos = jnp.arange(s)
    k_idx32 = k_idx.astype(jnp.float32)

    def to_blocks(a):
        return jnp.moveaxis(a.reshape(b, nqb, Q_BLOCK, *a.shape[2:]), 1, 0)

    def gather_rows(a, idx):
        return jax.vmap(lambda ab, ib: ab[ib])(a, idx)

    def block(args):
        qb, qib, wib, blk = args
        t_pos = blk * Q_BLOCK + jnp.arange(Q_BLOCK)
        visible = chunk_visible(t_pos[:, None], s_pos[None, :])
        rel = jnp.maximum(jnp.einsum('bqhd,bsd->bqhs', qib.astype(jnp.float32), k_idx32), 0.0)
        score = jnp.einsum('bqhs,bqh->bqs', rel, wib.astype(jnp.float32))
        score = jnp.where(visible[None], score, NEG_INF)
        _, sel = lax.top_k(score, topk)
        sel_ok = chunk_visible(t_pos[None, :, None], sel)
        k_sel = gather_rows(k, sel)
        v_sel = gather_rows(v, sel)
        logits = jnp.einsum('bqhd,bqkhd->bhqk', qb, k_sel).astype(jnp.float32) * (dh ** -0.5)
        logits = jnp.where(sel_ok[:, None], logits, NEG_INF)
        p = jax.nn.softmax(logits, axis=-1).astype(v.dtype)
        return jnp.einsum('bhqk,bqkhd->bqhd', p, v_sel)

    out = lax.map(block, (to_blocks(q), to_blocks(q_idx), to_blocks(w_idx), jnp.arange(nqb)))
    return jnp.moveaxis(out, 0, 1).reshape(b, s, h, dh)

def mlstm_mixer(q, k, v, i_pre, f_pre, o_pre, norm_g):
    b, s, h, d = q.shape
    n_chunks = s // CHUNK

    def to_chunks(a):
        a = a.reshape(b, n_chunks, CHUNK, h, *a.shape[3:])
        return jnp.moveaxis(jnp.moveaxis(a, 1, 0), 3, 2)

    qc = to_chunks(q.astype(jnp.float32))
    kc = to_chunks(k.astype(jnp.float32) * (d ** -0.5))
    vc = to_chunks(v.astype(jnp.float32))
    ic = to_chunks(i_pre.astype(jnp.float32))
    lfc = to_chunks(jax.nn.log_sigmoid(f_pre.astype(jnp.float32)))
    causal = jnp.tril(jnp.ones((CHUNK, CHUNK), dtype=bool))

    def step(carry, xs):
        c_mat, n_vec, m = carry
        qt, kt, vt, it, lft = xs
        cum = jnp.cumsum(lft, axis=-1)
        dmat = cum[..., :, None] - cum[..., None, :] + it[..., None, :]
        dmat = jnp.where(causal, dmat, NEG_INF)
        m_inter = cum + m[..., None]
        m_t = jnp.maximum(m_inter, jnp.max(dmat, axis=-1))
        w = jnp.exp(dmat - m_t[..., None]) * jnp.einsum('bhtd,bhsd->bhts', qt, kt)
        inter = jnp.exp(m_inter - m_t)
        num = inter[..., None] * jnp.einsum('bhtk,bhvk->bhtv', qt, c_mat) + jnp.einsum('bhts,bhsv->bhtv', w, vt)
        den = inter * jnp.einsum('bhtk,bhk->bht', qt, n_vec) + jnp.sum(w, axis=-1)
        h_t = num / jnp.maximum(jnp.abs(den), jnp.exp(-m_t))[..., None]
        cum_end = cum[..., -1]
        g = cum_end[..., None] - cum + it
        m_new = jnp.maximum(cum_end + m, jnp.max(g, axis=-1))
        carry_scale = jnp.exp(cum_end + m - m_new)
        src = jnp.exp(g - m_new[..., None])
        c_new = carry_scale[..., None, None] * c_mat + jnp.einsum('bhs,bhsv,bhsk->bhvk', src, vt, kt)
        n_new = carry_scale[..., None] * n_vec + jnp.einsum('bhs,bhsk->bhk', src, kt)
        return (c_new, n_new, m_new), h_t

    init = (jnp.zeros((b, h, d, d), jnp.float32), jnp.zeros((b, h, d), jnp.float32),
            jnp.zeros((b, h), jnp.float32))
    _, hc = lax.scan(step, init, (qc, kc, vc, ic, lfc))
    hs = jnp.moveaxis(jnp.moveaxis(hc, 2, 3), 0, 1).reshape(b, s, h, d).astype(q.dtype)
    return jax.nn.sigmoid(o_pre) * head_rmsnorm(hs, norm_g)

def chunk_band_attention(q, k, v, rel_bias):
    b, s, h, d = q.shape
    n_chunks = s // CHUNK
    n_band = N_PREV_CHUNKS + 1
    qc = q.reshape(b, n_chunks, CHUNK, h, d)
    pad = ((0, 0), (N_PREV_CHUNKS, 0), (0, 0), (0, 0), (0, 0))
    kp = jnp.pad(k.reshape(b, n_chunks, CHUNK, h, d), pad)
    vp = jnp.pad(v.reshape(b, n_chunks, CHUNK, h, d), pad)
    band_idx = jnp.arange(n_chunks)[:, None] + jnp.arange(n_band)[None, :]
    kb = kp[:, band_idx].reshape(b, n_chunks, n_band * CHUNK, h, d)
    vb = vp[:, band_idx].reshape(b, n_chunks, n_band * CHUNK, h, d)
    band_ok = (jnp.arange(n_chunks)[:, None] - N_PREV_CHUNKS + jnp.arange(n_band)[None, :]) >= 0
    key_ok = jnp.repeat(band_ok, CHUNK, axis=1)
    dist = N_PREV_CHUNKS * CHUNK + jnp.arange(CHUNK)[:, None] - jnp.arange(n_band * CHUNK)[None, :]
    rel_id = jnp.clip(dist, -(CHUNK - 1), MAX_REL_PAST) + (CHUNK - 1)
    bias = rel_bias[:, rel_id].astype(jnp.float32)
    logits = jnp.einsum('bcihd,bcphd->bhcip', qc, kb).astype(jnp.float32) * (d ** -0.5) + bias[:, None]
    logits = jnp.where(key_ok[None, None, :, None, :], logits, NEG_INF)
    p = jax.nn.softmax(logits, axis=-1).astype(v.dtype)
    return jnp.einsum('bhcip,bcphd->bcihd', p, vb).reshape(b, s, h, d)

def diff_attention(q, k, v, lam_params, norm_g, lam_init):
    b, s, h, _, dq = q.shape
    lp = lam_params.astype(jnp.float32)
    lam = jnp.exp(jnp.sum(lp[0] * lp[1])) - jnp.exp(jnp.sum(lp[2] * lp[3])) + lam_init
    nqb = s // Q_BLOCK
    s_pos = jnp.arange(s)
    q_blocks = jnp.moveaxis(q.reshape(b, nqb, Q_BLOCK, h, 2, dq), 1, 0)

    def block(args):
        qb, blk = args
        t_pos = blk * Q_BLOCK + jnp.arange(Q_BLOCK)
        visible = chunk_visible(t_pos[:, None], s_pos[None, :])
        logits = jnp.einsum('bqhrd,bshrd->bhrqs', qb, k).astype(jnp.float32) * (dq ** -0.5)
        p = jax.nn.softmax(jnp.where(visible, logits, NEG_INF), axis=-1)
        a = (p[:, :, 0] - lam * p[:, :, 1]).astype(v.dtype)
        return jnp.einsum('bhqs,bshd->bqhd', a, v)

    out = lax.map(block, (q_blocks, jnp.arange(nqb)))
    out = jnp.moveaxis(out, 0, 1).reshape(b, s, h, v.shape[-1])
    return head_rmsnorm(out, norm_g) * (1.0 - lam_init)

def hier_moe(h, gw, gb, ew, eb, w1, w3, w2):
    b, s, d = h.shape
    t = b * s
    xt = h.reshape(t, d)
    g_logits = jnp.einsum('td,dg->tg', xt, gw).astype(jnp.float32) + gb.astype(jnp.float32)
    g_sel = jnp.argmax(g_logits, axis=-1)
    g_gate = jnp.take_along_axis(jax.nn.softmax(g_logits, axis=-1), g_sel[:, None], axis=1)
    e_logits = (jnp.einsum('td,de->te', xt, ew).astype(jnp.float32) + eb.astype(jnp.float32))
    e_logits = e_logits.reshape(t, N_GROUPS, EXPERTS_PER_GROUP)
    e_in_group = jnp.take_along_axis(e_logits, g_sel[:, None, None], axis=1)[:, 0]
    top_v, top_i = lax.top_k(e_in_group, TOP_K_INNER)
    gate = jax.nn.softmax(top_v, axis=-1) * g_gate
    n_assign = t * TOP_K_INNER
    eid = (g_sel[:, None] * EXPERTS_PER_GROUP + top_i).reshape(n_assign).astype(jnp.int32)
    tok = jnp.repeat(jnp.arange(t, dtype=jnp.int32), TOP_K_INNER)
    wt = gate.reshape(n_assign)
    order = jnp.argsort(eid)
    se = eid[order]
    counts = jnp.bincount(eid, length=N_EXPERTS)
    padded = (counts + MOE_BLOCK - 1) // MOE_BLOCK * MOE_BLOCK
    ends_pad = jnp.cumsum(padded)
    starts_pad = ends_pad - padded
    starts = jnp.cumsum(counts) - counts
    dest = starts_pad[se] + (jnp.arange(n_assign) - starts[se])
    n_rows = -(-(n_assign + N_EXPERTS * (MOE_BLOCK - 1)) // MOE_BLOCK) * MOE_BLOCK
    n_blocks = n_rows // MOE_BLOCK
    row_tok = jnp.zeros((n_rows,), jnp.int32).at[dest].set(tok[order])
    row_w = jnp.zeros((n_rows,), jnp.float32).at[dest].set(wt[order])
    block_e = jnp.minimum(jnp.searchsorted(ends_pad, jnp.arange(n_blocks) * MOE_BLOCK, side='right'),
                          N_EXPERTS - 1)
    xs = xt[row_tok].reshape(n_blocks, MOE_BLOCK, d)

    def expert_block(args):
        xb, e = args
        return (jax.nn.silu(xb @ w1[e]) * (xb @ w3[e])) @ w2[e]

    ys = lax.map(expert_block, (xs, block_e)).reshape(n_rows, d)
    out = jnp.zeros((t, d), h.dtype).at[row_tok].add((ys * row_w[:, None]).astype(h.dtype))
    return out.reshape(b, s, d)

def hybrid_layer(x, layer_idx, norm_mix_g, w_in, conv_w, conv_b, i_bias, f_bias, mnorm_g,
                 rel_bias, lam_p, dnorm_g, w_branch, w_gate, w_out, norm_ffn_g,
                 rgw, rgb, rew, reb, w1, w3, w2):
    b, s, d = x.shape
    h = rmsnorm(x, norm_mix_g)
    proj = jnp.einsum('bsd,dc->bsc', h, w_in)
    (qa, ka, va, qi, ki, wi, qb, kb, vb, ib, fb, ob, qc, kc, vc, qd, kd, vd) = split_columns(proj)

    y_a = dsa_mixer(qa.reshape(b, s, H_A, HEAD_DIM), ka.reshape(b, s, H_A, HEAD_DIM),
                    va.reshape(b, s, H_A, HEAD_DIM), qi.reshape(b, s, H_IDX, D_IDX), ki, wi)

    qk_b = jax.nn.silu(causal_dwconv(jnp.concatenate([qb, kb], axis=-1), conv_w, conv_b))
    y_b = mlstm_mixer(qk_b[..., :W_B].reshape(b, s, H_B, HEAD_DIM),
                      qk_b[..., W_B:].reshape(b, s, H_B, HEAD_DIM),
                      vb.reshape(b, s, H_B, HEAD_DIM), ib + i_bias, fb + f_bias,
                      ob.reshape(b, s, H_B, HEAD_DIM), mnorm_g)

    y_c = chunk_band_attention(qc.reshape(b, s, H_C, HEAD_DIM), kc.reshape(b, s, H_C, HEAD_DIM),
                               vc.reshape(b, s, H_C, HEAD_DIM), rel_bias)

    lam_init = 0.8 - 0.6 * math.exp(-0.3 * layer_idx)
    y_d = diff_attention(qd.reshape(b, s, H_D, 2, DQ_D), kd.reshape(b, s, H_D, 2, DQ_D),
                         vd.reshape(b, s, H_D, 2 * DQ_D), lam_p, dnorm_g, lam_init)

    branches = jnp.stack([y_a.reshape(b, s, W_BRANCH), y_b.reshape(b, s, W_BRANCH),
                          y_c.reshape(b, s, W_BRANCH), y_d.reshape(b, s, W_BRANCH)], axis=2)
    up = jnp.einsum('bsnw,nwd->bsnd', branches, w_branch)
    gates = jax.nn.sigmoid(jnp.einsum('bsd,de->bse', h, w_gate)).reshape(b, s, N_BRANCH, d)
    mixed = jnp.sum(gates * up, axis=2)
    x = x + jnp.einsum('bsd,de->bse', mixed, w_out)

    h2 = rmsnorm(x, norm_ffn_g)
    return x + hier_moe(h2, rgw, rgb, rew, reb, w1, w3, w2)

def setup_inputs(seed: int = 0) -> dict:
    key = jax.random.key(seed)
    ks = jax.random.split(key, 24)
    f32 = jnp.float32
    nl = DEPTH

    def nrm(k, shape, scale):
        return jax.random.normal(k, shape, f32) * scale

    return {
        'x': nrm(ks[0], (BATCH, SEQ, D_MODEL), 1.0),
        'norm_mix_g': 1.0 + nrm(ks[1], (nl, D_MODEL), 0.01),
        'w_in': nrm(ks[2], (nl, D_MODEL, C_IN), D_MODEL ** -0.5),
        'conv_w': nrm(ks[3], (nl, CONV_K, 2 * W_B), CONV_K ** -0.5),
        'conv_b': nrm(ks[4], (nl, 2 * W_B), 0.01),
        'mlstm_i_bias': nrm(ks[5], (nl, H_B), 0.1),
        'mlstm_f_bias': jnp.linspace(3.0, 6.0, H_B, dtype=f32)[None, :] + nrm(ks[6], (nl, H_B), 0.1),
        'mlstm_norm_g': 1.0 + nrm(ks[7], (nl, W_B), 0.01),
        'relpos_bias': nrm(ks[8], (nl, H_C, N_REL), 0.1),
        'diff_lambda': nrm(ks[9], (nl, 4, DQ_D), 0.1),
        'diff_norm_g': 1.0 + nrm(ks[10], (nl, W_D), 0.01),
        'w_branch': nrm(ks[11], (nl, N_BRANCH, W_BRANCH, D_MODEL), W_BRANCH ** -0.5),
        'w_gate': nrm(ks[12], (nl, D_MODEL, N_BRANCH * D_MODEL), D_MODEL ** -0.5),
        'w_out': nrm(ks[13], (nl, D_MODEL, D_MODEL), (N_BRANCH * D_MODEL) ** -0.5),
        'norm_ffn_g': 1.0 + nrm(ks[14], (nl, D_MODEL), 0.01),
        'router_group_w': nrm(ks[15], (nl, D_MODEL, N_GROUPS), D_MODEL ** -0.5),
        'router_group_b': nrm(ks[16], (nl, N_GROUPS), 0.01),
        'router_expert_w': nrm(ks[17], (nl, D_MODEL, N_EXPERTS), D_MODEL ** -0.5),
        'router_expert_b': nrm(ks[18], (nl, N_EXPERTS), 0.01),
        'expert_w1': nrm(ks[19], (nl, N_EXPERTS, D_MODEL, F_EXPERT), D_MODEL ** -0.5),
        'expert_w3': nrm(ks[20], (nl, N_EXPERTS, D_MODEL, F_EXPERT), D_MODEL ** -0.5),
        'expert_w2': nrm(ks[21], (nl, N_EXPERTS, F_EXPERT, D_MODEL), F_EXPERT ** -0.5),
        'final_norm_g': 1.0 + nrm(ks[22], (D_MODEL,), 0.01),
    }

def reference(x, norm_mix_g, w_in, conv_w, conv_b, mlstm_i_bias, mlstm_f_bias, mlstm_norm_g,
              relpos_bias, diff_lambda, diff_norm_g, w_branch, w_gate, w_out, norm_ffn_g,
              router_group_w, router_group_b, router_expert_w, router_expert_b,
              expert_w1, expert_w3, expert_w2, final_norm_g):
    for l in range(DEPTH):
        x = hybrid_layer(x, l, norm_mix_g[l], w_in[l], conv_w[l], conv_b[l], mlstm_i_bias[l],
                         mlstm_f_bias[l], mlstm_norm_g[l], relpos_bias[l], diff_lambda[l],
                         diff_norm_g[l], w_branch[l], w_gate[l], w_out[l], norm_ffn_g[l],
                         router_group_w[l], router_group_b[l], router_expert_w[l],
                         router_expert_b[l], expert_w1[l], expert_w3[l], expert_w2[l])
    return rmsnorm(x, final_norm_g)


_drawn_inputs = setup_inputs


def setup_inputs(seed=0):
    import zlib

    import numpy as np

    out = dict(_drawn_inputs(seed))
    spreads = {}
    factors = {'norm_mix_g': 2.824,
     'conv_b': 27.349,
     'mlstm_i_bias': 64.0,
     'mlstm_norm_g': 45.869,
     'relpos_bias': 8.0,
     'diff_lambda': 4.0,
     'diff_norm_g': 27.688,
     'router_group_b': 31.801,
     'router_expert_b': 11.526,
     'final_norm_g': 31.862,
     'norm_ffn_g': 5.579}
    for name, (base, spread) in spreads.items():
        noise = np.random.default_rng([zlib.crc32(name.encode()), seed]).standard_normal(out[name].shape)
        drawn = base * np.exp(spread * noise) if base else spread * noise
        out[name] = jnp.asarray(drawn.astype(out[name].dtype))
    for name, factor in factors.items():
        out[name] = (out[name] * factor).astype(out[name].dtype)
    return out
```

```python
from contextlib import ExitStack

import concourse.bass as bass
from concourse import mybir

F32 = mybir.dt.float32
F32R = mybir.dt.float32r
I32 = mybir.dt.int32
U32 = mybir.dt.uint32
ALU = mybir.AluOpType
ACT = mybir.ActivationFunctionType
AX = mybir.AxisListType

P = 128
SEQ = 1024
DM = 1024
NT = SEQ // P
KC = DM // P
CH = 64
HD = 64
NH = 4
W = NH * HD
DI = 32
TOPK = 256
EPS = 1e-6
NEG = -1e30
TAKEN = -3e38
N_REL = 192
BAND = 640
GW = W + 3 * NH
NG, EG, NE = 4, 8, 32
FE = 512
FT = FE // P
CAP = 96
N_OV = (2 * SEQ - NE) // CAP
SLOTS = (NE + N_OV) * CAP
KB = 1024

T_QI, T_KI, T_QB, T_KB, T_QC, T_KC, T_QD, T_KD, T_QA, T_KA = 0, 1, 2, 4, 6, 8, 10, 12, 14, 16
NTT = 18


def width(b):
    return (b + 1) * P


SEL_AT = {}
_at = 0
for _b in range(2, NT):
    SEL_AT[_b] = _at
    _at += width(_b)
SEL_COLS = _at


class Shared:
    pass


def chained(eng, chain):
    sem, count = chain

    def link(ins):
        count[0] += 1
        ins.then_inc(sem, 1)
        eng.wait_ge(sem, count[0])
    return link


def build(nc, a):
    ctx = ExitStack()
    with ctx:
        first = 16512
        ctx.enter_context(nc.sbuf_tensor("sbuf_room", [P, 207 * 256], F32))

        def sb(name, shape, at_kb, dt=F32):
            return nc.alloc_sbuf_tensor_at(name, shape, dt, offset=first + int(at_kb * KB))

        def sem(name):
            return ctx.enter_context(nc.semaphore(name))

        def dram(name, shape, dt=F32):
            return nc.dram_tensor(name, shape, dt, kind="Internal").ap()

        s = Shared()
        s.sb, s.sem, s.dram = sb, sem, dram
        s.dve_chain, s.act_chain, s.pool_chain = ((sem(n), [0]) for n in ("dve_chain", "act_chain", "pool_chain"))
        s.psum = ctx.enter_context(nc.psum_tensor("psum", [P, 8, 512], F32))
        s.ident = sb("ident", [P, P], 204)
        s.hT = sb("hT", [P, KC, SEQ], 0)
        s.tT = sb("tT", [P, NTT, SEQ], 32)
        s.vA = sb("vA", [P, NT, W], 104)
        s.vC = sb("vC", [P, NT, W], 112)
        s.vD = sb("vD", [P, NT, W], 120)
        s.vB = sb("vB", [P, NT, NH, HD + 1], 128)
        s.oB = sb("oB", [P, NT, W], 136.25)
        s.g12 = sb("g12", [P, NT, 3 * NH], 144.25)
        s.sel = sb("sel", [P, SEL_COLS], 144.75)
        s.negm = sb("negm", [NH, SEQ], 194)
        s.a_tok = sb("a_tok", [P, NT, NH], 204.5)
        s.enm = sb("enm", [P, NT, NH], 204.75)
        s.sel4 = sb("sel4", [NH, NH, P], 198)
        s.h2_rows = dram("h2_rows", [SEQ, DM])
        s.shifted = dram("shifted", [P, NH, 768])
        s.ys = dram("ys", [SLOTS, DM])
        s.y_stored = [sem(f"y_stored{i}") for i in range(2)]
        s.x_in = [sem(f"x_in{i}") for i in range(NT)]
        project(nc, a, s)
        attend(nc, a, s)

        s.x2 = [sb(f"x2_{t}", [P, DM], 32 + 16 * (t // 2) + 4 * (t % 2)) for t in range(NT)]
        s.gates = sb("gates", [P, 2, NT], 202)
        s.row_of = sb("row_of", [P, 2 * NT], 202.125, I32)
        s.tok_of = sb("tok_of", [CAP, NE + N_OV], 202.25, I32)
        s.ov_f = sb("ov_f", [1, 2, N_OV], 202.5)
        s.ov_i = sb("ov_i", [1, 2, N_OV], 202.75, I32)
        s.w1 = [sb(f"w1_{i}", [P, KC, FE], at) for i, at in enumerate((0, 96))]
        s.w3 = [sb(f"w3_{i}", [P, KC, FE], at) for i, at in enumerate((16, 112))]
        s.w2 = [sb(f"w2_{i}", [P, FT, DM], at) for i, at in enumerate((128, 160))]
        s.w1_in, s.w3_in, s.w2_in = ([sem(f"{n}_in{i}") for i in range(2)] for n in ("w1", "w3", "w2"))

        def load_expert(eng, e, j, which, done=None):
            dst, src, into = {"w1": (s.w1, a["expert_w1"], s.w1_in), "w3": (s.w3, a["expert_w3"], s.w3_in),
                              "w2": (s.w2, a["expert_w2"], s.w2_in)}[which]
            eng.dma_start(dst[j][:, :, :], src[bass.ds(e, 1)].rearrange("o (c p) n -> p (o c) n", p=P)
                          ).then_inc(into[j] if done is None else done, 16)
        s.load_expert = load_expert
        mix(nc, a, s)
        route(nc, a, s)
        experts(nc, a, s)
        combine(nc, a, s)
    return nc


def project(nc, a, s):
    sb, sem, psum = s.sb, s.sem, s.psum
    xs = sb("xs", [P, NT, DM], 40)
    wt = [sb(f"wt{i}", [P, KC, P], 161.5 + 4 * i) for i in range(2)]
    wk = sb("wk", [P, KC, 512], 169.5)
    relu = [sb(f"relu{i}", [P, SEQ], 185.5 + 4 * i) for i in range(2)]
    rows = [sb(f"rows{i}", [NH, SEQ], 104 + 4 * i) for i in range(4)]
    gT = sb("gT", [P, KC], 205)
    rstd = sb("rstd", [P, NT], 205.125)
    ssq = sb("ssq", [P, NT], 205.25)
    ifb = sb("ifb", [NH, 2], 205.375)
    conv = sb("conv", [P, 4, 5], 205.5)
    top8 = sb("top8", [P, 8], 205.75)
    eps = sb("eps", [P, 1], 205.875)
    one = sb("one", [NH, 1], 205.9375)
    zeros = sb("zeros", [CAP, DM], 120)
    far = sb("far", [P, NH, 768], 144.75)
    rel = sb("rel", [P, NH, N_REL], 157)

    x_in = s.x_in
    small_in, rel_in, far_ready, far_out = sem("small_in"), sem("rel_in"), sem("far_ready"), sem("far_out")
    w_in = [sem(f"w_in{i}") for i in range(2)]
    wk_in = sem("wk_in")
    ident_ready, const_ready = sem("ident_ready"), sem("const_ready")
    squared, mean_ready, root_ready, normed = sem("squared"), sem("mean_ready"), sem("root_ready"), sem("normed")
    xT_ready, xT_taken = sem("xT_ready"), sem("xT_taken")
    zeros_ready = sem("zeros_ready")
    tok_ready, tok_taken = sem("tok_ready"), sem("tok_taken")
    gate_rows, gate_rows_taken = sem("gate_rows"), sem("gate_rows_taken")
    soft_ready, rows_done = sem("soft_ready"), sem("rows_done")
    idx_proj, idx_proj_taken = sem("idx_proj"), sem("idx_proj_taken")
    idx_ready, idx_taken, relu_used = sem("idx_ready"), sem("idx_taken"), sem("relu_used")
    gate_cols, gate_cols_taken = sem("gate_cols"), sem("gate_cols_taken")
    proj_ready, proj_taken = sem("proj_ready"), sem("proj_taken")
    conv_ready, sig_ready = sem("conv_ready"), sem("sig_ready")

    idx_blocks = list(range(2, NT))
    NTOK = 3
    chunk_cols = [GW, 512, 512]
    NP = NTT - 2

    with nc.Block() as block:
        @block.sync
        def _(sp):
            sp.dma_start(gT[:, :], a["g_mix"]).then_inc(small_in, 16)
            sp.dma_start(ifb[:, :], a["if_bias"]).then_inc(small_in, 16)
            sp.dma_start(conv[:, :, :], a["conv"]).then_inc(small_in, 16)
            sp.dma_start(rel[:, :, :], a["rel"].partition_broadcast(P)).then_inc(rel_in, 16)
            for t in range(NT):
                sp.dma_start(xs[:, t, :], a["x"][t * P:(t + 1) * P, :]).then_inc(x_in[t], 16)
            sp.wait_ge(far_ready, 1)
            sp.dma_start(s.shifted, far[:, :, :]).then_inc(far_out, 16)
            sp.dma_start(wk[:, :, 0:GW], a["w_gates12"]).then_inc(wk_in, 16)
            for j in range(2):
                sp.dma_start(wt[j][:, :, :], a["w_T"][j]).then_inc(w_in[j], 16)
            sp.wait_ge(zeros_ready, 1)
            sp.dma_start(s.ys[NE * CAP:SLOTS, :].rearrange("(b p) n -> p b n", p=CAP),
                         zeros[:, :].unsqueeze(1).to_broadcast([CAP, N_OV, DM])).then_inc(s.y_stored[1], 16)
            for c in range(2):
                sp.wait_ge(tok_ready, NT * (c + 1))
                sp.dma_start(wk[:, :, :], a["w_V"][c]).then_inc(wk_in, 16)
            sp.wait_ge(idx_proj, 1)
            sp.dma_start(wt[0][:, :, :], a["w_T"][2]).then_inc(w_in[0], 16)
            sp.wait_ge(idx_proj, 2)
            sp.dma_start(wt[1][:, :, :], a["w_T"][3]).then_inc(w_in[1], 16)
            with sp.Fori(1, NP // 2) as i:
                for j in range(2):
                    sp.wait_ge(proj_ready, i * 2 + (j - 1))
                    sp.dma_start(wt[j][:, :, :], a["w_T"][bass.ds(i * 2 + (2 + j), 1)]
                                 .rearrange("o p c n -> (o p) c n")).then_inc(w_in[j], 16)

        @block.gpsimd
        def _(pool):
            pool.memset(s.ident[:, :], 0.0).then_inc(ident_ready, 1)
            pool.wait_ge(ident_ready, 1)
            pool.affine_select(out=s.ident[:, :], in_=s.ident[:, :], compare_op=ALU.not_equal, fill=1.0,
                               base=0, pattern=[[-1, P]], channel_multiplier=1).then_inc(ident_ready, 1)
            pool.memset(zeros[:, :], 0.0).then_inc(zeros_ready, 1)
            pool.memset(eps[:, :], EPS).then_inc(const_ready, 1)
            pool.memset(one[:, :], 1.0).then_inc(const_ready, 1)
            pool.memset(s.sel4[:, :, :], 0.0).then_inc(const_ready, 1)
            pool.wait_ge(const_ready, 3)
            pool.affine_select(out=s.sel4[:, :, :], in_=s.sel4[:, :, :], compare_op=ALU.not_equal, fill=1.0,
                               base=0, pattern=[[-1, NH], [0, P]], channel_multiplier=1).then_inc(const_ready, 1)
            pool.memset(s.vB[:, :, :, HD:HD + 1], 1.0).then_inc(const_ready, 1)
            pool.wait_ge(rel_in, 16)
            pool.tensor_copy(far[:, :, 0:511], rel[:, :, 0:1].to_broadcast([P, NH, 511]))
            pool.tensor_copy(far[:, :, 511:511 + N_REL], rel[:, :, :])
            pool.tensor_copy(far[:, :, 511 + N_REL:768],
                             rel[:, :, N_REL - 1:N_REL].to_broadcast([P, NH, 768 - 511 - N_REL])).then_inc(far_ready, 1)

        @block.scalar
        def _(act):
            link = chained(act, s.act_chain)
            for t in range(NT):
                act.wait_ge(x_in[t], 16)
                nc.scalar.activation(relu[t % 2][:, :], xs[:, t, :], ACT.Square,
                                     accum_out=ssq[:, t:t + 1]).then_inc(squared, 1)
                if t < NT - 1:
                    act.wait_ge(squared, t + 1)
            act.wait_ge(mean_ready, 1)
            act.wait_ge(const_ready, 5)
            nc.scalar.activation(rstd[:, :], ssq[:, :], ACT.Sqrt, bias=eps[:, 0:1],
                                 scale=1.0 / DM).then_inc(root_ready, 1)
            act.wait_ge(small_in, 48)
            for n in range(2 * KC):
                h, c = n // KC, n % KC
                act.wait_ge(xT_ready, n + 1)
                nc.scalar.activation(s.hT[:, c, h * 512:(h + 1) * 512], psum[:, n % 4, :], ACT.Copy,
                                     scale=gT[:, c:c + 1]).then_inc(xT_taken, 1)
            for t in range(NT):
                act.wait_ge(tok_ready, t + 1)
                nc.scalar.activation(s.g12[:, t, :], psum[:, t % 4, W:GW], ACT.Copy)
                nc.scalar.activation(s.oB[:, t, :], psum[:, t % 4, 0:W], ACT.Sigmoid).then_inc(tok_taken, 1)
            act.wait_ge(gate_rows, 2)
            link(nc.scalar.activation(rows[0][:, :], psum[0:NH, 4:6, :].rearrange("p a b -> p (a b)"),
                                      ACT.Identity, bias=ifb[:, 0:1]))
            link(nc.scalar.activation(rows[1][:, :], psum[0:NH, 6:8, :].rearrange("p a b -> p (a b)"),
                                      ACT.Identity, bias=ifb[:, 1:2]))
            link(nc.scalar.activation(rows[2][:, :], rows[1][:, :], ACT.Abs))
            link(nc.scalar.activation(rows[2][:, :], rows[2][:, :], ACT.Exp, scale=-1.0))
            nc.scalar.activation(rows[2][:, :], rows[2][:, :], ACT.Ln, bias=one[:, 0:1]).then_inc(soft_ready, 1)
            for n in range(4):
                act.wait_ge(idx_proj, n // 2 + 1)
                nc.scalar.activation(s.tT[:, n // 2, (n % 2) * 512:(n % 2 + 1) * 512], psum[:, n, :],
                                     ACT.Copy).then_inc(idx_proj_taken, 1)
            n = 0
            for b in idx_blocks:
                for h in range(NH):
                    act.wait_ge(idx_ready, n + 1)
                    if n >= 2:
                        act.wait_ge(relu_used, n - 1)
                    k = 4 + 2 * (n % 2)
                    nc.scalar.activation(relu[n % 2][:, 0:width(b)],
                                         psum[:, k:k + 2, :].rearrange("p a b -> p (a b)")[:, 0:width(b)],
                                         ACT.Relu).then_inc(idx_taken, 1)
                    n += 1
            act.wait_ge(gate_cols, 1)
            nc.scalar.activation(s.a_tok[:, :, :], psum[:, 0, 0:NT * NH].rearrange("p (t h) -> p t h", h=NH),
                                 ACT.Copy).then_inc(gate_cols_taken, 1)
            nc.scalar.activation(s.enm[:, :, :], psum[:, 0, NT * NH:2 * NT * NH]
                                 .rearrange("p (t h) -> p t h", h=NH), ACT.Exp).then_inc(gate_cols_taken, 1)
            act.wait_ge(s.y_stored[1], 16)
            for c in range(2):
                for t in range(NT):
                    n = NT * (c + 1) + t
                    act.wait_ge(tok_ready, n + 1)
                    if c == 0:
                        nc.scalar.activation(s.vA[:, t, :], psum[:, t % 4, 0:W], ACT.Copy)
                        nc.scalar.activation(s.vC[:, t, :], psum[:, t % 4, W:2 * W], ACT.Copy).then_inc(tok_taken, 1)
                    else:
                        nc.scalar.activation(s.vB[:, t, :, 0:HD],
                                             psum[:, t % 4, 0:W].rearrange("p (h d) -> p h d", d=HD), ACT.Copy)
                        nc.scalar.activation(s.vD[:, t, :], psum[:, t % 4, W:2 * W], ACT.Copy).then_inc(tok_taken, 1)
            with act.Fori(0, NP // 2) as i:
                for j in range(2):
                    act.wait_ge(proj_ready, i * 2 + (j + 1))
                    nc.scalar.activation(s.tT[:, bass.ds(i * 2 + (2 + j), 1), :].rearrange("p o n -> p (o n)"),
                                         psum[:, 2 * j:2 * j + 2, :].rearrange("p a b -> p (a b)"),
                                         ACT.Copy).then_inc(proj_taken, 1)
            for n in range(4):
                act.wait_ge(conv_ready, n + 1)
                nc.scalar.activation(relu[n % 2][:, :], wk[:, 2 * (n % 2):2 * (n % 2) + 2, :]
                                     .rearrange("p a b -> p (a b)"), ACT.Sigmoid).then_inc(sig_ready, 1)

        @block.vector
        def _(dve):
            link = chained(dve, s.dve_chain)
            dve.wait_ge(squared, NT)
            nc.vector.engine_nop().then_inc(mean_ready, 1)
            dve.wait_ge(root_ready, 1)
            link(nc.vector.reciprocal(rstd[:, :], rstd[:, :]))
            for t in range(NT):
                nc.vector.tensor_scalar(xs[:, t, :], xs[:, t, :], rstd[:, t:t + 1], None,
                                        ALU.mult).then_inc(normed, 1)
            dve.wait_ge(soft_ready, 1)
            link(nc.vector.tensor_scalar(rows[1][:, :], rows[1][:, :], 0.0, None, ALU.min))
            link(nc.vector.tensor_tensor(rows[1][:, :], rows[1][:, :], rows[2][:, :], ALU.subtract))
            link(nc.vector.memset(rows[3][:, :], 1.0))
            link(nc.vector.tensor_tensor_scan(rows[2][:, :], rows[3][:, :], rows[1][:, :], 0.0,
                                              ALU.mult, ALU.add))
            link(nc.vector.tensor_tensor(rows[0][:, :], rows[0][:, :], rows[2][:, :], ALU.subtract))
            link(nc.vector.tensor_tensor_scan(rows[3][:, :], rows[0][:, :], rows[0][:, :], 0.0,
                                              ALU.max, ALU.max))
            link(nc.vector.tensor_scalar(s.negm[:, :], rows[3][:, :], -1.0, None, ALU.mult))
            nc.vector.tensor_tensor(rows[1][:, :], s.negm[:, :], rows[2][:, :],
                                    ALU.subtract).then_inc(rows_done, 1)
            dve.wait_ge(far_out, 16)
            n = 0
            for b in idx_blocks:
                wd = width(b)
                sc = s.sel[:, SEL_AT[b]:SEL_AT[b] + wd]
                for h in range(NH):
                    dve.wait_ge(idx_taken, n + 1)
                    wi = s.g12[:, b, h:h + 1]
                    if h == 0:
                        ins = nc.vector.tensor_scalar(sc, relu[n % 2][:, 0:wd], wi, None, ALU.mult)
                    else:
                        ins = nc.vector.scalar_tensor_tensor(out=sc, in0=relu[n % 2][:, 0:wd], scalar=wi, in1=sc,
                                                             op0=ALU.mult, op1=ALU.add)
                    ins.then_inc(relu_used, 1)
                    n += 1
                    dve.wait_ge(relu_used, n)
                link(nc.vector.memset(s.sel[0:CH, SEL_AT[b] + wd - CH:SEL_AT[b] + wd], NEG))
            for b in idx_blocks:
                wd = width(b)
                sc = s.sel[:, SEL_AT[b]:SEL_AT[b] + wd]
                for _ in range(TOPK // 8):
                    link(nc.vector.max(top8[:, :], sc))
                    link(nc.vector.match_replace(sc, top8[:, :], sc, TAKEN))
                link(nc.vector.tensor_scalar(sc, sc, 0.5 * TAKEN, NEG, ALU.is_gt, ALU.mult))
            for n in range(4):
                if n == 0:
                    dve.wait_ge(proj_taken, NP)
                    dve.wait_ge(small_in, 48)
                src = s.tT[:, T_QB + n, :]
                y = wk[:, 2 * (n % 2):2 * (n % 2) + 2, :].rearrange("p a b -> p (a b)")
                link(nc.vector.tensor_scalar(y, src, conv[:, n, 3:4], conv[:, n, 4:5], ALU.mult, ALU.add))
                for k in range(3):
                    d = 3 - k
                    ins = nc.vector.scalar_tensor_tensor(out=y[:, d:], in0=src[:, 0:SEQ - d],
                                                         scalar=conv[:, n, k:k + 1], in1=y[:, d:],
                                                         op0=ALU.mult, op1=ALU.add)
                    if k < 2:
                        link(ins)
                ins.then_inc(conv_ready, 1)
                dve.wait_ge(sig_ready, n + 1)
                link(nc.vector.tensor_tensor(src, y, relu[n % 2][:, :], ALU.mult))

        @block.tensor
        def _(pe):
            pe.wait_ge(ident_ready, 2)
            for n in range(2 * KC):
                h, c = n // KC, n % KC
                pe.wait_ge(normed, 4 * (h + 1))
                if n >= 4:
                    pe.wait_ge(xT_taken, n - 3)
                for t in range(4):
                    ins = nc.tensor.transpose(psum[:, n % 4, t * P:(t + 1) * P],
                                              xs[:, 4 * h + t, c * P:(c + 1) * P], s.ident[:, :])
                ins.then_inc(xT_ready, 1)

            def tok_chunk(c):
                cols = chunk_cols[c]
                pe.wait_ge(wk_in, 16 * (c + 1))
                for t in range(NT):
                    n = c * NT + t
                    if c == 0:
                        pe.wait_ge(xT_taken, 2 * KC if t >= 4 else KC)
                        if t == 0:
                            pe.wait_ge(xT_taken, 2 * KC)
                    if n >= 4:
                        pe.wait_ge(tok_taken, n - 3)
                    for k in range(KC):
                        ins = nc.tensor.matmul(psum[:, n % 4, 0:cols], s.hT[:, k, t * P:(t + 1) * P],
                                               wk[:, k, 0:cols], start=(k == 0), stop=(k == KC - 1))
                    ins.then_inc(tok_ready, 1)

            tok_chunk(0)
            pe.wait_ge(tok_taken, NT)
            for g in range(2):
                for t in range(NT):
                    ins = nc.tensor.transpose(psum[0:NH, 4 + 2 * g + t // 4, (t % 4) * P:(t % 4 + 1) * P],
                                              s.g12[:, t, NH * (g + 1):NH * (g + 2)], s.ident[:, :])
                ins.then_inc(gate_rows, 1)

            def tile(j, bank):
                for h in range(2):
                    for k in range(KC):
                        ins = nc.tensor.matmul(psum[:, bank + h, :], wt[j][:, k, :],
                                               s.hT[:, k, h * 512:(h + 1) * 512],
                                               start=(k == 0), stop=(k == KC - 1))
                return ins

            for j in range(2):
                pe.wait_ge(w_in[j], 16)
                tile(j, 2 * j).then_inc(idx_proj, 1)
            pe.wait_ge(idx_proj_taken, 4)
            pe.wait_ge(soft_ready, 1)
            n = 0
            for b in idx_blocks:
                wd = width(b)
                for h in range(NH):
                    if n >= 2:
                        pe.wait_ge(idx_taken, n - 1)
                    for c0 in range(0, wd, 512):
                        c1 = min(wd, c0 + 512)
                        ins = nc.tensor.matmul(psum[:, 4 + 2 * (n % 2) + c0 // 512, 0:c1 - c0],
                                               s.tT[DI * h:DI * (h + 1), T_QI, b * P:(b + 1) * P],
                                               s.tT[DI * h:DI * (h + 1), T_KI, c0:c1], start=True, stop=True)
                    ins.then_inc(idx_ready, 1)
                    n += 1
            pe.wait_ge(rows_done, 1)
            for g in range(2):
                for t in range(NT):
                    at = (g * NT + t) * NH
                    ins = nc.tensor.transpose(psum[:, 0, at:at + NH], rows[g][:, t * P:(t + 1) * P],
                                              s.ident[0:NH, 0:NH])
            ins.then_inc(gate_cols, 1)
            pe.wait_ge(gate_cols_taken, 2)
            tok_chunk(1)
            tok_chunk(2)
            pe.wait_ge(tok_taken, 3 * NT)
            for j in range(2):
                pe.wait_ge(w_in[j], 32)
                tile(j, 2 * j).then_inc(proj_ready, 1)
            with pe.Fori(1, NP // 2) as i:
                for j in range(2):
                    pe.wait_ge(w_in[j], i * 16 + 32)
                    pe.wait_ge(proj_taken, i * 2 + (j - 1))
                    tile(j, 2 * j).then_inc(proj_ready, 1)


def attend(nc, a, s):
    sb, sem, psum = s.sb, s.sem, s.psum
    pbuf = [sb(f"pbuf{i}", [P, SEQ], 161.5 + 4 * i) for i in range(4)]
    pt = [sb(f"pt{i}", [P, 512], 177.5 + 2 * i) for i in range(4)]
    sq = sb("sq", [P, NT, NH, HD], 185.5)
    bias = sb("bias", [P, NH, BAND], 194)
    mask01 = sb("mask01", [P, 3 * P], 185.5)
    y = {"B": sb("yB", [P, NT, W], 32), "D": sb("yD", [P, NT, W], 128),
         "C": sb("yC", [P, NT, W], 32), "A": sb("yA", [P, NT, W], 128)}
    yT_at = {"B": T_QB, "D": T_QD, "C": T_QC, "A": T_QA}
    gainB = sb("gainB", [P, W], 200)
    gainD = sb("gainD", [P, W], 193.5 + 12.5)
    lam_in = sb("lam_in", [P, 4, DI], 201)
    lam = sb("lam", [P, 8], 204.875)
    a_neg = sb("a_neg", [P, NT, NH], 205)
    stat = sb("stat", [P, 4, 8], 205.125)
    sums = sb("sums", [P, 2, NH, 2], 205.25)
    inv = sb("inv", [P, NH], 205.375)
    ms = {"B": sb("msB", [P, NT * NH], 205.5), "D": sb("msD", [P, NT * NH], 205.625)}
    eps = sb("eps2", [P, 1], 205.875)

    loads_in, bias_in = sem("loads_in"), sem("bias_in")
    b_scores, b_mrow, b_exp, b_masked = sem("b_scores"), sem("b_mrow"), sem("b_exp"), sem("b_masked")
    b_weights, b_pv, b_normed = sem("b_weights"), sem("b_pv"), sem("b_normed")
    scores_ready, stats_ready, exp_done = sem("scores_ready"), sem("stats_ready"), sem("exp_done")
    diff_ready, pt_ready, pt_copied = sem("diff_ready"), sem("pt_ready"), sem("pt_copied")
    pv_done, out_normed = sem("pv_done"), sem("out_normed")
    squares_summed, roots, inverse, y_ready = sem("squares_summed"), sem("roots"), sem("inverse"), sem("y_ready")
    gain_ready, lam_ready, bias_ready, mask_ready = sem("gain_ready"), sem("lam_ready"), sem("bias_ready"), sem("mask_ready")
    aneg_ready = sem("aneg_ready")

    NB = NT * NH
    Y_AT = 24
    b_units = [(b, h) for b in range(NT) for h in range(NH)]
    units = [(kind, b, h) for kind in "DCA" for b, h in b_units]
    NU = len(units)

    def keys(kind, b):
        k0 = max(0, b - BAND // P + 1) if kind == "C" else 0
        return k0, b + 1 - k0

    def slots(u):
        return (0, 1) if units[u][0] == "D" else (u % 2,)

    def bufs(u):
        return (2 * (u % 2), 2 * (u % 2) + 1) if units[u][0] == "D" else (u % 4,)

    def before(u, of):
        mine = set(of(u))
        return max((v for v in range(u) if mine & set(of(v))), default=None)

    groups = []
    for u, (kind, b, h) in enumerate(units):
        k0, nk = keys(kind, b)
        for g0 in range(0, nk, 4):
            groups.append((u, g0, min(4, nk - g0), g0 + 4 >= nk))
        if u % NB == Y_AT:
            groups += [({"D": "B", "C": "D", "A": "C"}[kind], g, 4, False) for g in range(4)]
    groups += [("A", g, 4, False) for g in range(4)]
    ready_after = {g[0]: i + 1 for i, g in enumerate(groups)}
    pv_after, _m = {}, 0
    for g in groups:
        if not isinstance(g[0], str):
            _m += 1
            pv_after[g[0]] = _m

    def slot_cols(slot, n):
        return psum[:, 2 * slot:2 * slot + 2, :].rearrange("p a b -> p (a b)")[:, 0:n]

    out_heads = [psum[:, 6 + k, 0:NH * (HD + 1)].rearrange("p (h d) -> p h d", d=HD + 1) for k in range(2)]

    with nc.Block() as block:
        @block.sync
        def _(sp):
            sp.dma_start(gainB[:, :], a["g_mlstm"].partition_broadcast(P)).then_inc(loads_in, 16)
            sp.dma_start(gainD[:, :], a["g_diff"].partition_broadcast(P)).then_inc(loads_in, 16)
            sp.dma_start(lam_in[:, :, :], a["lam"].partition_broadcast(P)).then_inc(loads_in, 16)
            sp.wait_ge(b_pv, NB)
            sp.wait_ge(b_exp, NB)
            sp.wait_ge(gain_ready, 1)
            sp.wait_ge(lam_ready, 1)
            sp.dma_start(bias[:, :, :], bass.AP(s.shifted.tensor, P - 1, [[NH * 768 - 1, P], [768, NH], [1, BAND]])
                         ).then_inc(bias_in, 16)

        @block.gpsimd
        def _(pool):
            link = chained(pool, s.pool_chain)
            pool.memset(eps[:, :], EPS).then_inc(aneg_ready, 1)
            pool.wait_ge(loads_in, 48)
            for t in range(NT):
                ins = pool.tensor_tensor(s.oB[:, t, :], s.oB[:, t, :], gainB[:, :], ALU.mult)
            ins.then_inc(gain_ready, 1)
            pool.wait_ge(gain_ready, 1)
            link(pool.tensor_scalar(gainD[:, :], gainD[:, :], 0.8, 0.0, ALU.mult, ALU.add))
            for u, (b, h) in enumerate(b_units):
                pool.wait_ge(b_exp, u + 1)
                e = pbuf[u % 2][:, b * P:(b + 1) * P]
                pool.affine_select(out=e, in_=e, compare_op=ALU.is_ge, fill=0.0, base=0,
                                   pattern=[[1, P]], channel_multiplier=-1).then_inc(b_masked, 1)

            def head_norm(kind, n, waits):
                sem_, value = waits
                pool.wait_ge(sem_, value)
                yy = y[kind][:, :, :].rearrange("p t (h d) -> p (t h) d", d=HD)
                link(pool.tensor_tensor(sq[:, :, :, :].rearrange("p t h d -> p (t h) d"), yy, yy, ALU.mult))
                q = sq[:, :, :, :].rearrange("p t h d -> p (t h) d")
                half = HD // 2
                while half:
                    ins = pool.tensor_tensor(q[:, :, 0:half], q[:, :, 0:half], q[:, :, half:2 * half], ALU.add)
                    if half > 1:
                        link(ins)
                    half //= 2
                ins.then_inc(squares_summed, 1)
                pool.wait_ge(inverse, n + 1)
                link(pool.tensor_tensor(yy, yy, ms[kind][:, :].unsqueeze(2).to_broadcast([P, NT * NH, HD]), ALU.mult))

            head_norm("B", 0, (b_normed, NT))
            pool.tensor_tensor(y["B"][:, :, :], y["B"][:, :, :], s.oB[:, :, :], ALU.mult).then_inc(y_ready, 1)
            pool.wait_ge(bias_in, 16)
            link(pool.tensor_scalar(bias[:, :, :], bias[:, :, :], 8.0, 0.0, ALU.mult, ALU.add))
            pool.memset(bias[0:CH, :, BAND - CH:BAND], NEG)
            pool.memset(bias[CH:P, :, 0:CH], NEG).then_inc(bias_ready, 1)
            head_norm("D", 1, (out_normed, NT))
            pool.tensor_tensor(y["D"][:, :, :], y["D"][:, :, :],
                               gainD[:, :].unsqueeze(1).to_broadcast([P, NT, W]), ALU.mult).then_inc(y_ready, 1)
            pool.wait_ge(y_ready, 2)
            link(pool.memset(mask01[:, :], 0.0))
            pool.memset(mask01[0:CH, CH:P], NEG)
            pool.memset(mask01[0:CH, 3 * P - CH:3 * P], NEG).then_inc(mask_ready, 1)

        @block.scalar
        def _(act):
            link = chained(act, s.act_chain)
            link(nc.scalar.activation(a_neg[:, :, :], s.a_tok[:, :, :], ACT.Copy, scale=-1.0))
            act.wait_ge(lam_ready, 1)
            nc.scalar.activation(lam[:, 2:4], lam[:, 0:2], ACT.Exp).then_inc(lam_ready, 1)
            for u, (b, h) in enumerate(b_units):
                act.wait_ge(b_mrow, b + 1)
                if u >= 2:
                    act.wait_ge(b_weights, u - 1)
                m = psum[:, 4 + b % 2, h * P:(h + 1) * P]
                diag = pbuf[u % 2][:, b * P:(b + 1) * P]
                link(nc.scalar.activation(diag, m, ACT.Relu, bias=a_neg[:, b, h:h + 1], scale=-1.0))
                for j in range(b):
                    nc.scalar.activation(pbuf[u % 2][:, j * P:(j + 1) * P], m, ACT.Exp, bias=s.a_tok[:, j, h:h + 1])
                nc.scalar.activation(diag, diag, ACT.Exp, scale=-1.0).then_inc(b_exp, 1)

            def root(n):
                kind = "BD"[n]
                act.wait_ge(squares_summed, n + 1)
                act.wait_ge(aneg_ready, 1)
                nc.scalar.activation(ms[kind][:, :], sq[:, :, :, 0:1].rearrange("p t h o -> p (t h o)"), ACT.Sqrt,
                                     bias=eps[:, 0:1], scale=1.0 / HD).then_inc(roots, 1)

            at, m = 0, 0
            for u in range(NU + 1):
                kind, b, h = units[u] if u < NU else ("", 0, 0)
                if u < NU:
                    wd = keys(kind, b)[1] * P
                    prev = before(u, bufs)
                    if kind == "D":
                        if prev is None:
                            act.wait_ge(b_pv, NB)
                            act.wait_ge(b_weights, NB)
                        else:
                            act.wait_ge(pt_ready, ready_after[prev])
                    if h == 0 and u // NH >= 2:
                        act.wait_ge(out_normed, u // NH - 1)
                    act.wait_ge(stats_ready, u + 1)

                def diff_exp(r):
                    nc.scalar.activation(pbuf[bufs(u)[r]][:, 0:wd], slot_cols(r, wd), ACT.Exp,
                                         bias=stat[:, u % 4, 2 + r:3 + r], scale=DI ** -0.5,
                                         accum_out=sums[:, b % 2, h, r:r + 1]).then_inc(exp_done, 1)
                if kind == "D":
                    diff_exp(0)
                elif kind:
                    buf = pbuf[bufs(u)[0]][:, 0:wd]
                    nc.scalar.activation(buf, buf, ACT.Exp, bias=stat[:, u % 4, 0:1], scale=-1.0,
                                         accum_out=sums[:, b % 2, h, 0:1]).then_inc(exp_done, 1)
                if u == 12:
                    root(0)
                if u == NB + 12:
                    root(1)
                while u and at < len(groups) and (isinstance(groups[at][0], str) or groups[at][0] < u):
                    what, g0, ng, last = groups[at]
                    act.wait_ge(pt_ready, at + 1)
                    src = psum[:, 4 + at % 2, 0:ng * P]
                    if isinstance(what, str):
                        c, t0 = g0 % 2, g0 // 2 * 4
                        dst = s.tT[:, yT_at[what] + c, t0 * P:(t0 + 4) * P]
                    else:
                        dst = pt[m % 4][:, 0:ng * P]
                        if m >= 4:
                            act.wait_ge(pv_done, m - 3)
                        m += 1
                    nc.scalar.activation(dst, src, ACT.Copy).then_inc(pt_copied, 1)
                    at += 1
                if kind == "D":
                    diff_exp(1)

        @block.vector
        def _(dve):
            link = chained(dve, s.dve_chain)
            dve.wait_ge(loads_in, 48)
            for k in range(2):
                ins = nc.vector.tensor_tensor_reduce(out=lam_in[:, 2 * k, :], in0=lam_in[:, 2 * k, :],
                                                     in1=lam_in[:, 2 * k + 1, :], scale=1.0, scalar=0.0,
                                                     op0=ALU.mult, op1=ALU.add, accum_out=lam[:, k:k + 1])
            ins.then_inc(lam_ready, 1)
            dve.wait_ge(lam_ready, 2)
            link(nc.vector.tensor_tensor(lam[:, 4:5], lam[:, 3:4], lam[:, 2:3], ALU.subtract))
            link(nc.vector.tensor_scalar(lam[:, 4:5], lam[:, 4:5], -0.2, None, ALU.add))

            def b_norm(b):
                dve.wait_ge(b_pv, NH * (b + 1))
                o = out_heads[b % 2]
                link(nc.vector.tensor_tensor(inv[:, :], o[:, :, HD], s.enm[:, b, :], ALU.max))
                link(nc.vector.scalar_tensor_tensor(out=inv[:, :], in0=o[:, :, HD], scalar=-1.0,
                                                    in1=inv[:, :], op0=ALU.mult, op1=ALU.max))
                link(nc.vector.reciprocal(inv[:, :], inv[:, :]))
                nc.vector.tensor_tensor(y["B"][:, b, :].rearrange("p (h d) -> p h d", d=HD), o[:, :, 0:HD],
                                        inv[:, :].unsqueeze(2).to_broadcast([P, NH, HD]),
                                        ALU.mult).then_inc(b_normed, 1)

            for u, (b, h) in enumerate(b_units):
                wd = width(b)
                dve.wait_ge(b_scores, u + 1)
                dve.wait_ge(b_masked, u + 1)
                if u >= 2:
                    dve.wait_ge(b_pv, u - 1)
                nc.vector.scalar_tensor_tensor(out=pbuf[2 + u % 2][:, 0:wd], in0=slot_cols(u % 2, wd),
                                               scalar=HD ** -0.5, in1=pbuf[u % 2][:, 0:wd],
                                               op0=ALU.mult, op1=ALU.mult).then_inc(b_weights, 1)
                if h == 1 and b:
                    b_norm(b - 1)
            b_norm(NT - 1)

            def norm(n):
                kind, b = units[n * NH][0:2]
                dve.wait_ge(pv_done, pv_after[n * NH + NH - 1])
                link(nc.vector.reciprocal(inv[:, :], sums[:, b % 2, :, 0]))
                if kind == "C" and b == 0:
                    dve.wait_ge(pt_copied, copied_before[NB + 1])
                if kind == "A" and b == 0:
                    dve.wait_ge(pt_copied, copied_before[2 * NB + 1])
                nc.vector.tensor_tensor(y[kind][:, b, :].rearrange("p (h d) -> p h d", d=HD),
                                        psum[:, 6 + n % 2, 0:W].rearrange("p (h d) -> p h d", d=HD),
                                        inv[:, :].unsqueeze(2).to_broadcast([P, NH, HD]),
                                        ALU.mult).then_inc(out_normed, 1)

            copied_before = {v: sum(1 for g in groups[:next(i for i, x in enumerate(groups) if x[0] == v)])
                             for v in (NB + 1, 2 * NB + 1)}
            n_slot, n_diff = 0, 0
            for u in range(NU + 3):
                if 0 < u <= NU and units[u - 1][0] == "D":
                    v = u - 1
                    _, b, h = units[v]
                    wd = width(b)
                    dve.wait_ge(exp_done, 2 * v + 2)
                    link(nc.vector.reciprocal(stat[:, v % 4, 4:5], sums[:, b % 2, h, 1:2]))
                    link(nc.vector.scalar_tensor_tensor(out=stat[:, v % 4, 5:6], in0=stat[:, v % 4, 4:5],
                                                        scalar=sums[:, b % 2, h, 0:1], in1=lam[:, 4:5],
                                                        op0=ALU.mult, op1=ALU.mult))
                    p0, p1 = (pbuf[k][:, 0:wd] for k in bufs(v))
                    nc.vector.scalar_tensor_tensor(out=p0, in0=p1, scalar=stat[:, v % 4, 5:6], in1=p0,
                                                   op0=ALU.mult, op1=ALU.add).then_inc(diff_ready, 1)
                if u < NU:
                    kind, b, h = units[u]
                    k0, nk = keys(kind, b)
                    wd = nk * P
                    if kind == "D":
                        for r in range(2):
                            dve.wait_ge(scores_ready, n_slot + 1)
                            n_slot += 1
                            link(nc.vector.memset(psum[0:CH, 2 * r + (wd - CH) // 512, (wd - CH) % 512:
                                                       (wd - CH) % 512 + CH], NEG))
                            link(nc.vector.reduce_max(stat[:, u % 4, r:r + 1], slot_cols(r, wd), AX.X))
                        nc.vector.tensor_scalar(stat[:, u % 4, 2:4], stat[:, u % 4, 0:2], -DI ** -0.5, None,
                                                ALU.mult).then_inc(stats_ready, 1)
                    else:
                        dve.wait_ge(scores_ready, n_slot + 1)
                        n_slot += 1
                        prev = before(u, bufs)
                        dve.wait_ge(pt_ready, ready_after[prev])
                        if kind == "C":
                            dve.wait_ge(bias_ready, 1)
                            add = bias[:, h, BAND - wd:BAND]
                        elif b < 2:
                            dve.wait_ge(mask_ready, 1)
                            add = mask01[:, b * P:b * P + wd]
                        else:
                            add = s.sel[:, SEL_AT[b]:SEL_AT[b] + wd]
                        nc.vector.tensor_tensor_reduce(out=pbuf[bufs(u)[0]][:, 0:wd], in0=slot_cols(slots(u)[0], wd),
                                                       in1=add, scale=-HD ** -0.5, scalar=3e38, op0=ALU.add,
                                                       op1=ALU.min, accum_out=stat[:, u % 4, 0:1]
                                                       ).then_inc(stats_ready, 1)
                if u >= 3 and (u - 3) % NH == NH - 1:
                    norm((u - 3) // NH)
                if u == 13:
                    dve.wait_ge(roots, 1)
                    nc.vector.reciprocal(ms["B"][:, :], ms["B"][:, :]).then_inc(inverse, 1)
                if u == NB + 13:
                    dve.wait_ge(roots, 2)
                    nc.vector.reciprocal(ms["D"][:, :], ms["D"][:, :]).then_inc(inverse, 1)

        @block.tensor
        def _(pe):
            qk = {"B": (T_QB, T_KB), "C": (T_QC, T_KC), "A": (T_QA, T_KA)}

            def head(kind, h, t0, n):
                r = HD * (h % 2)
                return s.tT[r:r + HD, kind + h // 2, t0 * P:(t0 + n) * P]

            def b_score(u):
                b, h = b_units[u]
                if h == 0:
                    if b >= 2:
                        pe.wait_ge(b_exp, NH * (b - 1))
                    for g in range(NH):
                        ins = nc.tensor.matmul(psum[:, 4 + b % 2, g * P:(g + 1) * P], s.sel4[:, g, :],
                                               s.negm[:, b * P:(b + 1) * P], start=True, stop=True)
                    ins.then_inc(b_mrow, 1)
                if u >= 2:
                    pe.wait_ge(b_weights, u - 1)
                for j in range(b + 1):
                    ins = nc.tensor.matmul(slot_cols(u % 2, SEQ)[:, j * P:(j + 1) * P], head(T_KB, h, j, 1),
                                           head(T_QB, h, b, 1), start=True, stop=True)
                ins.then_inc(b_scores, 1)

            b_score(0)
            for u, (b, h) in enumerate(b_units):
                if u + 1 < NB:
                    b_score(u + 1)
                pe.wait_ge(b_weights, u + 1)
                if h == 0 and b >= 2:
                    pe.wait_ge(b_normed, b - 1)
                for j in range(b + 1):
                    ins = nc.tensor.matmul(psum[:, 6 + b % 2, h * (HD + 1):(h + 1) * (HD + 1)],
                                           pbuf[2 + u % 2][:, j * P:(j + 1) * P], s.vB[:, j, h, :],
                                           start=(j == 0), stop=(j == b))
                ins.then_inc(b_pv, 1)

            n_exp = [0]
            for u in range(NU):
                n_exp.append(n_exp[-1] + (2 if units[u][0] == "D" else 1))

            def score(u):
                kind, b, h = units[u]
                k0, nk = keys(kind, b)
                prev = before(u, slots)
                if prev is not None and not units[prev][0] == "D":
                    pe.wait_ge(stats_ready, prev + 1)
                for r, slot in enumerate(slots(u)):
                    if prev is not None and units[prev][0] == "D":
                        pe.wait_ge(exp_done, n_exp[prev] + (r + 1 if kind == "D" else 2))
                    for c0 in range(0, nk * P, 512):
                        c1 = min(nk * P, c0 + 512)
                        if kind == "D":
                            row = DI * (2 * (h % 2) + r)
                            q = s.tT[row:row + DI, T_QD + h // 2, b * P:(b + 1) * P]
                            k = s.tT[row:row + DI, T_KD + h // 2, c0:c1]
                        else:
                            q = head(qk[kind][0], h, b, 1)
                            k = s.tT[HD * (h % 2):HD * (h % 2) + HD, qk[kind][1] + h // 2, k0 * P + c0:k0 * P + c1]
                        ins = nc.tensor.matmul(psum[:, 2 * slot + c0 // 512, 0:c1 - c0], q, k, start=True, stop=True)
                    ins.then_inc(scores_ready, 1)

            values = {"D": s.vD, "C": s.vC, "A": s.vA}

            def weigh(i, m):
                u, g0, ng, last = groups[i]
                kind, b, h = units[u]
                k0, nk = keys(kind, b)
                n = u // NH
                pe.wait_ge(pt_copied, i + 1)
                if h == 0 and g0 == 0 and n >= 2:
                    pe.wait_ge(out_normed, n - 1)
                for j in range(ng):
                    ins = nc.tensor.matmul(psum[:, 6 + n % 2, h * HD:(h + 1) * HD], pt[m % 4][:, j * P:(j + 1) * P],
                                           values[kind][:, k0 + g0 + j, h * HD:(h + 1) * HD],
                                           start=(g0 + j == 0), stop=(g0 + j == nk - 1))
                ins.then_inc(pv_done, 1)

            pe.wait_ge(b_weights, NB)
            pe.wait_ge(b_exp, NB)
            pe.wait_ge(b_normed, NT)
            score(0)
            scored = 0
            m = 0
            for i, (what, g0, ng, last) in enumerate(groups):
                if isinstance(what, str) and not isinstance(groups[i - 1][0], str):
                    weigh(i - 1, m)
                    m += 1
                if i >= 2:
                    pe.wait_ge(pt_copied, i - 1)
                if isinstance(what, str):
                    if g0 == 0:
                        if what in "BD":
                            pe.wait_ge(y_ready, "BD".index(what) + 1)
                        else:
                            pe.wait_ge(out_normed, {"C": 2 * NT, "A": 3 * NT}[what])
                    c, t0 = g0 % 2, g0 // 2 * 4
                    for t in range(4):
                        ins = nc.tensor.transpose(psum[:, 4 + i % 2, t * P:(t + 1) * P],
                                                  y[what][:, t0 + t, c * P:(c + 1) * P], s.ident[:, :])
                    ins.then_inc(pt_ready, 1)
                else:
                    kind, b, h = units[what]
                    if g0 == 0:
                        ahead = min(what + (1 if kind == "D" else 2), NU - 1)
                        for u in range(scored + 1, ahead + 1):
                            score(u)
                        scored = max(scored, ahead)
                    if g0 == 0:
                        if kind == "D":
                            pe.wait_ge(diff_ready, what + 1)
                        else:
                            pe.wait_ge(exp_done, n_exp[what + 1])
                    for j in range(ng):
                        ins = nc.tensor.transpose(psum[:, 4 + i % 2, j * P:(j + 1) * P],
                                                  pbuf[bufs(what)[0]][:, (g0 + j) * P:(g0 + j + 1) * P], s.ident[:, :])
                    ins.then_inc(pt_ready, 1)
                if i and not isinstance(what, str) and not isinstance(groups[i - 1][0], str):
                    weigh(i - 1, m)
                    m += 1
            pe.wait_ge(pt_copied, len(groups))


def mix(nc, a, s):
    sb, sem, psum = s.sb, s.sem, s.psum
    h_hi = sb("h_hi", [P, KC, SEQ], 128, F32R)
    h_lo = sb("h_lo", [P, KC, SEQ], 0, F32R)
    wg = [sb(f"wg{n}", [P, KC, P], 160 + 4 * n) for n in range(4)]
    wg_lo = [sb(f"wg_lo{n}", [P, KC, P], 160 + 4 * n, F32R) for n in range(4)]
    wg_hi = [sb(f"wg_hi{i}", [P, KC, P], 176 + 4 * i, F32R) for i in range(2)]
    wb = [sb(f"wb{n}", [P, 2, P], 184 + n) for n in range(4)]
    sig = [sb(f"sig{i}", [P, SEQ], 188 + 4 * i) for i in range(2)]
    prod = [sb(f"prod{i}", [P, SEQ], 196 + 4 * i) for i in range(2)]
    s.mixT = mixT = sb("mixT", [P, KC, SEQ], 96)
    w_in = [sem(f"wgb_in{n}") for n in range(4)]
    h_high, h_low, w_high, w_low = sem("h_high"), sem("h_low"), sem("w_high"), sem("w_low")
    gate_ready, sig_ready, up_used, summed = sem("gate_ready"), sem("sig_ready3"), sem("up_used"), sem("summed3")
    yT_of = (T_QA, T_QB, T_QC, T_QD)

    def steps(eng, body, last=None):
        for n in range(4):
            body(n, 0, n, n)
        with eng.Fori(1, KC) as d:
            for n in range(4):
                body(d * 4 + n, d, n, None)

    with nc.Block() as block:
        @block.sync
        def _(sp):
            def load(d, n):
                sp.dma_start(wg[n][:, :, :], a["w_gate"][n, bass.ds(d, 1)].rearrange("o p c m -> (o p) c m")
                             ).then_inc(w_in[n], 16)
                sp.dma_start(wb[n][:, :, :], a["w_branch"][n, bass.ds(d, 1)].rearrange("o p c m -> (o p) c m")
                             ).then_inc(w_in[n], 16)

            for n in range(4):
                load(0, n)
            for t in range(NT):
                sp.dma_start(s.x2[t][:, :], a["x"][t * P:(t + 1) * P, :]).then_inc(s.x_in[t], 16)
            with sp.Fori(1, KC) as d:
                for n in range(4):
                    sp.wait_ge(gate_ready, d * 4 + (n - 3))
                    load(d, n)

        @block.tensor
        def _(pe):
            def body(c, d, n, first):
                bank = 4 * (n % 2)
                pe.wait_ge(w_low, c + 1)
                pe.wait_ge(w_in[n], d * 32 + 32)
                if first is None or first >= 2:
                    pe.wait_ge(up_used, c - 1)
                for h in range(2):
                    cols = slice(h * 512, (h + 1) * 512)
                    for k in range(KC):
                        if first == 0 and h == 0:
                            pe.wait_ge(h_low, k + 1)
                        for w, x in ((wg_hi[n % 2], h_hi), (wg_hi[n % 2], h_lo), (wg_lo[n], h_hi)):
                            nc.tensor.matmul(psum[:, bank + h, :], w[:, k, :], x[:, k, cols],
                                             start=(k == 0 and w is wg_hi[n % 2] and x is h_hi),
                                             stop=(k == KC - 1 and w is wg_lo[n]))
                for h in range(2):
                    for k in range(2):
                        ins = nc.tensor.matmul(psum[:, bank + 2 + h, :], wb[n][:, k, :],
                                               s.tT[:, yT_of[n] + k, h * 512:(h + 1) * 512],
                                               start=(k == 0), stop=(k == 1))
                ins.then_inc(gate_ready, 1)
            steps(pe, body)

        @block.scalar
        def _(act):
            def gate(c, n, first):
                act.wait_ge(gate_ready, c + 1)
                if first is None or first >= 2:
                    act.wait_ge(up_used, c - 1)
                nc.scalar.activation(sig[n % 2][:, :], psum[:, 4 * (n % 2):4 * (n % 2) + 2, :]
                                     .rearrange("p a b -> p (a b)"), ACT.Sigmoid).then_inc(sig_ready, 1)

            def body(c, d, n, first):
                act.wait_ge(w_in[n], d * 32 + 32)
                if first is None or first >= 2:
                    act.wait_ge(gate_ready, c - 1)
                nc.scalar.activation(wg_hi[n % 2][:, :, :], wg[n][:, :, :], ACT.Copy).then_inc(w_high, 1)
                if first == 0:
                    for k in range(KC):
                        nc.scalar.activation(h_hi[:, k, :], s.hT[:, k, :], ACT.Copy).then_inc(h_high, 1)
                else:
                    gate(c - 1, (n - 1) % 4, None if first is None else first - 1)
            steps(act, body)
            gate(4 * KC - 1, 3, None)

        @block.vector
        def _(dve):
            def use(c, d, n, first):
                dve.wait_ge(sig_ready, c + 1)
                up = psum[:, 4 * (n % 2) + 2:4 * (n % 2) + 4, :].rearrange("p a b -> p (a b)")
                if first is None or first >= 2:
                    dve.wait_ge(summed, d * 3 + max(n - 1, 0))
                nc.vector.tensor_tensor(prod[min(n, 1)][:, :], up, sig[n % 2][:, :], ALU.mult).then_inc(up_used, 1)
                if n:
                    dve.wait_ge(up_used, c + 1)
                    dst = prod[0][:, :] if n < 3 else mixT[:, bass.ds(d, 1), :].rearrange("p o n -> p (o n)")
                    nc.vector.tensor_tensor(dst, prod[0][:, :], prod[1][:, :], ALU.add).then_inc(summed, 1)

            def body(c, d, n, first):
                dve.wait_ge(w_high, c + 1)
                nc.vector.tensor_tensor(wg_lo[n][:, :, :], wg[n][:, :, :], wg_hi[n % 2][:, :, :].bitcast(F32),
                                        ALU.subtract).then_inc(w_low, 1)
                if first == 0:
                    for k in range(KC):
                        dve.wait_ge(h_high, k + 1)
                        nc.vector.tensor_tensor(h_lo[:, k, :], s.hT[:, k, :], h_hi[:, k, :].bitcast(F32),
                                                ALU.subtract).then_inc(h_low, 1)
                elif n:
                    use(c - 1, d, n - 1, None if first is None else first - 1)
                else:
                    use(c - 1, d - 1, 3, 3)
            steps(dve, body)
            use(4 * KC - 1, KC - 1, 3, 3)


def route(nc, a, s):
    sb, sem, psum = s.sb, s.sem, s.psum
    NBLK = NE + N_OV
    w_out = sb("w_out", [P, KC, DM], 128)
    gain = sb("gain2", [P, DM], 160)
    h2 = [sb(f"h2_{i}", [P, DM], 164 + 4 * i) for i in range(2)]
    h2T = [sb(f"h2T{i}", [P, KC, P], 192 + 4 * i) for i in range(2)]
    rw = sb("rw", [P, KC, NG + NE], 200)
    rb = sb("rb", [P, NG + NE], 201.25)
    ssq, rms = sb("ssq2", [P, NT], 201.5), sb("rms2", [P, NT], 201.5625)
    eps = sb("eps4", [P, 1], 201.625)
    lg = sb("lg", [P, NT, NG + NE], 160)
    triu, ones = sb("triu", [P, P], 172), sb("ones", [P, P], 172.5)
    iota_e = sb("iota_e", [P, NE], 173)
    iota_r = sb("iota_r", [P, NE], 173.125)
    iota_c = sb("iota_c", [P, CAP], 173.25)
    iota_b = sb("iota_b", [P, NBLK], 173.75)
    iota_j = sb("iota_j", [1, N_OV, NE], 40)
    tok_id = sb("tok_id", [P, NT], 174)
    e1, e2, t1, t2 = (sb(f"r_{n}", [P, NT, NE], 162 + k) for k, n in enumerate(["e1", "e2", "t1", "t2"]))
    o1, o2, cum, tot = (sb(f"r_{n}", [P, NT, NE], 166 + k) for k, n in enumerate(["o1", "o2", "cum", "tot"]))
    g_d, g_e = sb("g_d", [P, NT, NG], 170), sb("g_e", [P, NT, NG], 170.125)
    v = sb("r_v", [P, 24, NT], 170.25)
    asg = sb("asg", [P, 8, 2 * NT], 171)
    cnt = sb("cnt", [P, 4, NE], 171.5)
    hot_c = [sb(f"hot_c{i}", [P, CAP], 176 + i) for i in range(2)]
    hot_b = [sb(f"hot_b{i}", [P, NBLK], 176.5 + i) for i in range(2)]
    cmpj = sb("cmpj", [1, N_OV, NE], 43)

    rw_in, gain_in = sem("rw_in"), sem("gain_in")
    out_ready, x2_ready, summed, rooted = sem("out_ready"), sem("x2_ready"), sem("summed4"), sem("rooted")
    h2_ready, h2_stored, h2T_ready, h2T_taken = sem("h2_ready"), [sem(f"h2_stored{i}") for i in range(2)], \
        sem("h2T_ready"), sem("h2T_taken")
    logits_ready, logits_taken = sem("logits_ready"), sem("logits_taken")
    const_ready = sem("const_ready4")
    soft_in, soft_out, assigned, counted = sem("soft_in"), sem("soft_out"), sem("assigned"), sem("counted")
    hot_ready, hot_used = sem("hot_ready"), sem("hot_used")
    w_out_in = [sem(f"w_out_in{i}") for i in range(2)]

    with nc.Block() as block:
        @block.sync
        def _(sp):
            for h in range(2):
                sp.dma_start(w_out[:, :, h * 512:(h + 1) * 512],
                             a["w_out"].rearrange("(c p) n -> p c n", p=P)[:, :, h * 512:(h + 1) * 512]
                             ).then_inc(w_out_in[h], 16)
            sp.dma_start(gain[:, :], a["g_ffn"].partition_broadcast(P)).then_inc(gain_in, 16)
            sp.dma_start(rw[:, :, :], a["w_router"]).then_inc(rw_in, 16)
            sp.dma_start(rb[:, :], a["b_router"].partition_broadcast(P)).then_inc(rw_in, 16)
            s.load_expert(sp, 0, 0, "w1"), s.load_expert(sp, 0, 0, "w3")
            for t in range(NT):
                sp.wait_ge(h2_ready, t + 1)
                sp.dma_start(s.h2_rows[t * P:(t + 1) * P, :], h2[t % 2][:, :]).then_inc(h2_stored[t % 2], 16)
            sp.wait_ge(out_ready, NT)
            s.load_expert(sp, 0, 0, "w2")
            s.load_expert(sp, 1, 1, "w1"), s.load_expert(sp, 1, 1, "w3")
            for k in range(2):
                sp.wait_ge(h2_stored[k], 16 * NT // 2)

        @block.gpsimd
        def _(pool):
            link = chained(pool, s.pool_chain)
            pool.memset(eps[:, :], EPS).then_inc(const_ready, 1)
            link(pool.memset(triu[:, :], 1.0))
            pool.affine_select(out=triu[:, :], in_=triu[:, :], compare_op=ALU.is_gt, fill=0.0, base=0,
                               pattern=[[1, P]], channel_multiplier=-1).then_inc(const_ready, 1)
            pool.memset(ones[:, :], 1.0).then_inc(const_ready, 1)
            exact = dict(allow_small_or_imprecise_dtypes=True)
            pool.iota(iota_e[:, :], pattern=[[1, NE]], base=0, channel_multiplier=0, **exact)
            pool.iota(iota_r[:, :], pattern=[[-1, NE]], base=NE, channel_multiplier=0, **exact)
            pool.iota(iota_c[:, :], pattern=[[1, CAP]], base=0, channel_multiplier=0, **exact)
            pool.iota(iota_b[:, :], pattern=[[1, NBLK]], base=0, channel_multiplier=0, **exact)
            pool.iota(iota_j[:, :, :], pattern=[[1, N_OV], [0, NE]], base=0, channel_multiplier=0, **exact)
            pool.iota(tok_id[:, :], pattern=[[P, NT]], base=0, channel_multiplier=1, **exact).then_inc(const_ready, 1)

        @block.scalar
        def _(act):
            for t in range(NT):
                act.wait_ge(const_ready, 4)
                act.wait_ge(summed, t + 1)
                nc.scalar.activation(rms[:, t:t + 1], ssq[:, t:t + 1], ACT.Sqrt, bias=eps[:, 0:1],
                                     scale=1.0 / DM).then_inc(rooted, 1)
                for h in range(2):
                    act.wait_ge(h2T_ready, 2 * t + h + 1)
                    if t >= 2 and h == 0:
                        act.wait_ge(logits_ready, t - 1)
                    nc.scalar.activation(h2T[t % 2][:, 4 * h:4 * h + 4, :].rearrange("p c n -> p (c n)"),
                                         psum[:, 4 + h, :], ACT.Copy).then_inc(h2T_taken, 1)
            act.wait_ge(soft_in, 1)
            nc.scalar.activation(g_e[:, :, :], g_d[:, :, :], ACT.Exp).then_inc(soft_out, 1)
            act.wait_ge(soft_in, 2)
            nc.scalar.activation(v[:, 6, :], v[:, 5, :], ACT.Exp).then_inc(soft_out, 1)

        @block.vector
        def _(dve):
            link = chained(dve, s.dve_chain)
            dve.wait_ge(gain_in, 16)
            for t in range(NT):
                dve.wait_ge(out_ready, t + 1)
                dve.wait_ge(s.x_in[t], 32)
                x2 = s.x2[t][:, :]
                link(nc.vector.tensor_tensor(x2, psum[:, 2 * (t % 2):2 * (t % 2) + 2, :]
                                             .rearrange("p a b -> p (a b)"), x2, ALU.add))
                nc.vector.engine_nop().then_inc(x2_ready, 1)
                if t >= 2:
                    dve.wait_ge(h2_stored[t % 2], 16 * (t // 2))
                    dve.wait_ge(h2T_ready, 2 * (t - 1))
                nc.vector.tensor_tensor_reduce(out=h2[t % 2][:, :], in0=x2, in1=x2, scale=1.0, scalar=0.0,
                                               op0=ALU.mult, op1=ALU.add, accum_out=ssq[:, t:t + 1]
                                               ).then_inc(summed, 1)
                dve.wait_ge(rooted, t + 1)
                link(nc.vector.reciprocal(rms[:, t:t + 1], rms[:, t:t + 1]))
                nc.vector.scalar_tensor_tensor(out=h2[t % 2][:, :], in0=x2, scalar=rms[:, t:t + 1], in1=gain[:, :],
                                               op0=ALU.mult, op1=ALU.mult).then_inc(h2_ready, 1)
            dve.wait_ge(rw_in, 32)
            dve.wait_ge(logits_ready, NT)
            dve.wait_ge(h2_ready, NT)
            for k in range(2):
                dve.wait_ge(h2_stored[k], 16 * NT // 2)
            L = psum[:, 6, 0:NT * (NG + NE)].rearrange("p (t n) -> p t n", n=NG + NE)
            link(nc.vector.tensor_tensor(lg[:, :, :], L, rb[:, :].unsqueeze(1).to_broadcast([P, NT, NG + NE]), ALU.add))
            lgg, lge = lg[:, :, 0:NG], lg[:, :, NG:NG + NE]

            def spread(x, n):
                return x.unsqueeze(2).to_broadcast([P, NT, n])

            def first_max(hot, x, top, tmp, n, m):
                rank = iota_r[:, 0:n].unsqueeze(1).to_broadcast([P, NT, n])
                link(nc.vector.tensor_reduce(out=top, in_=x, axis=AX.X, op=ALU.max))
                link(nc.vector.tensor_tensor(tmp, x, spread(top, n), ALU.is_equal))
                link(nc.vector.tensor_tensor(tmp, tmp, rank, ALU.mult))
                link(nc.vector.tensor_reduce(out=m, in_=tmp, axis=AX.X, op=ALU.max))
                link(nc.vector.tensor_tensor(hot, tmp, spread(m, n), ALU.is_equal))

            og = t1[:, :, 0:NG]
            first_max(og, lgg, v[:, 0, :], t2[:, :, 0:NG], NG, v[:, 1, :])
            nc.vector.tensor_tensor(g_d[:, :, :], lgg, spread(v[:, 0, :], NG), ALU.subtract).then_inc(soft_in, 1)
            dve.wait_ge(soft_out, 1)
            link(nc.vector.tensor_reduce(out=v[:, 2, :], in_=g_e[:, :, :], axis=AX.X, op=ALU.add))
            link(nc.vector.reciprocal(v[:, 2, :], v[:, 2, :]))
            link(nc.vector.tensor_scalar(og, og, -1.0, 1e30, ALU.add, ALU.mult))
            for g in range(NG):
                ins = nc.vector.tensor_tensor(e1[:, :, g * EG:(g + 1) * EG], lge[:, :, g * EG:(g + 1) * EG],
                                              og[:, :, g:g + 1].to_broadcast([P, NT, EG]), ALU.add)
            link(ins)
            first_max(o1[:, :, :], e1[:, :, :], v[:, 3, :], t2[:, :, :], NE, v[:, 1, :])
            link(nc.vector.tensor_scalar(t1[:, :, :], o1[:, :, :], -2e30, None, ALU.mult))
            link(nc.vector.tensor_tensor(e1[:, :, :], e1[:, :, :], t1[:, :, :], ALU.add))
            first_max(o2[:, :, :], e1[:, :, :], v[:, 4, :], t2[:, :, :], NE, v[:, 1, :])
            nc.vector.tensor_tensor(v[:, 5, :], v[:, 4, :], v[:, 3, :], ALU.subtract).then_inc(soft_in, 1)
            link(nc.vector.tensor_tensor(e2[:, :, :], o1[:, :, :], o2[:, :, :], ALU.add))
            link(nc.vector.memset(cum[:, 0, :], 0.0))
            for t in range(1, NT):
                link(nc.vector.tensor_tensor(cum[:, t, :], cum[:, t - 1, :], e2[:, t - 1, :], ALU.add))
            link(nc.vector.tensor_tensor(tot[:, 0, :], cum[:, NT - 1, :], e2[:, NT - 1, :], ALU.add))
            nc.vector.engine_nop().then_inc(assigned, 1)
            dve.wait_ge(soft_out, 2)
            link(nc.vector.tensor_scalar(v[:, 7, :], v[:, 6, :], 1.0, None, ALU.add))
            link(nc.vector.reciprocal(v[:, 7, :], v[:, 7, :]))
            link(nc.vector.tensor_tensor(s.gates[:, 0, :], v[:, 7, :], v[:, 2, :], ALU.mult))
            link(nc.vector.tensor_tensor(s.gates[:, 1, :], s.gates[:, 0, :], v[:, 6, :], ALU.mult))
            dve.wait_ge(counted, 1)
            pos = psum[:, 7, 0:NT * NE].rearrange("p (t e) -> p t e", e=NE)
            link(nc.vector.tensor_copy(e1[:, :, :], pos))
            link(nc.vector.tensor_copy(cnt[:, 0, :], psum[:, 7, NT * NE:NT * NE + NE]))
            link(nc.vector.tensor_scalar(cnt[:, 1, :], cnt[:, 0, :], float(CAP), None, ALU.is_gt))
            MORE = (SEQ - 1) // CAP
            for k in range(2, MORE + 1):
                link(nc.vector.scalar_tensor_tensor(out=cnt[:, 1, :], in0=cnt[:, 0, :], scalar=float(CAP * k),
                                                    in1=cnt[:, 1, :], op0=ALU.is_gt, op1=ALU.add))
            link(nc.vector.memset(cnt[:, 2, :], 1.0))
            link(nc.vector.tensor_tensor_scan(cnt[:, 3, :], cnt[:, 2, :], cnt[:, 1, :], 0.0, ALU.mult, ALU.add))
            link(nc.vector.tensor_tensor(cnt[:, 1, :], cnt[:, 3, :], cnt[:, 1, :], ALU.subtract))
            ends = cnt[0:1, 3, :].unsqueeze(1).to_broadcast([1, N_OV, NE])
            link(nc.vector.tensor_tensor(cmpj[:, :, :], iota_j[:, :, :], ends, ALU.is_ge))
            link(nc.vector.tensor_reduce(out=s.ov_f[:, 0, :], in_=cmpj[:, :, :], axis=AX.X, op=ALU.add))
            link(nc.vector.tensor_scalar(s.ov_f[:, 1, :], s.ov_f[:, 0, :], NE - 0.5, None, ALU.is_lt))
            link(nc.vector.tensor_scalar(s.ov_f[:, 0, :], s.ov_f[:, 0, :], float(NE - 1), None, ALU.min))
            link(nc.vector.tensor_copy(s.ov_i[:, :, :], s.ov_f[:, :, :]))
            for k, hot in enumerate((o1, o2)):
                for r, table in enumerate((e1[:, :, :],
                                           iota_e[:, :].unsqueeze(1).to_broadcast([P, NT, NE]),
                                           cnt[:, 1, :].unsqueeze(1).to_broadcast([P, NT, NE]))):
                    link(nc.vector.tensor_tensor(t1[:, :, :], hot[:, :, :], table, ALU.mult))
                    link(nc.vector.tensor_reduce(out=asg[:, r, k * NT:(k + 1) * NT], in_=t1[:, :, :], axis=AX.X,
                                                 op=ALU.add))
            link(nc.vector.tensor_scalar(asg[:, 3, :], asg[:, 0, :], float(CAP), None, ALU.is_ge))
            link(nc.vector.tensor_copy(asg[:, 6, :], asg[:, 3, :]))
            for k in range(2, MORE + 1):
                link(nc.vector.scalar_tensor_tensor(out=asg[:, 3, :], in0=asg[:, 0, :], scalar=float(CAP * k),
                                                    in1=asg[:, 3, :], op0=ALU.is_ge, op1=ALU.add))
            link(nc.vector.scalar_tensor_tensor(out=asg[:, 4, :], in0=asg[:, 3, :], scalar=-float(CAP),
                                                in1=asg[:, 0, :], op0=ALU.mult, op1=ALU.add))
            link(nc.vector.scalar_tensor_tensor(out=asg[:, 5, :], in0=asg[:, 3, :], scalar=float(NE - 1),
                                                in1=asg[:, 2, :], op0=ALU.add, op1=ALU.add))
            link(nc.vector.tensor_tensor(asg[:, 5, :], asg[:, 5, :], asg[:, 1, :], ALU.subtract))
            link(nc.vector.tensor_tensor(asg[:, 5, :], asg[:, 5, :], asg[:, 6, :], ALU.mult))
            link(nc.vector.tensor_tensor(asg[:, 5, :], asg[:, 5, :], asg[:, 1, :], ALU.add))
            link(nc.vector.scalar_tensor_tensor(out=asg[:, 7, :], in0=asg[:, 5, :], scalar=float(CAP),
                                                in1=asg[:, 4, :], op0=ALU.mult, op1=ALU.add))
            link(nc.vector.tensor_copy(s.row_of[:, :], asg[:, 7, :]))
            for q in range(2 * NT):
                if q >= 2:
                    dve.wait_ge(hot_used, q - 1)
                nc.vector.tensor_scalar(hot_c[q % 2][:, :], iota_c[:, :], asg[:, 4, q:q + 1], None, ALU.is_equal)
                nc.vector.tensor_scalar(hot_b[q % 2][:, :], iota_b[:, :], asg[:, 5, q:q + 1],
                                        tok_id[:, q % NT:q % NT + 1], ALU.is_equal, ALU.mult).then_inc(hot_ready, 1)
            dve.wait_ge(hot_used, 2 * NT)
            link(nc.vector.tensor_copy(s.tok_of[:, :], psum[0:CAP, 5, 0:NBLK]))

        @block.tensor
        def _(pe):
            pe.wait_ge(rw_in, 32)

            def project_out(t):
                if t >= 2:
                    pe.wait_ge(x2_ready, t - 1)
                for h in range(2):
                    if t == 0:
                        pe.wait_ge(w_out_in[h], 16)
                    for k in range(KC):
                        ins = nc.tensor.matmul(psum[:, 2 * (t % 2) + h, :], s.mixT[:, k, t * P:(t + 1) * P],
                                               w_out[:, k, h * 512:(h + 1) * 512],
                                               start=(k == 0), stop=(k == KC - 1))
                ins.then_inc(out_ready, 1)

            project_out(0)
            for t in range(NT):
                if t + 1 < NT:
                    project_out(t + 1)
                pe.wait_ge(h2_ready, t + 1)
                if t:
                    pe.wait_ge(h2T_taken, 2 * t)
                for h in range(2):
                    for c in range(4):
                        k = 4 * h + c
                        ins = nc.tensor.transpose(psum[:, 4 + h, c * P:(c + 1) * P],
                                                  h2[t % 2][:, k * P:(k + 1) * P], s.ident[:, :])
                    ins.then_inc(h2T_ready, 1)
                pe.wait_ge(h2T_taken, 2 * t + 2)
                for k in range(KC):
                    ins = nc.tensor.matmul(psum[:, 6, t * (NG + NE):(t + 1) * (NG + NE)], h2T[t % 2][:, k, :],
                                           rw[:, k, :], start=(k == 0), stop=(k == KC - 1))
                ins.then_inc(logits_ready, 1)
            pe.wait_ge(assigned, 1)
            pe.wait_ge(const_ready, 4)
            pe_pos = psum[:, 7, 0:NT * NE]
            nc.tensor.matmul(pe_pos, triu[:, :], e2[:, :, :].rearrange("p t e -> p (t e)"), start=True, stop=False)
            nc.tensor.matmul(pe_pos, ones[:, :], cum[:, :, :].rearrange("p t e -> p (t e)"), start=False, stop=True)
            nc.tensor.matmul(psum[:, 7, NT * NE:NT * NE + NE], ones[:, :], tot[:, 0, :], start=True,
                             stop=True).then_inc(counted, 1)
            for q in range(2 * NT):
                pe.wait_ge(hot_ready, q + 1)
                nc.tensor.matmul(psum[0:CAP, 5, 0:NBLK], hot_c[q % 2][:, :], hot_b[q % 2][:, :], start=(q == 0),
                                 stop=(q == 2 * NT - 1)).then_inc(hot_used, 1)


def experts(nc, a, s):
    sb, sem, psum = s.sb, s.sem, s.psum
    w1, w3, w2 = s.w1, s.w3, s.w2
    xg = [sb(f"xg{i}", [CAP, DM], 40 + 4 * i) for i in range(2)]
    xT = [sb(f"xT{i}", [P, KC, CAP], 56 + 4 * i) for i in range(2)]
    act_ = [sb(f"gl{i}", [P, FT, CAP], 72 + 2 * i) for i in range(2)]
    hid = [sb(f"hid{i}", [P, FT, CAP], 76 + 2 * i) for i in range(2)]
    yo = [sb(f"yo{i}", [CAP, DM], 88 + 4 * i) for i in range(2)]
    idx = [sb(f"idx{i}", [CAP, 1], 200 + 0.0625 * i, I32) for i in range(2)]

    idx_set, idx_seen = sem("idx_set"), sem("idx_seen")
    xg_in = [sem(f"xg_in{i}") for i in range(2)]
    xT_ready, xT_taken = sem("xT_ready5"), sem("xT_taken5")
    up_done, gate_done, hid_ready, y_done = sem("up_done"), sem("gate_done"), sem("hid_ready"), sem("y_done")
    glu_ready, glu_half, y_taken = sem("glu_ready"), sem("glu_half"), sem("y_taken")
    y_stored = s.y_stored
    ov = {n: sem("ov_" + n) for n in ("go", "idx", "rows", "w1", "w3", "w2", "xT", "xT_taken", "up", "glu", "half",
                                      "hid", "y", "y_taken", "stored")}

    def transposes(j):
        for c in range(KC):
            ins = nc.tensor.transpose(psum[:, c // 4, (c % 4) * CAP:(c % 4 + 1) * CAP],
                                      xg[j][:, c * P:(c + 1) * P], s.ident[0:CAP, 0:CAP])
        return ins

    def up(bank, w, j):
        for f in range(FT):
            for k in range(KC):
                ins = nc.tensor.matmul(psum[:, bank, f * CAP:(f + 1) * CAP], w[j][:, k, f * P:(f + 1) * P],
                                       xT[j][:, k, :], start=(k == 0), stop=(k == KC - 1))
        return ins

    def down(j):
        for h in range(2):
            for f in range(FT):
                ins = nc.tensor.matmul(psum[0:CAP, 4 + h, :], hid[j][:, f, :], w2[j][:, f, h * 512:(h + 1) * 512],
                                       start=(f == 0), stop=(f == FT - 1))
        return ins

    def banks(k, rows=P):
        return psum[0:rows, k:k + 2, :]

    def xT_out(j):
        return nc.scalar.activation(xT[j][:, :, :].rearrange("p (b c) n -> p b (c n)", b=2),
                                    psum[:, 0:2, 0:4 * CAP], ACT.Copy)

    def hidden(bank):
        return psum[:, bank, 0:FT * CAP]

    def flat(x):
        return x[:, :, :].rearrange("p f n -> p (f n)")

    def loop(eng, body):
        for j in range(2):
            body(0, j, True)
        with eng.Fori(1, NE // 2) as i:
            for j in range(2):
                body(i, j, False)

    def overflow(eng, body):
        with eng.Fori(0, N_OV) as b:
            used = eng.value_load(s.ov_i[0:1, 1, bass.ds(b, 1)], min_val=0, max_val=1)
            with eng.If(used):
                body(b)

    def expert_of(eng, b):
        return eng.value_load(s.ov_i[0:1, 0, bass.ds(b, 1)], min_val=0, max_val=NE - 1)

    with nc.Block() as block:
        @block.sync
        def _(sp):
            s.load_expert(sp, 1, 1, "w2")

            with sp.Fori(1, NE // 2) as i:
                for j in range(2):
                    sp.wait_ge(up_done, i * 2 + (j - 1))
                    s.load_expert(sp, i * 2 + j, j, "w1")
                    sp.wait_ge(gate_done, i * 2 + (j - 1))
                    s.load_expert(sp, i * 2 + j, j, "w3")
                    sp.wait_ge(y_done, i * 2 + (j - 1))
                    s.load_expert(sp, i * 2 + j, j, "w2")
            sp.wait_ge(y_done, NE)

            def body(b):
                sp.wait_ge(ov["go"], b + 1)
                e = expert_of(sp, b)
                s.load_expert(sp, e, 0, "w1", ov["w1"]), s.load_expert(sp, e, 0, "w3", ov["w3"])
                s.load_expert(sp, e, 0, "w2", ov["w2"])
            overflow(sp, body)

        @block.gpsimd
        def _(pool):
            def rows(j, done):
                pool.indirect_dma_start(xg[j][:, :], None, s.h2_rows,
                                        bass.IndirectOffsetOnAxis(ap=idx[j][:, 0:1].bitcast(U32), axis=0)
                                        ).then_inc(done, 16)

            def body(i, j, first):
                if not first:
                    pool.wait_ge(xT_ready, i * 2 + (j - 1))
                    pool.wait_ge(xg_in[j], i * 16)
                pool.tensor_copy(idx[j][:, :], s.tok_of[:, bass.ds(i * 2 + j, 1)]).then_inc(idx_set, 1)
                pool.wait_ge(idx_set, i * 2 + (j + 1))
                pool.sem_inc(idx_seen, 1)
                rows(j, xg_in[j])
            loop(pool, body)
            pool.wait_ge(y_done, NE)
            pool.sem_inc(ov["go"], 1)

            def body(b):
                pool.tensor_copy(idx[0][:, :], s.tok_of[:, bass.ds(b + NE, 1)]).then_inc(ov["idx"], 1)
                pool.wait_ge(ov["idx"], b + 1)
                pool.sem_inc(idx_seen, 1)
                rows(0, ov["rows"])
                pool.wait_ge(ov["stored"], b * 16 + 16)
                pool.sem_inc(ov["go"], 1)
            overflow(pool, body)

        @block.tensor
        def _(pe):
            def body(i, j, first):
                pe.wait_ge(xg_in[j], i * 16 + 16)
                if not (first and j == 0):
                    pe.wait_ge(xT_taken, i * 2 + j)
                transposes(j).then_inc(xT_ready, 1)
                if not (first and j == 0):
                    second(i * 2 + j - 1, 1 - j, first)
                pe.wait_ge(xT_taken, i * 2 + (j + 1))
                pe.wait_ge(s.w1_in[j], i * 16 + 16)
                if not (first and j == 0):
                    pe.wait_ge(hid_ready, i * 2 + j)
                up(2, w1, j).then_inc(up_done, 1)
                pe.wait_ge(s.w3_in[j], i * 16 + 16)
                up(3, w3, j).then_inc(gate_done, 1)

            def second(e, j, first):
                pe.wait_ge(hid_ready, e + 1)
                pe.wait_ge(s.w2_in[j], (e - j) * 8 + 16)
                if not first:
                    pe.wait_ge(y_taken, e)
                down(j).then_inc(y_done, 1)
            loop(pe, body)
            second(NE - 1, 1, False)
            pe.wait_ge(y_taken, NE)

            def body(b):
                pe.wait_ge(ov["rows"], b * 16 + 16)
                transposes(0).then_inc(ov["xT"], 1)
                pe.wait_ge(ov["xT_taken"], b + 1)
                pe.wait_ge(ov["w1"], b * 16 + 16)
                pe.wait_ge(ov["w3"], b * 16 + 16)
                up(2, w1, 0)
                up(3, w3, 0).then_inc(ov["up"], 1)
                pe.wait_ge(ov["hid"], b + 1)
                pe.wait_ge(ov["w2"], b * 16 + 16)
                down(0).then_inc(ov["y"], 1)
            overflow(pe, body)

        @block.scalar
        def _(act):
            def y_out(e, j, first):
                act.wait_ge(y_done, e + 1)
                if not first:
                    act.wait_ge(y_stored[j], (e + j) * 8)
                nc.scalar.activation(yo[j][:, :], banks(4, CAP).rearrange("p a b -> p (a b)"),
                                     ACT.Copy).then_inc(y_taken, 1)
                act.wait_ge(y_taken, e + 1)
                act.dma_start(s.ys[bass.ds(e * CAP, CAP), :], yo[j][:, :]).then_inc(y_stored[j], 16)

            def body(i, j, first):
                act.wait_ge(xT_ready, i * 2 + (j + 1))
                if not first:
                    act.wait_ge(gate_done, i * 2 + (j - 1))
                xT_out(j).then_inc(xT_taken, 1)
                if not (first and j == 0):
                    y_out(i * 2 + j - 1, 1 - j, first)
                act.wait_ge(up_done, i * 2 + (j + 1))
                if not first:
                    act.wait_ge(glu_half, i * 2 + (j - 1))
                nc.scalar.activation(flat(act_[j]), hidden(2), ACT.Sigmoid).then_inc(glu_ready, 1)
            loop(act, body)
            y_out(NE - 1, 1, False)
            for j in range(2):
                act.wait_ge(y_stored[j], 16 * (NE // 2 + j))

            def body(b):
                act.wait_ge(ov["xT"], b + 1)
                xT_out(0).then_inc(ov["xT_taken"], 1)
                act.wait_ge(ov["up"], b + 1)
                nc.scalar.activation(flat(act_[0]), hidden(2), ACT.Sigmoid).then_inc(ov["glu"], 1)
                act.wait_ge(ov["y"], b + 1)
                nc.scalar.activation(yo[0][:, :], banks(4, CAP).rearrange("p a b -> p (a b)"),
                                     ACT.Copy).then_inc(ov["y_taken"], 1)
                act.wait_ge(ov["y_taken"], b + 1)
                act.dma_start(s.ys[bass.ds((b + NE) * CAP, CAP), :], yo[0][:, :]).then_inc(ov["stored"], 16)
            overflow(act, body)

        @block.vector
        def _(dve):
            def glu(j, half, done, value):
                nc.vector.tensor_tensor(flat(act_[j]), hidden(2), flat(act_[j]), ALU.mult).then_inc(half, 1)
                dve.wait_ge(half, value)
                return nc.vector.tensor_tensor(flat(hid[j]), hidden(3), flat(act_[j]), ALU.mult)

            def body(i, j, first):
                dve.wait_ge(glu_ready, i * 2 + (j + 1))
                dve.wait_ge(gate_done, i * 2 + (j + 1))
                if not first:
                    dve.wait_ge(y_done, i * 2 + (j - 1))
                glu(j, glu_half, hid_ready, i * 2 + (j + 1)).then_inc(hid_ready, 1)
            loop(dve, body)

            def body(b):
                dve.wait_ge(ov["glu"], b + 1)
                glu(0, ov["half"], ov["hid"], b + 1).then_inc(ov["hid"], 1)
            overflow(dve, body)


def combine(nc, a, s):
    sb, sem = s.sb, s.sem
    ya = [sb(f"ya{i}", [P, DM], 96 + 4 * i) for i in range(NT)]
    yb = [sb(f"yb{i}", [P, DM], 128 + 4 * i) for i in range(NT)]
    fg = sb("fg", [P, DM], 160)
    junk = sb("junk6", [P, DM], 164)
    ssq, rms, eps = sb("ssq6", [P, NT], 200), sb("rms6", [P, NT], 200.0625), sb("eps6", [P, 1], 200.125)
    fg_in, eps_set = sem("fg_in"), sem("eps_set")
    y_in = [sem(f"y_in{t}") for t in range(NT)]
    stored = s.x_in
    summed, rooted, final = sem("summed6"), sem("rooted6"), sem("final")
    with nc.Block() as block:
        @block.sync
        def _(sp):
            sp.dma_start(fg[:, :], a["g_final"].partition_broadcast(P)).then_inc(fg_in, 16)
            for t in range(NT):
                sp.wait_ge(final, t + 1)
                sp.dma_start(a["out"][t * P:(t + 1) * P, :], ya[t][:, :]).then_inc(stored[t], 16)
            for t in range(NT):
                sp.wait_ge(stored[t], 48)

        @block.gpsimd
        def _(pool):
            pool.memset(eps[:, :], EPS).then_inc(eps_set, 1)
            for t in range(NT):
                for k, dst in enumerate((ya, yb)):
                    col = k * NT + t
                    pool.indirect_dma_start(dst[t][:, :], None, s.ys,
                                            bass.IndirectOffsetOnAxis(ap=s.row_of[:, col:col + 1].bitcast(U32), axis=0)
                                            ).then_inc(y_in[t], 16)

        @block.scalar
        def _(act):
            act.wait_ge(eps_set, 1)
            for t in range(NT):
                act.wait_ge(summed, t + 1)
                nc.scalar.activation(rms[:, t:t + 1], ssq[:, t:t + 1], ACT.Sqrt, bias=eps[:, 0:1],
                                     scale=1.0 / DM).then_inc(rooted, 1)

        @block.vector
        def _(dve):
            link = chained(dve, s.dve_chain)
            dve.wait_ge(fg_in, 16)
            for t in range(NT):
                x2 = s.x2[t][:, :]
                dve.wait_ge(y_in[t], 32)
                link(nc.vector.scalar_tensor_tensor(out=x2, in0=ya[t][:, :], scalar=s.gates[:, 0, t:t + 1], in1=x2,
                                                    op0=ALU.mult, op1=ALU.add))
                link(nc.vector.scalar_tensor_tensor(out=x2, in0=yb[t][:, :], scalar=s.gates[:, 1, t:t + 1], in1=x2,
                                                    op0=ALU.mult, op1=ALU.add))
                nc.vector.tensor_tensor_reduce(out=junk[:, :], in0=x2, in1=x2, scale=1.0, scalar=0.0, op0=ALU.mult,
                                               op1=ALU.add, accum_out=ssq[:, t:t + 1]).then_inc(summed, 1)
                dve.wait_ge(rooted, t + 1)
                link(nc.vector.reciprocal(rms[:, t:t + 1], rms[:, t:t + 1]))
                nc.vector.scalar_tensor_tensor(out=ya[t][:, :], in0=x2, scalar=rms[:, t:t + 1], in1=fg[:, :],
                                               op0=ALU.mult, op1=ALU.mult).then_inc(final, 1)


def laid_out(i):
    import numpy as np
    w = i["w_in"][0].reshape(KC, P, -1)
    sizes = dict(qa=256, ka=256, va=256, qi=128, ki=32, wi=4, qb=256, kb=256, vb=256, ib=4, fb=4, ob=256,
                 qc=256, kc=256, vc=256, qd=256, kd=256, vd=256)
    col, at = {}, 0
    for n, z in sizes.items():
        col[n] = w[:, :, at:at + z]
        at += z

    def cat(*names):
        return np.concatenate([col[n] for n in names], axis=2).transpose(1, 0, 2)

    tiles = cat("qi", "ki", "ki", "ki", "ki", "qb", "kb", "qc", "kc", "qd", "kd", "qa", "ka")
    out = {
        "x": i["x"][0],
        "g_mix": i["norm_mix_g"][0].reshape(KC, P).T,
        "if_bias": np.stack([i["mlstm_i_bias"][0], i["mlstm_f_bias"][0]], axis=1),
        "conv": np.concatenate([i["conv_w"][0], i["conv_b"]], axis=0).reshape(5, 4, P).transpose(2, 1, 0),
        "rel": i["relpos_bias"][0][:, ::-1],
        "g_mlstm": i["mlstm_norm_g"][0],
        "g_diff": i["diff_norm_g"][0],
        "lam": i["diff_lambda"][0],
        "w_gate": i["w_gate"][0].reshape(KC, P, 4, KC, P).transpose(2, 3, 1, 0, 4),
        "w_branch": i["w_branch"][0].reshape(4, 2, P, KC, P).transpose(0, 3, 2, 1, 4),
        "w_out": i["w_out"][0],
        "g_ffn": i["norm_ffn_g"][0],
        "w_router": np.concatenate([i["router_group_w"][0], i["router_expert_w"][0]], axis=1)
        .reshape(KC, P, NG + NE).transpose(1, 0, 2),
        "b_router": np.concatenate([i["router_group_b"][0], i["router_expert_b"][0]]),
        "expert_w1": i["expert_w1"][0],
        "expert_w3": i["expert_w3"][0],
        "expert_w2": i["expert_w2"][0],
        "g_final": i["final_norm_g"],
        "w_gates12": cat("ob", "wi", "ib", "fb"),
        "w_T": tiles.reshape(P, KC, NTT, P).transpose(2, 0, 1, 3),
        "w_V": np.stack([cat("va", "vc"), cat("vb", "vd")]),
    }
    return {n: np.ascontiguousarray(v) for n, v in out.items()}


def kernel(**inputs):
    import numpy as np
    import concourse.bacc as bacc
    from concourse.bass_utils import run_bass_kernel_spmd

    inputs = {n: np.asarray(v) for n, v in inputs.items()}
    arrays = laid_out(inputs)
    nc = bacc.Bacc("TRN2", target_bir_lowering=False, num_devices=1)
    aps = {n: nc.dram_tensor(n, v.shape, mybir.dt.from_np(v.dtype), kind="ExternalInput").ap()
           for n, v in arrays.items()}
    aps["out"] = nc.dram_tensor("out", (SEQ, DM), F32, kind="ExternalOutput").ap()
    build(nc, aps)
    r = run_bass_kernel_spmd(nc, [arrays], core_ids=[0])
    return r.results[0]["out"].reshape(1, SEQ, DM)
```

```python
from contextlib import ExitStack

import concourse.bass as bass
from concourse import mybir

F32 = mybir.dt.float32
F32R = mybir.dt.float32r
I32 = mybir.dt.int32
U32 = mybir.dt.uint32
ALU = mybir.AluOpType
ACT = mybir.ActivationFunctionType
AX = mybir.AxisListType

P = 128
SEQ = 1024
DM = 1024
NT = SEQ // P
KC = DM // P
CH = 64
HD = 64
NH = 4
W = NH * HD
DI = 32
TOPK = 256
EPS = 1e-6
NEG = -1e30
LATE, LATE_B = 20, 8
TAKEN = -3e38
N_REL = 192
BAND = 640
GW = W + 3 * NH
NG, EG, NE = 4, 8, 32
FE = 512
FT = FE // P
CAP = 96
N_OV = (2 * SEQ - NE) // CAP
SLOTS = (NE + N_OV) * CAP
KB = 1024

T_QI, T_KI, T_QB, T_KB, T_QC, T_KC, T_QD, T_KD, T_QA, T_KA = 0, 1, 2, 4, 6, 8, 10, 12, 14, 16
NTT = 18


def width(b):
    return (b + 1) * P


SEL_AT = {}
_at = 0
for _b in range(2, NT):
    SEL_AT[_b] = _at
    _at += width(_b)
SEL_COLS = _at


class Shared:
    pass


def chained(eng, chain):
    sem, count = chain

    def link(ins):
        count[0] += 1
        ins.then_inc(sem, 1)
        eng.wait_ge(sem, count[0])
    return link


def build(nc, a):
    ctx = ExitStack()
    with ctx:
        first = 16512
        ctx.enter_context(nc.sbuf_tensor("sbuf_room", [P, 207 * 256], F32))

        def sb(name, shape, at_kb, dt=F32):
            return nc.alloc_sbuf_tensor_at(name, shape, dt, offset=first + int(at_kb * KB))

        def sem(name):
            return ctx.enter_context(nc.semaphore(name))

        def dram(name, shape, dt=F32):
            return nc.dram_tensor(name, shape, dt, kind="Internal").ap()

        s = Shared()
        s.sb, s.sem, s.dram = sb, sem, dram
        s.dve_chain, s.act_chain, s.pool_chain = ((sem(n), [0]) for n in ("dve_chain", "act_chain", "pool_chain"))
        s.psum = ctx.enter_context(nc.psum_tensor("psum", [P, 8, 512], F32))
        s.ident = sb("ident", [P, P], 204)
        s.hT = sb("hT", [P, KC, SEQ], 0)
        s.tT = sb("tT", [P, NTT, SEQ], 32)
        s.vA = sb("vA", [P, NT, W], 104)
        s.vC = sb("vC", [P, NT, W], 112)
        s.vD = sb("vD", [P, NT, W], 120)
        s.vB = sb("vB", [P, NT, NH, HD + 1], 128)
        s.oB = sb("oB", [P, NT, W], 136.25)
        s.g12 = sb("g12", [P, NT, 3 * NH], 144.25)
        s.sel = sb("sel", [P, SEL_COLS], 144.75)
        s.negm = sb("negm", [NH, SEQ], 194)
        s.a_tok = sb("a_tok", [P, NT, NH], 204.5)
        s.enm = sb("enm", [P, NT, NH], 204.75)
        s.sel4 = sb("sel4", [NH, NH, P], 198)
        s.top8 = top8 = sb("top8", [P, 8], 205.75)

        def block_scores(b):
            return s.sel[:, SEL_AT[b]:SEL_AT[b] + width(b)]

        def half_take8(link, b, second):
            sc = block_scores(b)
            if second:
                link(nc.vector.match_replace(sc, top8[:, :], sc, TAKEN))
            else:
                link(nc.vector.max(top8[:, :], sc))

        def take8(link, b):
            half_take8(link, b, False)
            half_take8(link, b, True)

        def taken_mask(link, b):
            sc = block_scores(b)
            link(nc.vector.tensor_scalar(sc, sc, 0.5 * TAKEN, NEG, ALU.is_gt, ALU.mult))
        s.half_take8, s.take8, s.taken_mask = half_take8, take8, taken_mask
        s.h2_rows = dram("h2_rows", [SEQ, DM])
        s.shifted = dram("shifted", [P, NH, 768])
        s.ys = dram("ys", [SLOTS, DM])
        s.y_stored = [sem(f"y_stored{i}") for i in range(2)]
        s.x_in = [sem(f"x_in{i}") for i in range(NT)]
        project(nc, a, s)
        attend(nc, a, s)

        s.x2 = [sb(f"x2_{t}", [P, DM], 32 + 16 * (t // 2) + 4 * (t % 2)) for t in range(NT)]
        s.gates = sb("gates", [P, 2, NT], 202)
        s.row_of = sb("row_of", [P, 2 * NT], 202.125, I32)
        s.tok_of = sb("tok_of", [CAP, NE + N_OV], 202.25, I32)
        s.ov_f = sb("ov_f", [1, 2, N_OV], 202.5)
        s.ov_i = sb("ov_i", [1, 2, N_OV], 202.75, I32)
        s.w1 = [sb(f"w1_{i}", [P, KC, FE], at) for i, at in enumerate((0, 96))]
        s.w3 = [sb(f"w3_{i}", [P, KC, FE], at) for i, at in enumerate((16, 112))]
        s.w2 = [sb(f"w2_{i}", [P, FT, DM], at) for i, at in enumerate((128, 160))]
        s.w1_in, s.w3_in, s.w2_in = ([sem(f"{n}_in{i}") for i in range(2)] for n in ("w1", "w3", "w2"))

        def load_expert(eng, e, j, which, done=None):
            dst, src, into = {"w1": (s.w1, a["expert_w1"], s.w1_in), "w3": (s.w3, a["expert_w3"], s.w3_in),
                              "w2": (s.w2, a["expert_w2"], s.w2_in)}[which]
            eng.dma_start(dst[j][:, :, :], src[bass.ds(e, 1)].rearrange("o (c p) n -> p (o c) n", p=P)
                          ).then_inc(into[j] if done is None else done, 16)
        s.load_expert = load_expert
        mix(nc, a, s)
        route(nc, a, s)
        experts(nc, a, s)
        combine(nc, a, s)
    return nc


def project(nc, a, s):
    sb, sem, psum = s.sb, s.sem, s.psum
    xs = sb("xs", [P, NT, DM], 40)
    wt = [sb(f"wt{i}", [P, KC, P], 161.5 + 4 * i) for i in range(2)]
    wk = sb("wk", [P, KC, 512], 169.5)
    relu = [sb(f"relu{i}", [P, SEQ], 185.5 + 4 * i) for i in range(2)]
    rows = [sb(f"rows{i}", [NH, SEQ], 104 + 4 * i) for i in range(4)]
    gT = sb("gT", [P, KC], 205)
    rstd = sb("rstd", [P, NT], 205.125)
    ssq = sb("ssq", [P, NT], 205.25)
    ifb = sb("ifb", [NH, 2], 205.375)
    conv = sb("conv", [P, 4, 5], 205.5)
    eps = sb("eps", [P, 1], 205.875)
    one = sb("one", [NH, 1], 205.9375)
    zeros = sb("zeros", [CAP, DM], 120)
    far = sb("far", [P, NH, 768], 144.75)
    rel = sb("rel", [P, NH, N_REL], 157)

    x_in = s.x_in
    small_in, rel_in, far_ready, far_out = sem("small_in"), sem("rel_in"), sem("far_ready"), sem("far_out")
    w_in = [sem(f"w_in{i}") for i in range(2)]
    wk_in = sem("wk_in")
    ident_ready, const_ready = sem("ident_ready"), sem("const_ready")
    s.squared = squared = sem("squared")
    mean_ready, root_ready, normed = sem("mean_ready"), sem("root_ready"), sem("normed")
    xT_ready, xT_taken = sem("xT_ready"), sem("xT_taken")
    zeros_ready = sem("zeros_ready")
    tok_ready, tok_taken = sem("tok_ready"), sem("tok_taken")
    gate_rows = sem("gate_rows")
    soft_ready, rows_done = sem("soft_ready"), sem("rows_done")
    idx_proj, idx_proj_taken = sem("idx_proj"), sem("idx_proj_taken")
    idx_ready, idx_taken, relu_used = sem("idx_ready"), sem("idx_taken"), sem("relu_used")
    gate_cols, gate_cols_taken = sem("gate_cols"), sem("gate_cols_taken")
    proj_ready, proj_taken = sem("proj_ready"), sem("proj_taken")
    conv_ready, sig_ready = sem("conv_ready"), sem("sig_ready")

    idx_blocks = list(range(2, NT))
    NTOK = 3
    chunk_cols = [GW, 512, 512]
    NP = NTT - 2

    with nc.Block() as block:
        @block.sync
        def _(sp):
            sp.dma_start(gT[:, :], a["g_mix"]).then_inc(small_in, 16)
            sp.dma_start(ifb[:, :], a["if_bias"]).then_inc(small_in, 16)
            sp.dma_start(conv[:, :, :], a["conv"]).then_inc(small_in, 16)
            sp.dma_start(rel[:, :, :], a["rel"].partition_broadcast(P)).then_inc(rel_in, 16)
            for t in range(NT):
                sp.dma_start(xs[:, t, :], a["x"][t * P:(t + 1) * P, :]).then_inc(x_in[t], 16)
            sp.wait_ge(far_ready, 1)
            sp.dma_start(s.shifted, far[:, :, :]).then_inc(far_out, 16)
            sp.dma_start(wk[:, :, 0:GW], a["w_gates12"]).then_inc(wk_in, 16)
            for j in range(2):
                sp.dma_start(wt[j][:, :, :], a["w_T"][j]).then_inc(w_in[j], 16)
            sp.wait_ge(zeros_ready, 1)
            sp.dma_start(s.ys[NE * CAP:SLOTS, :].rearrange("(b p) n -> p b n", p=CAP),
                         zeros[:, :].unsqueeze(1).to_broadcast([CAP, N_OV, DM])).then_inc(s.y_stored[1], 16)
            for c in range(2):
                sp.wait_ge(tok_ready, NT * (c + 1))
                sp.dma_start(wk[:, :, :], a["w_V"][c]).then_inc(wk_in, 16)
            sp.wait_ge(idx_proj, 1)
            sp.dma_start(wt[0][:, :, :], a["w_T"][2]).then_inc(w_in[0], 16)
            sp.wait_ge(idx_proj, 2)
            sp.dma_start(wt[1][:, :, :], a["w_T"][3]).then_inc(w_in[1], 16)
            with sp.Fori(1, NP // 2) as i:
                for j in range(2):
                    sp.wait_ge(proj_ready, i * 2 + (j - 1))
                    sp.dma_start(wt[j][:, :, :], a["w_T"][bass.ds(i * 2 + (2 + j), 1)]
                                 .rearrange("o p c n -> (o p) c n")).then_inc(w_in[j], 16)

        @block.gpsimd
        def _(pool):
            pool.memset(s.ident[:, :], 0.0).then_inc(ident_ready, 1)
            pool.wait_ge(ident_ready, 1)
            pool.affine_select(out=s.ident[:, :], in_=s.ident[:, :], compare_op=ALU.not_equal, fill=1.0,
                               base=0, pattern=[[-1, P]], channel_multiplier=1).then_inc(ident_ready, 1)
            pool.memset(zeros[:, :], 0.0).then_inc(zeros_ready, 1)
            pool.memset(eps[:, :], EPS).then_inc(const_ready, 1)
            pool.memset(one[:, :], 1.0).then_inc(const_ready, 1)
            pool.memset(s.sel4[:, :, :], 0.0).then_inc(const_ready, 1)
            pool.wait_ge(const_ready, 3)
            pool.affine_select(out=s.sel4[:, :, :], in_=s.sel4[:, :, :], compare_op=ALU.not_equal, fill=1.0,
                               base=0, pattern=[[-1, NH], [0, P]], channel_multiplier=1).then_inc(const_ready, 1)
            pool.memset(s.vB[:, :, :, HD:HD + 1], 1.0).then_inc(const_ready, 1)
            pool.wait_ge(rel_in, 16)
            pool.tensor_copy(far[:, :, 0:511], rel[:, :, 0:1].to_broadcast([P, NH, 511]))
            pool.tensor_copy(far[:, :, 511:511 + N_REL], rel[:, :, :])
            pool.tensor_copy(far[:, :, 511 + N_REL:768],
                             rel[:, :, N_REL - 1:N_REL].to_broadcast([P, NH, 768 - 511 - N_REL])).then_inc(far_ready, 1)

        @block.scalar
        def _(act):
            link = chained(act, s.act_chain)
            for t in range(NT):
                act.wait_ge(x_in[t], 16)
                nc.scalar.activation(relu[t % 2][:, :], xs[:, t, :], ACT.Square,
                                     accum_out=ssq[:, t:t + 1]).then_inc(squared, 1)
                if t < NT - 1:
                    act.wait_ge(squared, t + 1)
            act.wait_ge(mean_ready, 1)
            act.wait_ge(const_ready, 5)
            nc.scalar.activation(rstd[:, :], ssq[:, :], ACT.Sqrt, bias=eps[:, 0:1],
                                 scale=1.0 / DM).then_inc(root_ready, 1)
            act.wait_ge(small_in, 48)
            for n in range(2 * KC):
                h, c = n // KC, n % KC
                act.wait_ge(xT_ready, n + 1)
                nc.scalar.activation(s.hT[:, c, h * 512:(h + 1) * 512], psum[:, n % 4, :], ACT.Copy,
                                     scale=gT[:, c:c + 1]).then_inc(xT_taken, 1)
            for t in range(NT):
                act.wait_ge(tok_ready, t + 1)
                nc.scalar.activation(s.g12[:, t, :], psum[:, t % 4, W:GW], ACT.Copy)
                nc.scalar.activation(s.oB[:, t, :], psum[:, t % 4, 0:W], ACT.Sigmoid).then_inc(tok_taken, 1)
            act.wait_ge(gate_rows, 2)
            link(nc.scalar.activation(rows[0][:, :], psum[0:NH, 4:6, :].rearrange("p a b -> p (a b)"),
                                      ACT.Identity, bias=ifb[:, 0:1]))
            link(nc.scalar.activation(rows[1][:, :], psum[0:NH, 6:8, :].rearrange("p a b -> p (a b)"),
                                      ACT.Identity, bias=ifb[:, 1:2]))
            link(nc.scalar.activation(rows[2][:, :], rows[1][:, :], ACT.Abs))
            link(nc.scalar.activation(rows[2][:, :], rows[2][:, :], ACT.Exp, scale=-1.0))
            nc.scalar.activation(rows[2][:, :], rows[2][:, :], ACT.Ln, bias=one[:, 0:1]).then_inc(soft_ready, 1)
            for n in range(4):
                act.wait_ge(idx_proj, n // 2 + 1)
                nc.scalar.activation(s.tT[:, n // 2, (n % 2) * 512:(n % 2 + 1) * 512], psum[:, n, :],
                                     ACT.Copy).then_inc(idx_proj_taken, 1)
            n = 0
            for b in idx_blocks:
                for h in range(NH):
                    act.wait_ge(idx_ready, n + 1)
                    if n >= 2:
                        act.wait_ge(relu_used, n - 1)
                    k = 4 + 2 * (n % 2)
                    nc.scalar.activation(relu[n % 2][:, 0:width(b)],
                                         psum[:, k:k + 2, :].rearrange("p a b -> p (a b)")[:, 0:width(b)],
                                         ACT.Relu).then_inc(idx_taken, 1)
                    n += 1
            act.wait_ge(gate_cols, 1)
            nc.scalar.activation(s.a_tok[:, :, :], psum[:, 0, 0:NT * NH].rearrange("p (t h) -> p t h", h=NH),
                                 ACT.Copy).then_inc(gate_cols_taken, 1)
            nc.scalar.activation(s.enm[:, :, :], psum[:, 0, NT * NH:2 * NT * NH]
                                 .rearrange("p (t h) -> p t h", h=NH), ACT.Exp).then_inc(gate_cols_taken, 1)
            act.wait_ge(s.y_stored[1], 16)
            for c in range(2):
                for t in range(NT):
                    n = NT * (c + 1) + t
                    act.wait_ge(tok_ready, n + 1)
                    if c == 0:
                        nc.scalar.activation(s.vA[:, t, :], psum[:, t % 4, 0:W], ACT.Copy)
                        nc.scalar.activation(s.vC[:, t, :], psum[:, t % 4, W:2 * W], ACT.Copy).then_inc(tok_taken, 1)
                    else:
                        nc.scalar.activation(s.vB[:, t, :, 0:HD],
                                             psum[:, t % 4, 0:W].rearrange("p (h d) -> p h d", d=HD), ACT.Copy)
                        nc.scalar.activation(s.vD[:, t, :], psum[:, t % 4, W:2 * W], ACT.Copy).then_inc(tok_taken, 1)
            def tile_out(t, j):
                act.wait_ge(proj_ready, t + 1)
                nc.scalar.activation(s.tT[:, bass.ds(t + 2, 1), :].rearrange("p o n -> p (o n)"),
                                     psum[:, 2 * j:2 * j + 2, :].rearrange("p a b -> p (a b)"),
                                     ACT.Copy).then_inc(proj_taken, 1)

            with act.Fori(0, NP // 2 - 2) as i:
                for j in range(2):
                    tile_out(i * 2 + j, j)
            for n in range(4):
                act.wait_ge(conv_ready, n + 1)
                nc.scalar.activation(relu[n % 2][:, :], wk[:, 2 * (n % 2):2 * (n % 2) + 2, :]
                                     .rearrange("p a b -> p (a b)"), ACT.Sigmoid).then_inc(sig_ready, 1)
                if n != 1:
                    tile_out(NP - 4 + max(n - 1, 0), max(n - 1, 0) % 2)
            tile_out(NP - 1, 1)

        @block.vector
        def _(dve):
            link = chained(dve, s.dve_chain)

            def convolve():
                dve.wait_ge(tok_ready, 3 * NT)
                dve.wait_ge(small_in, 48)
                for n in range(4):
                    dve.wait_ge(proj_taken, n + 1)
                    src = s.tT[:, T_QB + n, :]
                    y = wk[:, 2 * (n % 2):2 * (n % 2) + 2, :].rearrange("p a b -> p (a b)")
                    link(nc.vector.tensor_scalar(y, src, conv[:, n, 3:4], conv[:, n, 4:5], ALU.mult, ALU.add))
                    for k in range(3):
                        d = 3 - k
                        ins = nc.vector.scalar_tensor_tensor(out=y[:, d:], in0=src[:, 0:SEQ - d],
                                                             scalar=conv[:, n, k:k + 1], in1=y[:, d:],
                                                             op0=ALU.mult, op1=ALU.add)
                        if k < 2:
                            link(ins)
                    ins.then_inc(conv_ready, 1)
                    dve.wait_ge(sig_ready, n + 1)
                    link(nc.vector.tensor_tensor(src, y, relu[n % 2][:, :], ALU.mult))

            dve.wait_ge(squared, NT)
            nc.vector.engine_nop().then_inc(mean_ready, 1)
            dve.wait_ge(root_ready, 1)
            link(nc.vector.reciprocal(rstd[:, :], rstd[:, :]))
            for t in range(NT):
                nc.vector.tensor_scalar(xs[:, t, :], xs[:, t, :], rstd[:, t:t + 1], None,
                                        ALU.mult).then_inc(normed, 1)
            dve.wait_ge(soft_ready, 1)
            link(nc.vector.tensor_scalar(rows[1][:, :], rows[1][:, :], 0.0, None, ALU.min))
            link(nc.vector.tensor_tensor(rows[1][:, :], rows[1][:, :], rows[2][:, :], ALU.subtract))
            link(nc.vector.memset(rows[3][:, :], 1.0))
            link(nc.vector.tensor_tensor_scan(rows[2][:, :], rows[3][:, :], rows[1][:, :], 0.0,
                                              ALU.mult, ALU.add))
            link(nc.vector.tensor_tensor(rows[0][:, :], rows[0][:, :], rows[2][:, :], ALU.subtract))
            link(nc.vector.tensor_tensor_scan(rows[3][:, :], rows[0][:, :], rows[0][:, :], 0.0,
                                              ALU.max, ALU.max))
            link(nc.vector.tensor_scalar(s.negm[:, :], rows[3][:, :], -1.0, None, ALU.mult))
            nc.vector.tensor_tensor(rows[1][:, :], s.negm[:, :], rows[2][:, :],
                                    ALU.subtract).then_inc(rows_done, 1)
            dve.wait_ge(far_out, 16)
            n = 0
            for b in idx_blocks:
                wd = width(b)
                sc = s.sel[:, SEL_AT[b]:SEL_AT[b] + wd]
                for h in range(NH):
                    dve.wait_ge(idx_taken, n + 1)
                    wi = s.g12[:, b, h:h + 1]
                    if h == 0:
                        ins = nc.vector.tensor_scalar(sc, relu[n % 2][:, 0:wd], wi, None, ALU.mult)
                    else:
                        ins = nc.vector.scalar_tensor_tensor(out=sc, in0=relu[n % 2][:, 0:wd], scalar=wi, in1=sc,
                                                             op0=ALU.mult, op1=ALU.add)
                    ins.then_inc(relu_used, 1)
                    n += 1
                    dve.wait_ge(relu_used, n)
                link(nc.vector.memset(s.sel[0:CH, SEL_AT[b] + wd - CH:SEL_AT[b] + wd], NEG))
            for b in idx_blocks[:-1]:
                for k in range(TOPK // 8):
                    s.take8(link, b)
                s.taken_mask(link, b)
            convolve()
            for k in range(TOPK // 8 - LATE):
                s.take8(link, NT - 1)

        @block.tensor
        def _(pe):
            pe.wait_ge(ident_ready, 2)
            for n in range(2 * KC):
                h, c = n // KC, n % KC
                pe.wait_ge(normed, 4 * (h + 1))
                if n >= 4:
                    pe.wait_ge(xT_taken, n - 3)
                for t in range(4):
                    ins = nc.tensor.transpose(psum[:, n % 4, t * P:(t + 1) * P],
                                              xs[:, 4 * h + t, c * P:(c + 1) * P], s.ident[:, :])
                ins.then_inc(xT_ready, 1)

            def tok_chunk(c):
                cols = chunk_cols[c]
                pe.wait_ge(wk_in, 16 * (c + 1))
                for t in range(NT):
                    n = c * NT + t
                    if c == 0:
                        pe.wait_ge(xT_taken, 2 * KC if t >= 4 else KC)
                        if t == 0:
                            pe.wait_ge(xT_taken, 2 * KC)
                    if n >= 4:
                        pe.wait_ge(tok_taken, n - 3)
                    for k in range(KC):
                        ins = nc.tensor.matmul(psum[:, n % 4, 0:cols], s.hT[:, k, t * P:(t + 1) * P],
                                               wk[:, k, 0:cols], start=(k == 0), stop=(k == KC - 1))
                    ins.then_inc(tok_ready, 1)

            tok_chunk(0)
            pe.wait_ge(tok_taken, NT)
            for g in range(2):
                for t in range(NT):
                    ins = nc.tensor.transpose(psum[0:NH, 4 + 2 * g + t // 4, (t % 4) * P:(t % 4 + 1) * P],
                                              s.g12[:, t, NH * (g + 1):NH * (g + 2)], s.ident[:, :])
                ins.then_inc(gate_rows, 1)

            def tile(j, bank):
                for h in range(2):
                    for k in range(KC):
                        ins = nc.tensor.matmul(psum[:, bank + h, :], wt[j][:, k, :],
                                               s.hT[:, k, h * 512:(h + 1) * 512],
                                               start=(k == 0), stop=(k == KC - 1))
                return ins

            for j in range(2):
                pe.wait_ge(w_in[j], 16)
                tile(j, 2 * j).then_inc(idx_proj, 1)
            pe.wait_ge(idx_proj_taken, 4)
            pe.wait_ge(soft_ready, 1)
            n = 0
            for b in idx_blocks:
                wd = width(b)
                for h in range(NH):
                    if n >= 2:
                        pe.wait_ge(idx_taken, n - 1)
                    for c0 in range(0, wd, 512):
                        c1 = min(wd, c0 + 512)
                        ins = nc.tensor.matmul(psum[:, 4 + 2 * (n % 2) + c0 // 512, 0:c1 - c0],
                                               s.tT[DI * h:DI * (h + 1), T_QI, b * P:(b + 1) * P],
                                               s.tT[DI * h:DI * (h + 1), T_KI, c0:c1], start=True, stop=True)
                    ins.then_inc(idx_ready, 1)
                    n += 1
            pe.wait_ge(rows_done, 1)
            for g in range(2):
                for t in range(NT):
                    at = (g * NT + t) * NH
                    ins = nc.tensor.transpose(psum[:, 0, at:at + NH], rows[g][:, t * P:(t + 1) * P],
                                              s.ident[0:NH, 0:NH])
            ins.then_inc(gate_cols, 1)
            pe.wait_ge(gate_cols_taken, 2)
            tok_chunk(1)
            tok_chunk(2)
            pe.wait_ge(tok_taken, 3 * NT)
            for j in range(2):
                pe.wait_ge(w_in[j], 32)
                tile(j, 2 * j).then_inc(proj_ready, 1)
            with pe.Fori(1, NP // 2) as i:
                for j in range(2):
                    pe.wait_ge(w_in[j], i * 16 + 32)
                    pe.wait_ge(proj_taken, i * 2 + (j - 1))
                    tile(j, 2 * j).then_inc(proj_ready, 1)


def attend(nc, a, s):
    sb, sem, psum = s.sb, s.sem, s.psum
    pbuf = [sb(f"pbuf{i}", [P, SEQ], 161.5 + 4 * i) for i in range(4)]
    pt = [sb(f"pt{i}", [P, 512], 177.5 + 2 * i) for i in range(4)]
    sq = sb("sq", [P, NT, NH, HD], 185.5)
    kt = sb("kt", [P, NT, W], 161.5)
    o_sum = sb("o_sum", [P, NH, HD + 1], 161.5)
    ex = [sb(f"ex{i}", [P, NH, P], 169.5 + 2 * i) for i in range(2)]
    wts = [sb(f"wts{i}", [P, NH, P], 173.5 + 2 * i) for i in range(2)]
    state = sb("state", [P, NT - 1, NH, HD + 1], 177.5)
    vw = sb("vw", [P, NT - 1, NH, HD + 1], 185.5)
    ends = sb("ends", [P, 2, NT, NH], 192.75)
    decay = sb("decay", [P, 3, NT, NH], 193.5)
    bias = sb("bias", [P, NH, BAND], 194)
    mask01 = sb("mask01", [P, 3 * P], 185.5)
    y = {"B": sb("yB", [P, NT, W], 32), "D": sb("yD", [P, NT, W], 128),
         "C": sb("yC", [P, NT, W], 32), "A": sb("yA", [P, NT, W], 128)}
    yT_at = {"B": T_QB, "D": T_QD, "C": T_QC, "A": T_QA}
    gainB = sb("gainB", [P, W], 200)
    gainD = sb("gainD", [P, W], 193.5 + 12.5)
    lam_in = sb("lam_in", [P, 4, DI], 201)
    lam = sb("lam", [P, 8], 204.875)
    stat = sb("stat", [P, 4, 8], 205.125)
    sums = sb("sums", [P, 2, NH, 2], 205.25)
    inv = sb("inv", [P, NH], 205.375)
    ms = {"B": sb("msB", [P, NT * NH], 205.5), "D": sb("msD", [P, NT * NH], 205.625)}
    eps = sb("eps2", [P, 1], 205.875)

    loads_in, bias_in = sem("loads_in"), sem("bias_in")
    prep_ready, prep_taken = sem("prep_ready"), sem("prep_taken")
    step_ready, state_ready, b_arg = sem("step_ready"), sem("state_ready"), sem("b_arg")
    b_scores, b_exp, b_masked = sem("b_scores"), sem("b_exp"), sem("b_masked")
    b_weights, b_pv, b_normed = sem("b_weights"), sem("b_pv"), sem("b_normed")
    scores_ready, stats_ready, exp_done = sem("scores_ready"), sem("stats_ready"), sem("exp_done")
    diff_ready, pt_ready, pt_copied = sem("diff_ready"), sem("pt_ready"), sem("pt_copied")
    pv_done, out_normed = sem("pv_done"), sem("out_normed")
    squares_summed, roots, inverse, y_ready = sem("squares_summed"), sem("roots"), sem("inverse"), sem("y_ready")
    gain_ready, lam_ready, band_ready = sem("gain_ready"), sem("lam_ready"), sem("band_ready")
    aneg_ready = sem("aneg_ready")

    NB = NT * NH
    KT_BANKS, STEP_BANKS = (0, 1, 4, 5), (2, 3, 6, 7)
    Y_AT = 24
    D_FROM = NB - 2 * (LATE - LATE_B)
    b_units = [(b, h) for b in range(NT) for h in range(NH)]
    units = [(kind, b, h) for kind in "DCA" for b, h in b_units]
    NU = len(units)

    def keys(kind, b):
        k0 = max(0, b - BAND // P + 1) if kind == "C" else 0
        return k0, b + 1 - k0

    def slots(u):
        return (0, 1) if units[u][0] == "D" else (u % 2,)

    def bufs(u):
        return (2 * (u % 2), 2 * (u % 2) + 1) if units[u][0] == "D" else (u % 4,)

    def before(u, of):
        mine = set(of(u))
        return max((v for v in range(u) if mine & set(of(v))), default=None)

    groups = []
    for u, (kind, b, h) in enumerate(units):
        k0, nk = keys(kind, b)
        for g0 in range(0, nk, 4):
            groups.append((u, g0, min(4, nk - g0), g0 + 4 >= nk))
        if u % NB == Y_AT:
            groups += [({"D": "B", "C": "D", "A": "C"}[kind], g, 4, False) for g in range(4)]
    groups += [("A", g, 4, False) for g in range(4)]
    ready_after = {g[0]: i + 1 for i, g in enumerate(groups)}
    pv_after, _m = {}, 0
    for g in groups:
        if not isinstance(g[0], str):
            _m += 1
            pv_after[g[0]] = _m

    n_exp = [0]
    for kind, _, _ in units:
        n_exp.append(n_exp[-1] + (2 if kind == "D" else 1))

    def slot_cols(slot, n):
        return psum[:, 2 * slot:2 * slot + 2, :].rearrange("p a b -> p (a b)")[:, 0:n]

    out_heads = [psum[:, 6 + k, 0:NH * (HD + 1)].rearrange("p (h d) -> p h d", d=HD + 1) for k in range(2)]

    with nc.Block() as block:
        @block.sync
        def _(sp):
            sp.dma_start(gainB[:, :], a["g_mlstm"].partition_broadcast(P)).then_inc(loads_in, 16)
            sp.dma_start(gainD[:, :], a["g_diff"].partition_broadcast(P)).then_inc(loads_in, 16)
            sp.dma_start(lam_in[:, :, :], a["lam"].partition_broadcast(P)).then_inc(loads_in, 16)
            sp.wait_ge(b_pv, NT)
            sp.wait_ge(gain_ready, 1)
            sp.wait_ge(lam_ready, 1)
            sp.dma_start(bias[:, :, :], bass.AP(s.shifted.tensor, P - 1, [[NH * 768 - 1, P], [768, NH], [1, BAND]])
                         ).then_inc(bias_in, 16)

        @block.gpsimd
        def _(pool):
            link = chained(pool, s.pool_chain)
            pool.memset(eps[:, :], EPS).then_inc(aneg_ready, 1)
            pool.wait_ge(loads_in, 48)
            for t in range(NT):
                ins = pool.tensor_tensor(s.oB[:, t, :], s.oB[:, t, :], gainB[:, :], ALU.mult)
            ins.then_inc(gain_ready, 1)
            pool.wait_ge(gain_ready, 1)
            link(pool.tensor_scalar(gainD[:, :], gainD[:, :], 0.8, 0.0, ALU.mult, ALU.add))
            for b in range(NT):
                pool.wait_ge(b_exp, b + 1)
                e = ex[b % 2][:, :, :]
                pool.affine_select(out=e, in_=e, compare_op=ALU.is_ge, fill=0.0, base=0,
                                   pattern=[[0, NH], [1, P]], channel_multiplier=-1).then_inc(b_masked, 1)

            def head_norm(kind, n, waits):
                sem_, value = waits
                pool.wait_ge(sem_, value)
                yy = y[kind][:, :, :].rearrange("p t (h d) -> p (t h) d", d=HD)
                link(pool.tensor_tensor(sq[:, :, :, :].rearrange("p t h d -> p (t h) d"), yy, yy, ALU.mult))
                q = sq[:, :, :, :].rearrange("p t h d -> p (t h) d")
                half = HD // 2
                while half:
                    ins = pool.tensor_tensor(q[:, :, 0:half], q[:, :, 0:half], q[:, :, half:2 * half], ALU.add)
                    if half > 1:
                        link(ins)
                    half //= 2
                ins.then_inc(squares_summed, 1)
                pool.wait_ge(inverse, n + 1)
                link(pool.tensor_tensor(yy, yy, ms[kind][:, :].unsqueeze(2).to_broadcast([P, NT * NH, HD]), ALU.mult))

            head_norm("B", 0, (b_normed, NT))
            pool.tensor_tensor(y["B"][:, :, :], y["B"][:, :, :], s.oB[:, :, :], ALU.mult).then_inc(y_ready, 1)
            pool.wait_ge(bias_in, 16)
            link(pool.tensor_scalar(bias[:, :, :], bias[:, :, :], 8.0, 0.0, ALU.mult, ALU.add))
            pool.memset(bias[0:CH, :, BAND - CH:BAND], NEG)
            pool.memset(bias[CH:P, :, 0:CH], NEG).then_inc(band_ready, 1)
            head_norm("D", 1, (out_normed, NT))
            pool.tensor_tensor(y["D"][:, :, :], y["D"][:, :, :],
                               gainD[:, :].unsqueeze(1).to_broadcast([P, NT, W]), ALU.mult).then_inc(y_ready, 1)
            pool.wait_ge(y_ready, 2)
            link(pool.memset(mask01[:, :], 0.0))
            pool.memset(mask01[0:CH, CH:P], NEG)
            pool.memset(mask01[0:CH, 3 * P - CH:3 * P], NEG).then_inc(band_ready, 1)

        @block.scalar
        def _(act):
            link = chained(act, s.act_chain)
            for n in range(NT // 2):
                act.wait_ge(prep_ready, n + 2)
                nc.scalar.activation(kt[:, 2 * n:2 * n + 2, :].rearrange("p t n -> p (t n)"),
                                     psum[:, KT_BANKS[n], :], ACT.Copy).then_inc(prep_taken, 1)
            act.wait_ge(lam_ready, 1)
            nc.scalar.activation(lam[:, 2:4], lam[:, 0:2], ACT.Exp).then_inc(lam_ready, 1)
            act.wait_ge(b_arg, 1)
            nc.scalar.activation(decay[:, :, :, :], decay[:, :, :, :], ACT.Exp).then_inc(prep_taken, 1)
            for b in range(NT):
                act.wait_ge(b_arg, b + 2)
                nc.scalar.activation(ex[b % 2][:, :, :], ex[b % 2][:, :, :], ACT.Exp).then_inc(b_exp, 1)

            def root(n):
                kind = "BD"[n]
                act.wait_ge(squares_summed, n + 1)
                act.wait_ge(aneg_ready, 1)
                nc.scalar.activation(ms[kind][:, :], sq[:, :, :, 0:1].rearrange("p t h o -> p (t h o)"), ACT.Sqrt,
                                     bias=eps[:, 0:1], scale=1.0 / HD).then_inc(roots, 1)

            at, m = 0, 0
            for u in range(NU + 1):
                kind, b, h = units[u] if u < NU else ("", 0, 0)
                if u < NU:
                    wd = keys(kind, b)[1] * P
                    prev = before(u, bufs)
                    if kind == "D":
                        if prev is None:
                            act.wait_ge(b_pv, NT)
                        else:
                            act.wait_ge(pt_ready, ready_after[prev])
                    if h == 0 and u // NH >= 2:
                        act.wait_ge(out_normed, u // NH - 1)
                    act.wait_ge(stats_ready, n_exp[u] + 1)

                def diff_exp(r):
                    nc.scalar.activation(pbuf[bufs(u)[r]][:, 0:wd], slot_cols(r, wd), ACT.Exp,
                                         bias=stat[:, u % 4, 2 + r:3 + r], scale=DI ** -0.5,
                                         accum_out=sums[:, b % 2, h, r:r + 1]).then_inc(exp_done, 1)
                if kind == "D":
                    diff_exp(0)
                elif kind:
                    buf = pbuf[bufs(u)[0]][:, 0:wd]
                    nc.scalar.activation(buf, buf, ACT.Exp, bias=stat[:, u % 4, 0:1], scale=-1.0,
                                         accum_out=sums[:, b % 2, h, 0:1]).then_inc(exp_done, 1)
                if u == 12:
                    root(0)
                if u == NB + 12:
                    root(1)
                while u and at < len(groups) and (isinstance(groups[at][0], str) or groups[at][0] < u):
                    what, g0, ng, last = groups[at]
                    act.wait_ge(pt_ready, at + 1)
                    src = psum[:, 4 + at % 2, 0:ng * P]
                    if isinstance(what, str):
                        c, t0 = g0 % 2, g0 // 2 * 4
                        dst = s.tT[:, yT_at[what] + c, t0 * P:(t0 + 4) * P]
                    else:
                        dst = pt[m % 4][:, 0:ng * P]
                        if m >= 4:
                            act.wait_ge(pv_done, m - 3)
                        m += 1
                    nc.scalar.activation(dst, src, ACT.Copy).then_inc(pt_copied, 1)
                    at += 1
                if kind == "D":
                    act.wait_ge(stats_ready, n_exp[u] + 2)
                    diff_exp(1)

        @block.vector
        def _(dve):
            link = chained(dve, s.dve_chain)
            dve.wait_ge(loads_in, 48)
            for k in range(2):
                ins = nc.vector.tensor_tensor_reduce(out=lam_in[:, 2 * k, :], in0=lam_in[:, 2 * k, :],
                                                     in1=lam_in[:, 2 * k + 1, :], scale=1.0, scalar=0.0,
                                                     op0=ALU.mult, op1=ALU.add, accum_out=lam[:, k:k + 1])
            ins.then_inc(lam_ready, 1)
            dve.wait_ge(lam_ready, 2)
            link(nc.vector.tensor_tensor(lam[:, 4:5], lam[:, 3:4], lam[:, 2:3], ALU.subtract))
            link(nc.vector.tensor_scalar(lam[:, 4:5], lam[:, 4:5], -0.2, None, ALU.add))

            dve.wait_ge(prep_ready, 1)
            link(nc.vector.tensor_copy(ends[:, :, :, :].rearrange("p k t h -> p (k t h)"),
                                       psum[:, 3, 0:2 * NT * NH]))
            link(nc.vector.memset(decay[:, 1:3, 0, :], 0.0))
            nc.vector.tensor_tensor(decay[:, 0, :, :], s.a_tok[:, :, :], ends[:, 0, :, :], ALU.add)
            nc.vector.tensor_tensor(decay[:, 1, 1:NT, :], ends[:, 1, 1:NT, :], ends[:, 0, 0:NT - 1, :],
                                    ALU.subtract)
            nc.vector.tensor_tensor(decay[:, 2, 1:NT, :], ends[:, 0, 1:NT, :], ends[:, 0, 0:NT - 1, :],
                                    ALU.subtract).then_inc(b_arg, 1)

            def b_exponent(b):
                dve.wait_ge(b_scores, 3 * b + 1)
                if b >= 2:
                    dve.wait_ge(b_weights, b - 1)
                link(nc.vector.tensor_tensor(ex[b % 2][:, :, :], psum[:, 4 + b % 2, :]
                                             .rearrange("p (h n) -> p h n", h=NH),
                                             s.a_tok[:, b, :].unsqueeze(2).to_broadcast([P, NH, P]), ALU.add))
                nc.vector.tensor_scalar(ex[b % 2][:, :, :], ex[b % 2][:, :, :], 0.0, None,
                                        ALU.min).then_inc(b_arg, 1)

            def b_norm(b):
                dve.wait_ge(b_pv, b + 1)
                o = o_sum[:, :, :]
                own = out_heads[b % 2]
                if b:
                    off = psum[:, 2 + b % 2, 0:NH * (HD + 1)].rearrange("p (h d) -> p h d", d=HD + 1)
                    link(nc.vector.scalar_tensor_tensor(
                        out=o, in0=off, scalar=HD ** -0.5,
                        in1=decay[:, 1, b, :].unsqueeze(2).to_broadcast([P, NH, HD + 1]),
                        op0=ALU.mult, op1=ALU.mult))
                    link(nc.vector.tensor_tensor(o, o, own, ALU.add))
                else:
                    o = own
                link(nc.vector.tensor_tensor(inv[:, :], o[:, :, HD], s.enm[:, b, :], ALU.max))
                link(nc.vector.scalar_tensor_tensor(out=inv[:, :], in0=o[:, :, HD], scalar=-1.0,
                                                    in1=inv[:, :], op0=ALU.mult, op1=ALU.max))
                link(nc.vector.reciprocal(inv[:, :], inv[:, :]))
                nc.vector.tensor_tensor(y["B"][:, b, :].rearrange("p (h d) -> p h d", d=HD), o[:, :, 0:HD],
                                        inv[:, :].unsqueeze(2).to_broadcast([P, NH, HD]),
                                        ALU.mult).then_inc(b_normed, 1)
                dve.wait_ge(b_normed, b + 1)

            b_exponent(0)
            b_exponent(1)
            dve.wait_ge(prep_taken, NT // 2 + 1)
            nc.vector.tensor_tensor(vw[:, :, :, :], s.vB[:, 0:NT - 1, :, :],
                                    decay[:, 0, 0:NT - 1, :].unsqueeze(3).to_broadcast([P, NT - 1, NH, HD + 1]),
                                    ALU.mult).then_inc(state_ready, 1)
            for b in range(NT - 1):
                dve.wait_ge(step_ready, b + 1)
                step = psum[:, STEP_BANKS[b % 4], 0:NH * (HD + 1)].rearrange("p (h d) -> p h d", d=HD + 1)
                if b:
                    link(nc.vector.tensor_tensor(state[:, b, :, :], state[:, b - 1, :, :],
                                                 decay[:, 2, b, :].unsqueeze(2).to_broadcast([P, NH, HD + 1]),
                                                 ALU.mult))
                    ins = nc.vector.tensor_tensor(state[:, b, :, :], state[:, b, :, :], step, ALU.add)
                else:
                    ins = nc.vector.tensor_copy(state[:, b, :, :], step)
                ins.then_inc(state_ready, 1)
                dve.wait_ge(state_ready, b + 2)
            for b in range(NT):
                if 1 <= b < NT - 1:
                    b_exponent(b + 1)
                dve.wait_ge(b_scores, 3 * b + 3)
                dve.wait_ge(b_masked, b + 1)
                if b >= 2:
                    dve.wait_ge(b_pv, b - 1)
                nc.vector.scalar_tensor_tensor(out=wts[b % 2][:, :, :].rearrange("p h n -> p (h n)"),
                                               in0=psum[:, b % 2, :], scalar=HD ** -0.5,
                                               in1=ex[b % 2][:, :, :].rearrange("p h n -> p (h n)"),
                                               op0=ALU.mult, op1=ALU.mult).then_inc(b_weights, 1)
                if b:
                    b_norm(b - 1)
                for k in range(2 * LATE_B // NT):
                    s.half_take8(link, NT - 1, k % 2)
            b_norm(NT - 1)

            def norm(n):
                kind, b = units[n * NH][0:2]
                dve.wait_ge(pv_done, pv_after[n * NH + NH - 1])
                link(nc.vector.reciprocal(inv[:, :], sums[:, b % 2, :, 0]))
                if kind == "C" and b == 0:
                    dve.wait_ge(pt_copied, copied_before[NB + 1])
                if kind == "A" and b == 0:
                    dve.wait_ge(pt_copied, copied_before[2 * NB + 1])
                nc.vector.tensor_tensor(y[kind][:, b, :].rearrange("p (h d) -> p h d", d=HD),
                                        psum[:, 6 + n % 2, 0:W].rearrange("p (h d) -> p h d", d=HD),
                                        inv[:, :].unsqueeze(2).to_broadcast([P, NH, HD]),
                                        ALU.mult).then_inc(out_normed, 1)

            copied_before = {v: sum(1 for g in groups[:next(i for i, x in enumerate(groups) if x[0] == v)])
                             for v in (NB + 1, 2 * NB + 1)}
            n_slot, n_diff = 0, 0
            for u in range(NU + 3):
                if 0 < u <= NU and units[u - 1][0] == "D":
                    v = u - 1
                    _, b, h = units[v]
                    wd = width(b)
                    dve.wait_ge(exp_done, 2 * v + 2)
                    link(nc.vector.reciprocal(stat[:, v % 4, 4:5], sums[:, b % 2, h, 1:2]))
                    link(nc.vector.scalar_tensor_tensor(out=stat[:, v % 4, 5:6], in0=stat[:, v % 4, 4:5],
                                                        scalar=sums[:, b % 2, h, 0:1], in1=lam[:, 4:5],
                                                        op0=ALU.mult, op1=ALU.mult))
                    p0, p1 = (pbuf[k][:, 0:wd] for k in bufs(v))
                    nc.vector.scalar_tensor_tensor(out=p0, in0=p1, scalar=stat[:, v % 4, 5:6], in1=p0,
                                                   op0=ALU.mult, op1=ALU.add).then_inc(diff_ready, 1)
                if u < NU:
                    kind, b, h = units[u]
                    k0, nk = keys(kind, b)
                    wd = nk * P
                    if kind == "D":
                        for r in range(2):
                            dve.wait_ge(scores_ready, n_slot + 1)
                            n_slot += 1
                            link(nc.vector.memset(psum[0:CH, 2 * r + (wd - CH) // 512, (wd - CH) % 512:
                                                       (wd - CH) % 512 + CH], NEG))
                            link(nc.vector.reduce_max(stat[:, u % 4, r:r + 1], slot_cols(r, wd), AX.X))
                            nc.vector.tensor_scalar(stat[:, u % 4, 2 + r:3 + r], stat[:, u % 4, r:r + 1],
                                                    -DI ** -0.5, None, ALU.mult).then_inc(stats_ready, 1)
                    else:
                        dve.wait_ge(scores_ready, n_slot + 1)
                        n_slot += 1
                        prev = before(u, bufs)
                        dve.wait_ge(pt_ready, ready_after[prev])
                        if kind == "C":
                            dve.wait_ge(band_ready, 1)
                            add = bias[:, h, BAND - wd:BAND]
                        elif b < 2:
                            dve.wait_ge(band_ready, 2)
                            add = mask01[:, b * P:b * P + wd]
                        else:
                            add = s.sel[:, SEL_AT[b]:SEL_AT[b] + wd]
                        nc.vector.tensor_tensor_reduce(out=pbuf[bufs(u)[0]][:, 0:wd], in0=slot_cols(slots(u)[0], wd),
                                                       in1=add, scale=-HD ** -0.5, scalar=3e38, op0=ALU.add,
                                                       op1=ALU.min, accum_out=stat[:, u % 4, 0:1]
                                                       ).then_inc(stats_ready, 1)
                if D_FROM <= u < NB:
                    s.half_take8(link, NT - 1, (u - D_FROM) % 2)
                if u == NB:
                    s.taken_mask(link, NT - 1)
                if u >= 3 and (u - 3) % NH == NH - 1:
                    norm((u - 3) // NH)
                if u == 13:
                    dve.wait_ge(roots, 1)
                    nc.vector.reciprocal(ms["B"][:, :], ms["B"][:, :]).then_inc(inverse, 1)
                if u == NB + 13:
                    dve.wait_ge(roots, 2)
                    nc.vector.reciprocal(ms["D"][:, :], ms["D"][:, :]).then_inc(inverse, 1)

        @block.tensor
        def _(pe):
            qk = {"B": (T_QB, T_KB), "C": (T_QC, T_KC), "A": (T_QA, T_KA)}

            def head(kind, h, t0, n):
                r = HD * (h % 2)
                return s.tT[r:r + HD, kind + h // 2, t0 * P:(t0 + n) * P]

            for g in range(NH):
                nc.tensor.matmul(psum[:, 3, g:NT * NH:NH], s.sel4[:, g, :], s.negm[:, P - 1:SEQ:P],
                                 start=True, stop=True)
            for t in range(NT):
                ins = nc.tensor.transpose(psum[:, 3, (NT + t) * NH:(NT + t + 1) * NH],
                                          s.negm[:, t * P:(t + 1) * P], s.ident[0:NH, 0:NH])
            ins.then_inc(prep_ready, 1)
            for n in range(NT // 2):
                for q in range(4):
                    b, c = 2 * n + q // 2, q % 2
                    ins = nc.tensor.transpose(psum[:, KT_BANKS[n], q * P:(q + 1) * P],
                                              s.tT[:, T_KB + c, b * P:(b + 1) * P], s.ident[:, :])
                ins.then_inc(prep_ready, 1)

            def b_score(b):
                if b < 2:
                    pe.wait_ge(prep_taken, NT // 2)
                else:
                    pe.wait_ge(b_arg, b)
                for g in range(NH):
                    ins = nc.tensor.matmul(psum[:, 4 + b % 2, g * P:(g + 1) * P], s.sel4[:, g, :],
                                           s.negm[:, b * P:(b + 1) * P], start=True, stop=True)
                ins.then_inc(b_scores, 1)
                if b >= 2:
                    pe.wait_ge(b_weights, b - 1)
                for odd in range(2):
                    if odd:
                        pe.wait_ge(b_scores, 3 * b + 2)
                    for h in (odd, odd + 2):
                        ins = nc.tensor.matmul(psum[:, b % 2, h * P:(h + 1) * P], head(T_KB, h, b, 1),
                                               head(T_QB, h, b, 1), start=True, stop=True)
                    ins.then_inc(b_scores, 1)

            b_score(0)
            b_score(1)
            pe.wait_ge(state_ready, 1)
            for b in range(NT - 1):
                if b >= 4:
                    pe.wait_ge(state_ready, b - 2)
                for c in range(2):
                    ins = nc.tensor.matmul(psum[:, STEP_BANKS[b % 4], 2 * c * (HD + 1):2 * (c + 1) * (HD + 1)],
                                           kt[:, b, c * P:(c + 1) * P],
                                           vw[:, b, 2 * c:2 * c + 2, :].rearrange("p h d -> p (h d)"),
                                           start=True, stop=True)
                ins.then_inc(step_ready, 1)
            pe.wait_ge(state_ready, NT)
            for b in range(NT):
                if 1 <= b < NT - 1:
                    b_score(b + 1)
                if b >= 2:
                    pe.wait_ge(b_normed, b - 1)
                if b:
                    for odd in range(2):
                        if odd:
                            pe.wait_ge(step_ready, NT - 1 + b)
                        for h in (odd, odd + 2):
                            ins = nc.tensor.matmul(psum[:, 2 + b % 2, h * (HD + 1):(h + 1) * (HD + 1)],
                                                   head(T_QB, h, b, 1), state[HD * odd:HD * odd + HD, b - 1, h, :],
                                                   start=True, stop=True)
                        if not odd:
                            ins.then_inc(step_ready, 1)
                pe.wait_ge(b_weights, b + 1)
                for h in range(NH):
                    ins = nc.tensor.matmul(psum[:, 6 + b % 2, h * (HD + 1):(h + 1) * (HD + 1)],
                                           wts[b % 2][:, h, :], s.vB[:, b, h, :], start=True, stop=True)
                ins.then_inc(b_pv, 1)

            def score(u):
                kind, b, h = units[u]
                k0, nk = keys(kind, b)
                prev = before(u, slots)
                if prev is not None and not units[prev][0] == "D":
                    pe.wait_ge(stats_ready, n_exp[prev + 1])
                for r, slot in enumerate(slots(u)):
                    if prev is not None and units[prev][0] == "D":
                        pe.wait_ge(exp_done, n_exp[prev] + (r + 1 if kind == "D" else 2))
                    for c0 in range(0, nk * P, 512):
                        c1 = min(nk * P, c0 + 512)
                        if kind == "D":
                            row = DI * (2 * (h % 2) + r)
                            q = s.tT[row:row + DI, T_QD + h // 2, b * P:(b + 1) * P]
                            k = s.tT[row:row + DI, T_KD + h // 2, c0:c1]
                        else:
                            q = head(qk[kind][0], h, b, 1)
                            k = s.tT[HD * (h % 2):HD * (h % 2) + HD, qk[kind][1] + h // 2, k0 * P + c0:k0 * P + c1]
                        ins = nc.tensor.matmul(psum[:, 2 * slot + c0 // 512, 0:c1 - c0], q, k, start=True, stop=True)
                    ins.then_inc(scores_ready, 1)

            values = {"D": s.vD, "C": s.vC, "A": s.vA}

            def weigh(i, m):
                u, g0, ng, last = groups[i]
                kind, b, h = units[u]
                k0, nk = keys(kind, b)
                n = u // NH
                pe.wait_ge(pt_copied, i + 1)
                if h == 0 and g0 == 0 and n >= 2:
                    pe.wait_ge(out_normed, n - 1)
                for j in range(ng):
                    ins = nc.tensor.matmul(psum[:, 6 + n % 2, h * HD:(h + 1) * HD], pt[m % 4][:, j * P:(j + 1) * P],
                                           values[kind][:, k0 + g0 + j, h * HD:(h + 1) * HD],
                                           start=(g0 + j == 0), stop=(g0 + j == nk - 1))
                ins.then_inc(pv_done, 1)

            pe.wait_ge(b_weights, NT)
            pe.wait_ge(b_normed, NT)
            score(0)
            scored = 0
            m = 0
            for i, (what, g0, ng, last) in enumerate(groups):
                if isinstance(what, str) and not isinstance(groups[i - 1][0], str):
                    weigh(i - 1, m)
                    m += 1
                if i >= 2:
                    pe.wait_ge(pt_copied, i - 1)
                if isinstance(what, str):
                    if g0 == 0:
                        if what in "BD":
                            pe.wait_ge(y_ready, "BD".index(what) + 1)
                        else:
                            pe.wait_ge(out_normed, {"C": 2 * NT, "A": 3 * NT}[what])
                    c, t0 = g0 % 2, g0 // 2 * 4
                    for t in range(4):
                        ins = nc.tensor.transpose(psum[:, 4 + i % 2, t * P:(t + 1) * P],
                                                  y[what][:, t0 + t, c * P:(c + 1) * P], s.ident[:, :])
                    ins.then_inc(pt_ready, 1)
                else:
                    kind, b, h = units[what]
                    if g0 == 0:
                        ahead = min(what + (1 if kind == "D" else 2), NU - 1)
                        for u in range(scored + 1, ahead + 1):
                            score(u)
                        scored = max(scored, ahead)
                    if g0 == 0:
                        if kind == "D":
                            pe.wait_ge(diff_ready, what + 1)
                        else:
                            pe.wait_ge(exp_done, n_exp[what + 1])
                    for j in range(ng):
                        ins = nc.tensor.transpose(psum[:, 4 + i % 2, j * P:(j + 1) * P],
                                                  pbuf[bufs(what)[0]][:, (g0 + j) * P:(g0 + j + 1) * P], s.ident[:, :])
                    ins.then_inc(pt_ready, 1)
                if i and not isinstance(what, str) and not isinstance(groups[i - 1][0], str):
                    weigh(i - 1, m)
                    m += 1
            pe.wait_ge(pt_copied, len(groups))


def mix(nc, a, s):
    sb, sem, psum = s.sb, s.sem, s.psum
    yT_of = (T_QA, T_QB, T_QC, T_QD)
    h_hi = sb("h_hi", [P, KC, SEQ], 128, F32R)
    h_lo = sb("h_lo", [P, KC, SEQ], 0, F32R)
    wg = [sb(f"wg{n}", [P, KC, P], 160 + 4 * n) for n in range(4)]
    wg_lo = [sb(f"wg_lo{n}", [P, KC, P], 160 + 4 * n, F32R) for n in range(4)]
    wg_hi = [sb(f"wg_hi{i}", [P, KC, P], 176 + 4 * i, F32R) for i in range(2)]
    wb = [sb(f"wb{n}", [P, 2, P], 184 + n) for n in range(4)]
    wb_lo = [sb(f"wb_lo{n}", [P, 2, P], 184 + n, F32R) for n in range(4)]
    wb_hi = [sb(f"wb_hi{i}", [P, 2, P], 204.5 + i, F32R) for i in range(2)]
    y_lo = [sb(f"y_lo{n}", [P, 2, SEQ], 32 + 4 * yT_of[n], F32R) for n in range(4)]
    y_hi = [sb(f"y_hi{n}", [P, 2, SEQ], 24 + 4 * yT_of[n], F32R) for n in range(4)]
    sig = [sb(f"sig{i}", [P, SEQ], 188 + 4 * i) for i in range(2)]
    prod = [sb(f"prod{i}", [P, SEQ], 196 + 4 * i) for i in range(2)]
    s.mixT = mixT = sb("mixT", [P, KC, SEQ], 96)
    w_in = [sem(f"wgb_in{n}") for n in range(4)]
    h_high, h_low, w_high, w_low = sem("h_high"), sem("h_low"), sem("w_high"), sem("w_low")
    s.w_high, s.w_low = w_high, w_low
    gate_ready, sig_ready, up_used, summed = sem("gate_ready"), sem("sig_ready3"), sem("up_used"), sem("summed3")

    def steps(eng, body, last=None):
        for n in range(4):
            body(n, 0, n, n)
        with eng.Fori(1, KC) as d:
            for n in range(4):
                body(d * 4 + n, d, n, None)

    with nc.Block() as block:
        @block.sync
        def _(sp):
            def load(d, n):
                sp.dma_start(wg[n][:, :, :], a["w_gate"][n, bass.ds(d, 1)].rearrange("o p c m -> (o p) c m")
                             ).then_inc(w_in[n], 16)
                sp.dma_start(wb[n][:, :, :], a["w_branch"][n, bass.ds(d, 1)].rearrange("o p c m -> (o p) c m")
                             ).then_inc(w_in[n], 16)

            for n in range(4):
                load(0, n)
            with sp.Fori(1, KC) as d:
                for n in range(4):
                    sp.wait_ge(gate_ready, d * 4 + (n - 3))
                    load(d, n)

        @block.tensor
        def _(pe):
            def body(c, d, n, first):
                bank = 4 * (n % 2)
                pe.wait_ge(w_low, c + 1)
                pe.wait_ge(w_in[n], d * 32 + 32)
                if first is None or first >= 2:
                    pe.wait_ge(up_used, c - 1)
                for h in range(2):
                    cols = slice(h * 512, (h + 1) * 512)
                    for k in range(KC):
                        if first == 0 and h == 0:
                            pe.wait_ge(h_low, k + 1)
                        for w, x in ((wg_hi[n % 2], h_hi), (wg_hi[n % 2], h_lo), (wg_lo[n], h_hi)):
                            nc.tensor.matmul(psum[:, bank + h, :], w[:, k, :], x[:, k, cols],
                                             start=(k == 0 and w is wg_hi[n % 2] and x is h_hi),
                                             stop=(k == KC - 1 and w is wg_lo[n]))
                if first is not None:
                    pe.wait_ge(h_low, KC + n + 1)
                for h in range(2):
                    for k in range(2):
                        for w, x in ((wb_hi[n % 2], y_hi[n]), (wb_hi[n % 2], y_lo[n]), (wb_lo[n], y_hi[n])):
                            ins = nc.tensor.matmul(psum[:, bank + 2 + h, :], w[:, k, :],
                                                   x[:, k, h * 512:(h + 1) * 512],
                                                   start=(k == 0 and w is wb_hi[n % 2] and x is y_hi[n]),
                                                   stop=(k == 1 and w is wb_lo[n]))
                ins.then_inc(gate_ready, 1)
            steps(pe, body)

        @block.scalar
        def _(act):
            def gate(c, n, first):
                act.wait_ge(gate_ready, c + 1)
                if first is None or first >= 2:
                    act.wait_ge(up_used, c - 1)
                nc.scalar.activation(sig[n % 2][:, :], psum[:, 4 * (n % 2):4 * (n % 2) + 2, :]
                                     .rearrange("p a b -> p (a b)"), ACT.Sigmoid).then_inc(sig_ready, 1)

            def body(c, d, n, first):
                act.wait_ge(w_in[n], d * 32 + 32)
                if first is None or first >= 2:
                    act.wait_ge(gate_ready, c - 1)
                nc.scalar.activation(wb_hi[n % 2][:, :, :], wb[n][:, :, :], ACT.Copy)
                nc.scalar.activation(wg_hi[n % 2][:, :, :], wg[n][:, :, :], ACT.Copy).then_inc(w_high, 1)
                if first == 0:
                    for k in range(KC):
                        nc.scalar.activation(h_hi[:, k, :], s.hT[:, k, :], ACT.Copy).then_inc(h_high, 1)
                if first is not None:
                    nc.scalar.activation(y_hi[n][:, :, :], s.tT[:, yT_of[n]:yT_of[n] + 2, :],
                                         ACT.Copy).then_inc(h_high, 1)
                if first != 0:
                    gate(c - 1, (n - 1) % 4, None if first is None else first - 1)
            steps(act, body)
            gate(4 * KC - 1, 3, None)

        @block.vector
        def _(dve):
            def use(c, d, n, first):
                dve.wait_ge(sig_ready, c + 1)
                up = psum[:, 4 * (n % 2) + 2:4 * (n % 2) + 4, :].rearrange("p a b -> p (a b)")
                if first is None or first >= 2:
                    dve.wait_ge(summed, d * 3 + max(n - 1, 0))
                nc.vector.tensor_tensor(prod[min(n, 1)][:, :], up, sig[n % 2][:, :], ALU.mult).then_inc(up_used, 1)
                if n:
                    dve.wait_ge(up_used, c + 1)
                    dst = prod[0][:, :] if n < 3 else mixT[:, bass.ds(d, 1), :].rearrange("p o n -> p (o n)")
                    nc.vector.tensor_tensor(dst, prod[0][:, :], prod[1][:, :], ALU.add).then_inc(summed, 1)

            def body(c, d, n, first):
                dve.wait_ge(w_high, c + 1)
                nc.vector.tensor_tensor(wb_lo[n][:, :, :], wb[n][:, :, :], wb_hi[n % 2][:, :, :].bitcast(F32),
                                        ALU.subtract)
                nc.vector.tensor_tensor(wg_lo[n][:, :, :], wg[n][:, :, :], wg_hi[n % 2][:, :, :].bitcast(F32),
                                        ALU.subtract).then_inc(w_low, 1)
                if first == 0:
                    for k in range(KC):
                        dve.wait_ge(h_high, k + 1)
                        nc.vector.tensor_tensor(h_lo[:, k, :], s.hT[:, k, :], h_hi[:, k, :].bitcast(F32),
                                                ALU.subtract).then_inc(h_low, 1)
                if first is not None:
                    dve.wait_ge(h_high, KC + n + 1)
                    nc.vector.tensor_tensor(y_lo[n][:, :, :], s.tT[:, yT_of[n]:yT_of[n] + 2, :],
                                            y_hi[n][:, :, :].bitcast(F32), ALU.subtract).then_inc(h_low, 1)
                if first == 0:
                    pass
                elif n:
                    use(c - 1, d, n - 1, None if first is None else first - 1)
                else:
                    use(c - 1, d - 1, 3, 3)
            steps(dve, body)
            use(4 * KC - 1, KC - 1, 3, 3)


def route(nc, a, s):
    sb, sem, psum = s.sb, s.sem, s.psum
    NBLK = NE + N_OV
    w_out, w_lo = sb("w_out", [P, KC, DM], 128), sb("w_out_lo", [P, KC, DM], 128, F32R)
    w_hi = sb("w_out_hi", [P, KC, DM], 0, F32R)
    mix_lo = sb("mix_lo", [P, KC, SEQ], 96, F32R)
    mix_hi = [sb(f"mix_hi{k}", [P, SEQ], 40 + 16 * (k // 2) + 4 * (k % 2), F32R) for k in range(KC)]
    w_high, w_low = s.w_high, s.w_low
    halves = [(h, k) for h in range(2) for k in range(0, KC, 2)]
    gain = sb("gain2", [P, DM], 160)
    h2 = [sb(f"h2_{i}", [P, DM], 164 + 4 * i) for i in range(2)]
    h2T = [sb(f"h2T{i}", [P, KC, P], 192 + 4 * i) for i in range(2)]
    rw = sb("rw", [P, KC, NG + NE], 200)
    rb = sb("rb", [P, NG + NE], 201.25)
    ssq, rms = sb("ssq2", [P, NT], 201.5), sb("rms2", [P, NT], 201.5625)
    eps = sb("eps4", [P, 1], 201.625)
    lg = sb("lg", [P, NT, NG + NE], 160)
    triu, ones = sb("triu", [P, P], 172), sb("ones", [P, P], 172.5)
    iota_e = sb("iota_e", [P, NE], 173)
    iota_r = sb("iota_r", [P, NE], 173.125)
    iota_c = sb("iota_c", [P, CAP], 173.25)
    iota_b = sb("iota_b", [P, NBLK], 173.75)
    iota_j = sb("iota_j", [1, N_OV, NE], 180)
    tok_id = sb("tok_id", [P, NT], 174)
    e1, e2, t1, t2 = (sb(f"r_{n}", [P, NT, NE], 162 + k) for k, n in enumerate(["e1", "e2", "t1", "t2"]))
    o1, o2, cum, tot = (sb(f"r_{n}", [P, NT, NE], 166 + k) for k, n in enumerate(["o1", "o2", "cum", "tot"]))
    g_d, g_e = sb("g_d", [P, NT, NG], 170), sb("g_e", [P, NT, NG], 170.125)
    v = sb("r_v", [P, 24, NT], 170.25)
    asg = sb("asg", [P, 8, 2 * NT], 171)
    cnt = sb("cnt", [P, 4, NE], 171.5)
    hot_c = [sb(f"hot_c{i}", [P, CAP], 176 + i) for i in range(2)]
    hot_b = [sb(f"hot_b{i}", [P, NBLK], 176.5 + i) for i in range(2)]
    cmpj = sb("cmpj", [1, N_OV, NE], 184)

    rw_in, gain_in = sem("rw_in"), sem("gain_in")
    out_ready, x2_ready, summed, rooted = sem("out_ready"), sem("x2_ready"), sem("summed4"), sem("rooted")
    h2_ready, h2_stored, h2T_ready, h2T_taken = sem("h2_ready"), [sem(f"h2_stored{i}") for i in range(2)], \
        sem("h2T_ready"), sem("h2T_taken")
    logits_ready = sem("logits_ready")
    const_ready = sem("const_ready4")
    soft_in, soft_out, assigned, counted = sem("soft_in"), sem("soft_out"), sem("assigned"), sem("counted")
    hot_ready, hot_used = sem("hot_ready"), sem("hot_used")
    w_out_in = [sem(f"w_out_in{i}") for i in range(2)]

    with nc.Block() as block:
        @block.sync
        def _(sp):
            for h in range(2):
                sp.dma_start(w_out[:, :, h * 512:(h + 1) * 512],
                             a["w_out"].rearrange("(c p) n -> p c n", p=P)[:, :, h * 512:(h + 1) * 512]
                             ).then_inc(w_out_in[h], 16)
            for t in range(NT):
                sp.dma_start(s.x2[t][:, :], a["x"][t * P:(t + 1) * P, :]).then_inc(s.x_in[t], 16)
            sp.dma_start(gain[:, :], a["g_ffn"].partition_broadcast(P)).then_inc(gain_in, 16)
            sp.dma_start(rw[:, :, :], a["w_router"]).then_inc(rw_in, 16)
            sp.dma_start(rb[:, :], a["b_router"].partition_broadcast(P)).then_inc(rw_in, 16)
            for t in range(NT):
                sp.wait_ge(h2_ready, t + 1)
                sp.dma_start(s.h2_rows[t * P:(t + 1) * P, :], h2[t % 2][:, :]).then_inc(h2_stored[t % 2], 16)
            sp.wait_ge(out_ready, NT)
            s.load_expert(sp, 0, 0, "w1"), s.load_expert(sp, 0, 0, "w3")
            s.load_expert(sp, 0, 0, "w2")
            s.load_expert(sp, 1, 1, "w1"), s.load_expert(sp, 1, 1, "w3")
            for k in range(2):
                sp.wait_ge(h2_stored[k], 16 * NT // 2)

        @block.gpsimd
        def _(pool):
            link = chained(pool, s.pool_chain)
            pool.memset(eps[:, :], EPS).then_inc(const_ready, 1)
            link(pool.memset(triu[:, :], 1.0))
            pool.affine_select(out=triu[:, :], in_=triu[:, :], compare_op=ALU.is_gt, fill=0.0, base=0,
                               pattern=[[1, P]], channel_multiplier=-1).then_inc(const_ready, 1)
            pool.memset(ones[:, :], 1.0).then_inc(const_ready, 1)
            exact = dict(allow_small_or_imprecise_dtypes=True)
            pool.iota(iota_e[:, :], pattern=[[1, NE]], base=0, channel_multiplier=0, **exact)
            pool.iota(iota_r[:, :], pattern=[[-1, NE]], base=NE, channel_multiplier=0, **exact)
            pool.iota(iota_c[:, :], pattern=[[1, CAP]], base=0, channel_multiplier=0, **exact)
            pool.iota(iota_b[:, :], pattern=[[1, NBLK]], base=0, channel_multiplier=0, **exact)
            pool.iota(iota_j[:, :, :], pattern=[[1, N_OV], [0, NE]], base=0, channel_multiplier=0, **exact)
            pool.iota(tok_id[:, :], pattern=[[P, NT]], base=0, channel_multiplier=1, **exact).then_inc(const_ready, 1)

        @block.scalar
        def _(act):
            for k in range(KC):
                nc.scalar.activation(mix_hi[k][:, :], s.mixT[:, k, :], ACT.Copy).then_inc(w_high, 1)
            for h, k in halves:
                act.wait_ge(w_out_in[h], 16)
                cols = slice(h * 512, (h + 1) * 512)
                nc.scalar.activation(w_hi[:, k:k + 2, cols], w_out[:, k:k + 2, cols], ACT.Copy).then_inc(w_high, 1)
            for t in range(NT):
                act.wait_ge(const_ready, 4)
                act.wait_ge(summed, t + 1)
                nc.scalar.activation(rms[:, t:t + 1], ssq[:, t:t + 1], ACT.Sqrt, bias=eps[:, 0:1],
                                     scale=1.0 / DM).then_inc(rooted, 1)
                for h in range(2):
                    act.wait_ge(h2T_ready, 2 * t + h + 1)
                    if t >= 2 and h == 0:
                        act.wait_ge(logits_ready, t - 1)
                    nc.scalar.activation(h2T[t % 2][:, 4 * h:4 * h + 4, :].rearrange("p c n -> p (c n)"),
                                         psum[:, 4 + h, :], ACT.Copy).then_inc(h2T_taken, 1)
            act.wait_ge(soft_in, 1)
            nc.scalar.activation(g_e[:, :, :], g_d[:, :, :], ACT.Exp).then_inc(soft_out, 1)
            act.wait_ge(soft_in, 2)
            nc.scalar.activation(v[:, 6, :], v[:, 5, :], ACT.Exp).then_inc(soft_out, 1)

        @block.vector
        def _(dve):
            link = chained(dve, s.dve_chain)
            for k in range(KC):
                dve.wait_ge(w_high, 4 * KC + k + 1)
                nc.vector.tensor_tensor(mix_lo[:, k, :], s.mixT[:, k, :], mix_hi[k][:, :].bitcast(F32),
                                        ALU.subtract).then_inc(w_low, 1)
            for i, (h, k) in enumerate(halves):
                dve.wait_ge(w_high, 5 * KC + i + 1)
                cols = slice(h * 512, (h + 1) * 512)
                nc.vector.tensor_tensor(w_lo[:, k:k + 2, cols], w_out[:, k:k + 2, cols],
                                        w_hi[:, k:k + 2, cols].bitcast(F32), ALU.subtract).then_inc(w_low, 1)
            dve.wait_ge(gain_in, 16)
            for t in range(NT):
                dve.wait_ge(out_ready, t + 1)
                dve.wait_ge(s.x_in[t], 32)
                x2 = s.x2[t][:, :]
                link(nc.vector.tensor_tensor(x2, psum[:, 2 * (t % 2):2 * (t % 2) + 2, :]
                                             .rearrange("p a b -> p (a b)"), x2, ALU.add))
                nc.vector.engine_nop().then_inc(x2_ready, 1)
                if t >= 2:
                    dve.wait_ge(h2_stored[t % 2], 16 * (t // 2))
                    dve.wait_ge(h2T_ready, 2 * (t - 1))
                nc.vector.tensor_tensor_reduce(out=h2[t % 2][:, :], in0=x2, in1=x2, scale=1.0, scalar=0.0,
                                               op0=ALU.mult, op1=ALU.add, accum_out=ssq[:, t:t + 1]
                                               ).then_inc(summed, 1)
                dve.wait_ge(rooted, t + 1)
                link(nc.vector.reciprocal(rms[:, t:t + 1], rms[:, t:t + 1]))
                nc.vector.scalar_tensor_tensor(out=h2[t % 2][:, :], in0=x2, scalar=rms[:, t:t + 1], in1=gain[:, :],
                                               op0=ALU.mult, op1=ALU.mult).then_inc(h2_ready, 1)
            dve.wait_ge(rw_in, 32)
            dve.wait_ge(logits_ready, NT)
            dve.wait_ge(h2_ready, NT)
            for k in range(2):
                dve.wait_ge(h2_stored[k], 16 * NT // 2)
            L = psum[:, 6, 0:NT * (NG + NE)].rearrange("p (t n) -> p t n", n=NG + NE)
            link(nc.vector.tensor_tensor(lg[:, :, :], L, rb[:, :].unsqueeze(1).to_broadcast([P, NT, NG + NE]), ALU.add))
            lgg, lge = lg[:, :, 0:NG], lg[:, :, NG:NG + NE]

            def spread(x, n):
                return x.unsqueeze(2).to_broadcast([P, NT, n])

            def first_max(hot, x, top, tmp, n, m):
                rank = iota_r[:, 0:n].unsqueeze(1).to_broadcast([P, NT, n])
                link(nc.vector.tensor_reduce(out=top, in_=x, axis=AX.X, op=ALU.max))
                link(nc.vector.tensor_tensor(tmp, x, spread(top, n), ALU.is_equal))
                link(nc.vector.tensor_tensor(tmp, tmp, rank, ALU.mult))
                link(nc.vector.tensor_reduce(out=m, in_=tmp, axis=AX.X, op=ALU.max))
                link(nc.vector.tensor_tensor(hot, tmp, spread(m, n), ALU.is_equal))

            og = t1[:, :, 0:NG]
            first_max(og, lgg, v[:, 0, :], t2[:, :, 0:NG], NG, v[:, 1, :])
            nc.vector.tensor_tensor(g_d[:, :, :], lgg, spread(v[:, 0, :], NG), ALU.subtract).then_inc(soft_in, 1)
            dve.wait_ge(soft_out, 1)
            link(nc.vector.tensor_reduce(out=v[:, 2, :], in_=g_e[:, :, :], axis=AX.X, op=ALU.add))
            link(nc.vector.reciprocal(v[:, 2, :], v[:, 2, :]))
            link(nc.vector.tensor_scalar(og, og, -1.0, 1e30, ALU.add, ALU.mult))
            for g in range(NG):
                ins = nc.vector.tensor_tensor(e1[:, :, g * EG:(g + 1) * EG], lge[:, :, g * EG:(g + 1) * EG],
                                              og[:, :, g:g + 1].to_broadcast([P, NT, EG]), ALU.add)
            link(ins)
            first_max(o1[:, :, :], e1[:, :, :], v[:, 3, :], t2[:, :, :], NE, v[:, 1, :])
            link(nc.vector.tensor_scalar(t1[:, :, :], o1[:, :, :], -2e30, None, ALU.mult))
            link(nc.vector.tensor_tensor(e1[:, :, :], e1[:, :, :], t1[:, :, :], ALU.add))
            first_max(o2[:, :, :], e1[:, :, :], v[:, 4, :], t2[:, :, :], NE, v[:, 1, :])
            nc.vector.tensor_tensor(v[:, 5, :], v[:, 4, :], v[:, 3, :], ALU.subtract).then_inc(soft_in, 1)
            link(nc.vector.tensor_tensor(e2[:, :, :], o1[:, :, :], o2[:, :, :], ALU.add))
            link(nc.vector.memset(cum[:, 0, :], 0.0))
            for t in range(1, NT):
                link(nc.vector.tensor_tensor(cum[:, t, :], cum[:, t - 1, :], e2[:, t - 1, :], ALU.add))
            link(nc.vector.tensor_tensor(tot[:, 0, :], cum[:, NT - 1, :], e2[:, NT - 1, :], ALU.add))
            nc.vector.engine_nop().then_inc(assigned, 1)
            dve.wait_ge(soft_out, 2)
            link(nc.vector.tensor_scalar(v[:, 7, :], v[:, 6, :], 1.0, None, ALU.add))
            link(nc.vector.reciprocal(v[:, 7, :], v[:, 7, :]))
            link(nc.vector.tensor_tensor(s.gates[:, 0, :], v[:, 7, :], v[:, 2, :], ALU.mult))
            link(nc.vector.tensor_tensor(s.gates[:, 1, :], s.gates[:, 0, :], v[:, 6, :], ALU.mult))
            dve.wait_ge(counted, 1)
            pos = psum[:, 7, 0:NT * NE].rearrange("p (t e) -> p t e", e=NE)
            link(nc.vector.tensor_copy(e1[:, :, :], pos))
            link(nc.vector.tensor_copy(cnt[:, 0, :], psum[:, 7, NT * NE:NT * NE + NE]))
            link(nc.vector.tensor_scalar(cnt[:, 1, :], cnt[:, 0, :], float(CAP), None, ALU.is_gt))
            MORE = (SEQ - 1) // CAP
            for k in range(2, MORE + 1):
                link(nc.vector.scalar_tensor_tensor(out=cnt[:, 1, :], in0=cnt[:, 0, :], scalar=float(CAP * k),
                                                    in1=cnt[:, 1, :], op0=ALU.is_gt, op1=ALU.add))
            link(nc.vector.memset(cnt[:, 2, :], 1.0))
            link(nc.vector.tensor_tensor_scan(cnt[:, 3, :], cnt[:, 2, :], cnt[:, 1, :], 0.0, ALU.mult, ALU.add))
            link(nc.vector.tensor_tensor(cnt[:, 1, :], cnt[:, 3, :], cnt[:, 1, :], ALU.subtract))
            ends = cnt[0:1, 3, :].unsqueeze(1).to_broadcast([1, N_OV, NE])
            link(nc.vector.tensor_tensor(cmpj[:, :, :], iota_j[:, :, :], ends, ALU.is_ge))
            link(nc.vector.tensor_reduce(out=s.ov_f[:, 0, :], in_=cmpj[:, :, :], axis=AX.X, op=ALU.add))
            link(nc.vector.tensor_scalar(s.ov_f[:, 1, :], s.ov_f[:, 0, :], NE - 0.5, None, ALU.is_lt))
            link(nc.vector.tensor_scalar(s.ov_f[:, 0, :], s.ov_f[:, 0, :], float(NE - 1), None, ALU.min))
            link(nc.vector.tensor_copy(s.ov_i[:, :, :], s.ov_f[:, :, :]))
            for k, hot in enumerate((o1, o2)):
                for r, table in enumerate((e1[:, :, :],
                                           iota_e[:, :].unsqueeze(1).to_broadcast([P, NT, NE]),
                                           cnt[:, 1, :].unsqueeze(1).to_broadcast([P, NT, NE]))):
                    link(nc.vector.tensor_tensor(t1[:, :, :], hot[:, :, :], table, ALU.mult))
                    link(nc.vector.tensor_reduce(out=asg[:, r, k * NT:(k + 1) * NT], in_=t1[:, :, :], axis=AX.X,
                                                 op=ALU.add))
            link(nc.vector.tensor_scalar(asg[:, 3, :], asg[:, 0, :], float(CAP), None, ALU.is_ge))
            link(nc.vector.tensor_copy(asg[:, 6, :], asg[:, 3, :]))
            for k in range(2, MORE + 1):
                link(nc.vector.scalar_tensor_tensor(out=asg[:, 3, :], in0=asg[:, 0, :], scalar=float(CAP * k),
                                                    in1=asg[:, 3, :], op0=ALU.is_ge, op1=ALU.add))
            link(nc.vector.scalar_tensor_tensor(out=asg[:, 4, :], in0=asg[:, 3, :], scalar=-float(CAP),
                                                in1=asg[:, 0, :], op0=ALU.mult, op1=ALU.add))
            link(nc.vector.scalar_tensor_tensor(out=asg[:, 5, :], in0=asg[:, 3, :], scalar=float(NE - 1),
                                                in1=asg[:, 2, :], op0=ALU.add, op1=ALU.add))
            link(nc.vector.tensor_tensor(asg[:, 5, :], asg[:, 5, :], asg[:, 1, :], ALU.subtract))
            link(nc.vector.tensor_tensor(asg[:, 5, :], asg[:, 5, :], asg[:, 6, :], ALU.mult))
            link(nc.vector.tensor_tensor(asg[:, 5, :], asg[:, 5, :], asg[:, 1, :], ALU.add))
            link(nc.vector.scalar_tensor_tensor(out=asg[:, 7, :], in0=asg[:, 5, :], scalar=float(CAP),
                                                in1=asg[:, 4, :], op0=ALU.mult, op1=ALU.add))
            link(nc.vector.tensor_copy(s.row_of[:, :], asg[:, 7, :]))
            for q in range(2 * NT):
                if q >= 2:
                    dve.wait_ge(hot_used, q - 1)
                nc.vector.tensor_scalar(hot_c[q % 2][:, :], iota_c[:, :], asg[:, 4, q:q + 1], None, ALU.is_equal)
                nc.vector.tensor_scalar(hot_b[q % 2][:, :], iota_b[:, :], asg[:, 5, q:q + 1],
                                        tok_id[:, q % NT:q % NT + 1], ALU.is_equal, ALU.mult).then_inc(hot_ready, 1)
            dve.wait_ge(hot_used, 2 * NT)
            link(nc.vector.tensor_copy(s.tok_of[:, :], psum[0:CAP, 5, 0:NBLK]))

        @block.tensor
        def _(pe):
            def project_out(t):
                if t >= 2:
                    pe.wait_ge(x2_ready, t - 1)
                for h in range(2):
                    for k in range(KC):
                        if t == 0 and k % 2 == 0:
                            pe.wait_ge(w_low, 5 * KC + halves.index((h, k)) + 1)
                        toks, cols = slice(t * P, (t + 1) * P), slice(h * 512, (h + 1) * 512)
                        for i, (x, w) in enumerate(((mix_hi[k][:, toks], w_hi), (mix_hi[k][:, toks], w_lo),
                                                    (mix_lo[:, k, toks], w_hi))):
                            ins = nc.tensor.matmul(psum[:, 2 * (t % 2) + h, :], x, w[:, k, cols],
                                                   start=(k == 0 and i == 0), stop=(k == KC - 1 and i == 2))
                ins.then_inc(out_ready, 1)

            project_out(0)
            for t in range(NT):
                if t + 1 < NT:
                    project_out(t + 1)
                pe.wait_ge(h2_ready, t + 1)
                if t:
                    pe.wait_ge(h2T_taken, 2 * t)
                for h in range(2):
                    for c in range(4):
                        k = 4 * h + c
                        ins = nc.tensor.transpose(psum[:, 4 + h, c * P:(c + 1) * P],
                                                  h2[t % 2][:, k * P:(k + 1) * P], s.ident[:, :])
                    ins.then_inc(h2T_ready, 1)
                pe.wait_ge(h2T_taken, 2 * t + 2)
                if t == 0:
                    pe.wait_ge(rw_in, 32)
                for k in range(KC):
                    ins = nc.tensor.matmul(psum[:, 6, t * (NG + NE):(t + 1) * (NG + NE)], h2T[t % 2][:, k, :],
                                           rw[:, k, :], start=(k == 0), stop=(k == KC - 1))
                ins.then_inc(logits_ready, 1)
            pe.wait_ge(assigned, 1)
            pe.wait_ge(const_ready, 4)
            pe_pos = psum[:, 7, 0:NT * NE]
            nc.tensor.matmul(pe_pos, triu[:, :], e2[:, :, :].rearrange("p t e -> p (t e)"), start=True, stop=False)
            nc.tensor.matmul(pe_pos, ones[:, :], cum[:, :, :].rearrange("p t e -> p (t e)"), start=False, stop=True)
            nc.tensor.matmul(psum[:, 7, NT * NE:NT * NE + NE], ones[:, :], tot[:, 0, :], start=True,
                             stop=True).then_inc(counted, 1)
            for q in range(2 * NT):
                pe.wait_ge(hot_ready, q + 1)
                nc.tensor.matmul(psum[0:CAP, 5, 0:NBLK], hot_c[q % 2][:, :], hot_b[q % 2][:, :], start=(q == 0),
                                 stop=(q == 2 * NT - 1)).then_inc(hot_used, 1)


def experts(nc, a, s):
    sb, sem, psum = s.sb, s.sem, s.psum
    w1, w3, w2 = s.w1, s.w3, s.w2
    xg = [sb(f"xg{i}", [CAP, DM], 40 + 4 * i) for i in range(2)]
    xT = [sb(f"xT{i}", [P, KC, CAP], 56 + 4 * i) for i in range(2)]
    act_ = [sb(f"gl{i}", [P, FT, CAP], 72 + 2 * i) for i in range(2)]
    hid = [sb(f"hid{i}", [P, FT, CAP], 76 + 2 * i) for i in range(2)]
    hid_hi = [sb(f"hid_hi{i}", [P, FT, CAP], 192 + 2 * i, F32R) for i in range(2)]
    hid_lo = [sb(f"hid_lo{i}", [P, FT, CAP], 76 + 2 * i, F32R) for i in range(2)]
    w2_hi = [sb(f"w2_hi{i}", [P, FT, DM], 144 + 32 * i, F32R) for i in range(2)]
    w2_lo = [sb(f"w2_lo{i}", [P, FT, DM], 128 + 32 * i, F32R) for i in range(2)]
    yo = [sb(f"yo{i}", [CAP, DM], 88 + 4 * i) for i in range(2)]
    idx = [sb(f"idx{i}", [CAP, 1], 200 + 0.0625 * i, I32) for i in range(2)]

    idx_set, idx_seen = sem("idx_set"), sem("idx_seen")
    xg_in = [sem(f"xg_in{i}") for i in range(2)]
    xT_ready, xT_taken = sem("xT_ready5"), sem("xT_taken5")
    up_done, gate_done, hid_ready, y_done = sem("up_done"), sem("gate_done"), sem("hid_ready"), sem("y_done")
    glu_ready, glu_half, y_taken = sem("glu_ready"), sem("glu_half"), sem("y_taken")
    w2_high, w2_low, hid_high, hid_low = sem("w2_high"), sem("w2_low"), sem("hid_high"), sem("hid_low")
    y_stored = s.y_stored
    ov = {n: sem("ov_" + n) for n in ("go", "idx", "rows", "weights", "xT", "xT_taken", "up", "glu", "half",
                                      "hid", "y", "y_taken", "stored")}

    def transposes(j):
        for c in range(KC):
            ins = nc.tensor.transpose(psum[:, c // 4, (c % 4) * CAP:(c % 4 + 1) * CAP],
                                      xg[j][:, c * P:(c + 1) * P], s.ident[0:CAP, 0:CAP])
        return ins

    def up(bank, w, j):
        for f in range(FT):
            for k in range(KC):
                ins = nc.tensor.matmul(psum[:, bank, f * CAP:(f + 1) * CAP], w[j][:, k, f * P:(f + 1) * P],
                                       xT[j][:, k, :], start=(k == 0), stop=(k == KC - 1))
        return ins

    def down(j):
        for h in range(2):
            for f in range(FT):
                ins = nc.tensor.matmul(psum[0:CAP, 4 + h, :], hid[j][:, f, :], w2[j][:, f, h * 512:(h + 1) * 512],
                                       start=(f == 0), stop=(f == FT - 1))
        return ins

    def down_split(j):
        for f in range(FT):
            for x, w in ((hid_hi[j], w2_hi[j]), (hid_hi[j], w2_lo[j]), (hid_lo[j], w2_hi[j])):
                for h in range(2):
                    ins = nc.tensor.matmul(psum[0:CAP, 4 + h, :], x[:, f, :], w[:, f, h * 512:(h + 1) * 512],
                                           start=(f == 0 and x is hid_hi[j] and w is w2_hi[j]),
                                           stop=(f == FT - 1 and x is hid_lo[j]))
        return ins

    def banks(k, rows=P):
        return psum[0:rows, k:k + 2, :]

    def xT_out(j):
        return nc.scalar.activation(xT[j][:, :, :].rearrange("p (b c) n -> p b (c n)", b=2),
                                    psum[:, 0:2, 0:4 * CAP], ACT.Copy)

    def hidden(bank):
        return psum[:, bank, 0:FT * CAP]

    def of_w1(j):
        return 2 + 4 * j

    def of_w3(j):
        return 3 + 4 * j

    def flat(x):
        return x[:, :, :].rearrange("p f n -> p (f n)")

    def loop(eng, body):
        for j in range(2):
            body(0, j, True)
        with eng.Fori(1, NE // 2) as i:
            for j in range(2):
                body(i, j, False)

    def overflow(eng, body):
        with eng.Fori(0, N_OV) as b:
            used = eng.value_load(s.ov_i[0:1, 1, bass.ds(b, 1)], min_val=0, max_val=1)
            with eng.If(used):
                body(b)

    def expert_of(eng, b):
        return eng.value_load(s.ov_i[0:1, 0, bass.ds(b, 1)], min_val=0, max_val=NE - 1)

    with nc.Block() as block:
        @block.sync
        def _(sp):
            s.load_expert(sp, 1, 1, "w2")

            with sp.Fori(1, NE // 2) as i:
                for j in range(2):
                    sp.wait_ge(up_done, i * 2 + (j - 1))
                    s.load_expert(sp, i * 2 + j, j, "w1")
                    sp.wait_ge(gate_done, i * 2 + (j - 1))
                    s.load_expert(sp, i * 2 + j, j, "w3")
                    sp.wait_ge(y_done, i * 2 + (j - 1))
                    s.load_expert(sp, i * 2 + j, j, "w2")
            sp.wait_ge(y_done, NE)

            def body(b):
                sp.wait_ge(ov["go"], b + 1)
                e = expert_of(sp, b)
                s.load_expert(sp, e, 0, "w1", ov["weights"]), s.load_expert(sp, e, 0, "w3", ov["weights"])
                s.load_expert(sp, e, 0, "w2", ov["weights"])
            overflow(sp, body)

        @block.gpsimd
        def _(pool):
            def rows(j, done):
                pool.indirect_dma_start(xg[j][:, :], None, s.h2_rows,
                                        bass.IndirectOffsetOnAxis(ap=idx[j][:, 0:1].bitcast(U32), axis=0)
                                        ).then_inc(done, 16)

            def body(i, j, first):
                if not first:
                    pool.wait_ge(xT_ready, i * 2 + (j - 1))
                    pool.wait_ge(xg_in[j], i * 16)
                pool.tensor_copy(idx[j][:, :], s.tok_of[:, bass.ds(i * 2 + j, 1)]).then_inc(idx_set, 1)
                pool.wait_ge(idx_set, i * 2 + (j + 1))
                pool.sem_inc(idx_seen, 1)
                rows(j, xg_in[j])
            loop(pool, body)
            pool.wait_ge(y_done, NE)
            pool.sem_inc(ov["go"], 1)

            def body(b):
                pool.tensor_copy(idx[0][:, :], s.tok_of[:, bass.ds(b + NE, 1)]).then_inc(ov["idx"], 1)
                pool.wait_ge(ov["idx"], b + 1)
                pool.sem_inc(idx_seen, 1)
                rows(0, ov["rows"])
                pool.wait_ge(ov["stored"], b * 16 + 16)
                pool.sem_inc(ov["go"], 1)
            overflow(pool, body)

        @block.tensor
        def _(pe):
            def body(i, j, first):
                pe.wait_ge(xg_in[j], i * 16 + 16)
                if not (first and j == 0):
                    pe.wait_ge(xT_taken, i * 2 + j)
                transposes(j).then_inc(xT_ready, 1)
                if not (first and j == 0):
                    third(i * 2 + j - 1, 1 - j)
                pe.wait_ge(xT_taken, i * 2 + (j + 1))
                pe.wait_ge(s.w1_in[j], i * 16 + 16)
                up(of_w1(j), w1, j).then_inc(up_done, 1)
                if not (first and j == 0):
                    second(i * 2 + j - 1, 1 - j, first)

            def third(e, j):
                pe.wait_ge(s.w3_in[j], (e - j) * 8 + 16)
                up(of_w3(j), w3, j).then_inc(gate_done, 1)

            def second(e, j, first):
                pe.wait_ge(hid_low, e + 1)
                pe.wait_ge(w2_low, e + 1)
                if not first:
                    pe.wait_ge(y_taken, e)
                down_split(j).then_inc(y_done, 1)
            loop(pe, body)
            third(NE - 1, 1)
            second(NE - 1, 1, False)
            pe.wait_ge(y_taken, NE)

            def body(b):
                pe.wait_ge(ov["rows"], b * 16 + 16)
                transposes(0).then_inc(ov["xT"], 1)
                pe.wait_ge(ov["xT_taken"], b + 1)
                pe.wait_ge(ov["weights"], b * 48 + 48)
                up(of_w1(0), w1, 0)
                up(of_w3(0), w3, 0).then_inc(ov["up"], 1)
                pe.wait_ge(ov["hid"], b + 1)
                down(0).then_inc(ov["y"], 1)
            overflow(pe, body)

        @block.scalar
        def _(act):
            def y_out(e, j, first):
                act.wait_ge(y_done, e + 1)
                if not first:
                    act.wait_ge(y_stored[j], (e + j) * 8)
                nc.scalar.activation(yo[j][:, :], banks(4, CAP).rearrange("p a b -> p (a b)"),
                                     ACT.Copy).then_inc(y_taken, 1)
                act.wait_ge(y_taken, e + 1)
                act.dma_start(s.ys[bass.ds(e * CAP, CAP), :], yo[j][:, :]).then_inc(y_stored[j], 16)

            def high(e, j):
                act.wait_ge(hid_ready, e + 1)
                nc.scalar.activation(flat(hid_hi[j]), flat(hid[j]), ACT.Copy).then_inc(hid_high, 1)

            def body(i, j, first):
                act.wait_ge(xT_ready, i * 2 + (j + 1))
                if not first:
                    act.wait_ge(gate_done, i * 2 + (j - 1))
                xT_out(j).then_inc(xT_taken, 1)
                if not (first and j == 0):
                    high(i * 2 + j - 1, 1 - j)
                act.wait_ge(s.w2_in[j], i * 16 + 16)
                nc.scalar.activation(w2_hi[j][:, :, :], w2[j][:, :, :], ACT.Copy).then_inc(w2_high, 1)
                act.wait_ge(up_done, i * 2 + (j + 1))
                if not first:
                    act.wait_ge(glu_half, i * 2 + (j - 1))
                nc.scalar.activation(flat(act_[j]), hidden(of_w1(j)), ACT.Sigmoid).then_inc(glu_ready, 1)
                if not (first and j == 0):
                    y_out(i * 2 + j - 1, 1 - j, first)
            loop(act, body)
            high(NE - 1, 1)
            y_out(NE - 1, 1, False)
            for j in range(2):
                act.wait_ge(y_stored[j], 16 * (NE // 2 + j))

            def body(b):
                act.wait_ge(ov["xT"], b + 1)
                xT_out(0).then_inc(ov["xT_taken"], 1)
                act.wait_ge(ov["up"], b + 1)
                nc.scalar.activation(flat(act_[0]), hidden(of_w1(0)), ACT.Sigmoid).then_inc(ov["glu"], 1)
                act.wait_ge(ov["y"], b + 1)
                nc.scalar.activation(yo[0][:, :], banks(4, CAP).rearrange("p a b -> p (a b)"),
                                     ACT.Copy).then_inc(ov["y_taken"], 1)
                act.wait_ge(ov["y_taken"], b + 1)
                act.dma_start(s.ys[bass.ds((b + NE) * CAP, CAP), :], yo[0][:, :]).then_inc(ov["stored"], 16)
            overflow(act, body)

        @block.vector
        def _(dve):
            def glu(j, half, done, value):
                nc.vector.tensor_tensor(flat(act_[j]), hidden(of_w1(j)), flat(act_[j]), ALU.mult).then_inc(half, 1)
                dve.wait_ge(half, value)
                return nc.vector.tensor_tensor(flat(hid[j]), hidden(of_w3(j)), flat(act_[j]), ALU.mult)

            def hidden_rows(e, j, first):
                dve.wait_ge(glu_ready, e + 1)
                dve.wait_ge(gate_done, e + 1)
                if not first:
                    dve.wait_ge(y_done, e)
                glu(j, glu_half, hid_ready, e + 1).then_inc(hid_ready, 1)
                dve.wait_ge(hid_high, e + 1)
                nc.vector.tensor_tensor(flat(hid_lo[j]), flat(hid[j]), flat(hid_hi[j]).bitcast(F32),
                                        ALU.subtract).then_inc(hid_low, 1)

            def body(i, j, first):
                if not (first and j == 0):
                    hidden_rows(i * 2 + j - 1, 1 - j, first)
                dve.wait_ge(w2_high, i * 2 + (j + 1))
                nc.vector.tensor_tensor(w2_lo[j][:, :, :], w2[j][:, :, :], w2_hi[j][:, :, :].bitcast(F32),
                                        ALU.subtract).then_inc(w2_low, 1)
            loop(dve, body)
            hidden_rows(NE - 1, 1, False)

            def body(b):
                dve.wait_ge(ov["glu"], b + 1)
                glu(0, ov["half"], ov["hid"], b + 1).then_inc(ov["hid"], 1)
            overflow(dve, body)


def combine(nc, a, s):
    sb, sem = s.sb, s.sem
    ya = [sb(f"ya{i}", [P, DM], 96 + 4 * i) for i in range(NT)]
    yb = [sb(f"yb{i}", [P, DM], 128 + 4 * i) for i in range(NT)]
    fg = sb("fg", [P, DM], 160)
    junk = sb("junk6", [P, DM], 164)
    ssq, rms, eps = sb("ssq6", [P, NT], 200), sb("rms6", [P, NT], 200.0625), sb("eps6", [P, 1], 200.125)
    fg_in, eps_set = sem("fg_in"), sem("eps_set")
    squared = s.squared
    y_in = [sem(f"y_in{t}") for t in range(NT)]
    stored = s.x_in
    summed, rooted, final = sem("summed6"), sem("rooted6"), sem("final")
    with nc.Block() as block:
        @block.sync
        def _(sp):
            sp.dma_start(fg[:, :], a["g_final"].partition_broadcast(P)).then_inc(fg_in, 16)
            for t in range(NT):
                sp.wait_ge(final, t + 1)
                sp.dma_start(a["out"][t * P:(t + 1) * P, :], ya[t][:, :]).then_inc(stored[t], 16)
            for t in range(NT):
                sp.wait_ge(stored[t], 48)

        @block.gpsimd
        def _(pool):
            pool.memset(eps[:, :], EPS).then_inc(eps_set, 1)
            for t in range(NT):
                for k, dst in enumerate((ya, yb)):
                    col = k * NT + t
                    pool.indirect_dma_start(dst[t][:, :], None, s.ys,
                                            bass.IndirectOffsetOnAxis(ap=s.row_of[:, col:col + 1].bitcast(U32), axis=0)
                                            ).then_inc(y_in[t], 16)

        @block.scalar
        def _(act):
            act.wait_ge(eps_set, 1)
            for t in range(NT):
                act.wait_ge(summed, t + 1)
                if t:
                    act.wait_ge(rooted, t)
                nc.scalar.activation(junk[:, :], s.x2[t][:, :], ACT.Square,
                                     accum_out=ssq[:, t:t + 1]).then_inc(squared, 1)
                act.wait_ge(squared, NT + t + 1)
                nc.scalar.activation(rms[:, t:t + 1], ssq[:, t:t + 1], ACT.Sqrt, bias=eps[:, 0:1],
                                     scale=1.0 / DM).then_inc(rooted, 1)

        @block.vector
        def _(dve):
            link = chained(dve, s.dve_chain)
            dve.wait_ge(fg_in, 16)

            def finish(t):
                dve.wait_ge(rooted, t + 1)
                link(nc.vector.reciprocal(rms[:, t:t + 1], rms[:, t:t + 1]))
                nc.vector.scalar_tensor_tensor(out=ya[t][:, :], in0=s.x2[t][:, :], scalar=rms[:, t:t + 1], in1=fg[:, :],
                                               op0=ALU.mult, op1=ALU.mult).then_inc(final, 1)

            for t in range(NT):
                x2 = s.x2[t][:, :]
                dve.wait_ge(y_in[t], 32)
                link(nc.vector.scalar_tensor_tensor(out=x2, in0=ya[t][:, :], scalar=s.gates[:, 0, t:t + 1], in1=x2,
                                                    op0=ALU.mult, op1=ALU.add))
                link(nc.vector.scalar_tensor_tensor(out=x2, in0=yb[t][:, :], scalar=s.gates[:, 1, t:t + 1], in1=x2,
                                                    op0=ALU.mult, op1=ALU.add))
                nc.vector.engine_nop().then_inc(summed, 1)
                if t:
                    finish(t - 1)
            finish(NT - 1)
def laid_out(i):
    import numpy as np
    w = i["w_in"][0].reshape(KC, P, -1)
    sizes = dict(qa=256, ka=256, va=256, qi=128, ki=32, wi=4, qb=256, kb=256, vb=256, ib=4, fb=4, ob=256,
                 qc=256, kc=256, vc=256, qd=256, kd=256, vd=256)
    col, at = {}, 0
    for n, z in sizes.items():
        col[n] = w[:, :, at:at + z]
        at += z

    def cat(*names):
        return np.concatenate([col[n] for n in names], axis=2).transpose(1, 0, 2)

    tiles = cat("qi", "ki", "ki", "ki", "ki", "qb", "kb", "qc", "kc", "qd", "kd", "qa", "ka")
    out = {
        "x": i["x"][0],
        "g_mix": i["norm_mix_g"][0].reshape(KC, P).T,
        "if_bias": np.stack([i["mlstm_i_bias"][0], i["mlstm_f_bias"][0]], axis=1),
        "conv": np.concatenate([i["conv_w"][0], i["conv_b"]], axis=0).reshape(5, 4, P).transpose(2, 1, 0),
        "rel": i["relpos_bias"][0][:, ::-1],
        "g_mlstm": i["mlstm_norm_g"][0],
        "g_diff": i["diff_norm_g"][0],
        "lam": i["diff_lambda"][0],
        "w_gate": i["w_gate"][0].reshape(KC, P, 4, KC, P).transpose(2, 3, 1, 0, 4),
        "w_branch": i["w_branch"][0].reshape(4, 2, P, KC, P).transpose(0, 3, 2, 1, 4),
        "w_out": i["w_out"][0],
        "g_ffn": i["norm_ffn_g"][0],
        "w_router": np.concatenate([i["router_group_w"][0], i["router_expert_w"][0]], axis=1)
        .reshape(KC, P, NG + NE).transpose(1, 0, 2),
        "b_router": np.concatenate([i["router_group_b"][0], i["router_expert_b"][0]]),
        "expert_w1": i["expert_w1"][0],
        "expert_w3": i["expert_w3"][0],
        "expert_w2": i["expert_w2"][0],
        "g_final": i["final_norm_g"],
        "w_gates12": cat("ob", "wi", "ib", "fb"),
        "w_T": tiles.reshape(P, KC, NTT, P).transpose(2, 0, 1, 3),
        "w_V": np.stack([cat("va", "vc"), cat("vb", "vd")]),
    }
    return {n: np.ascontiguousarray(v) for n, v in out.items()}


def kernel(**inputs):
    import numpy as np
    import concourse.bacc as bacc
    from concourse.bass_utils import run_bass_kernel_spmd

    inputs = {n: np.asarray(v) for n, v in inputs.items()}
    arrays = laid_out(inputs)
    nc = bacc.Bacc("TRN2", target_bir_lowering=False, num_devices=1)
    aps = {n: nc.dram_tensor(n, v.shape, mybir.dt.from_np(v.dtype), kind="ExternalInput").ap()
           for n, v in arrays.items()}
    aps["out"] = nc.dram_tensor("out", (SEQ, DM), F32, kind="ExternalOutput").ap()
    build(nc, aps)
    r = run_bass_kernel_spmd(nc, [arrays], core_ids=[0])
    return r.results[0]["out"].reshape(1, SEQ, DM)
```
